# Optimizing a Trainium2 kernel written in Bass

```python
import jax, jax.numpy as jnp
from jax import lax
import numpy as np
import math

D_MODEL = 1024
BATCH = 1
SEQ = 256
DEPTH = 1

CHUNK = 64
MEM_LEN = 256
FOX_HEADS = 8
FOX_HEAD_DIM = 64
FOX_WIDTH = FOX_HEADS * FOX_HEAD_DIM
POOL_WIDTH = D_MODEL - FOX_WIDTH
POOL_WINDOWS = (2, 4, 8, 16)
POOL_GROUPS = len(POOL_WINDOWS)
POOL_GROUP_DIM = POOL_WIDTH // POOL_GROUPS
IN_COLS = 3 * FOX_WIDTH + POOL_WIDTH + FOX_HEADS
MEM_HEADS = 4
MEM_HEAD_DIM = 128
MEM_WIDTH = MEM_HEADS * MEM_HEAD_DIM
D_FF = ((-(-8 * D_MODEL // 3) + 255) // 256) * 256
Q_BLOCK = 128
EPS = 1e-6


def rmsnorm(x, g):
    xf = x.astype(jnp.float32)
    y = xf * lax.rsqrt(jnp.mean(xf * xf, axis=-1, keepdims=True) + EPS)
    return (y * g.astype(jnp.float32)).astype(x.dtype)

def forgetting_attention(q, k, v, f_logit):
    c = jnp.cumsum(jax.nn.log_sigmoid(f_logit.astype(jnp.float32)), axis=-1)
    scale = FOX_HEAD_DIM ** -0.5
    S = q.shape[2]
    outs = []
    for start in range(0, S, Q_BLOCK):
        end = start + Q_BLOCK
        qb = q[:, :, start:end]
        kb = k[:, :, :end]
        vb = v[:, :, :end]
        s = jnp.einsum('bhqd,bhkd->bhqk', qb, kb, preferred_element_type=jnp.float32) * scale
        s = s + c[:, :, start:end, None] - c[:, :, None, :end]
        qpos = start + jnp.arange(Q_BLOCK)
        kpos = jnp.arange(end)
        s = jnp.where(kpos[None, :] <= qpos[:, None], s, -jnp.inf)
        p = jax.nn.softmax(s, axis=-1)
        outs.append(jnp.einsum('bhqk,bhkd->bhqd', p.astype(vb.dtype), vb))
    return jnp.concatenate(outs, axis=2)

def multiscale_pool(p, w_pool, pool_scale):
    B, S, _ = p.shape
    pf = p.astype(jnp.float32).reshape(B, S, POOL_GROUPS, POOL_GROUP_DIM)
    cs = jnp.concatenate([jnp.zeros((B, 1, POOL_GROUPS, POOL_GROUP_DIM), jnp.float32),
                          jnp.cumsum(pf, axis=1)], axis=1)
    t = jnp.arange(S)
    outs = []
    for g, w in enumerate(POOL_WINDOWS):
        csg = cs[:, :, g]
        lower = jnp.pad(csg, ((0, 0), (w - 1, 0), (0, 0)))[:, :S]
        cnt = jnp.minimum(t + 1, w).astype(jnp.float32)[None, :, None]
        mixed = (csg[:, 1:] - lower) / cnt - pf[:, :, g]
        outs.append(jnp.einsum('bsc,cd->bsd', mixed, w_pool[g].astype(jnp.float32)))
    y = jnp.concatenate(outs, axis=-1) * pool_scale.astype(jnp.float32)
    return y.astype(p.dtype)

def head_split(t, n_heads, head_dim):
    B, S, _ = t.shape
    return t.reshape(B, S, n_heads, head_dim)

def first_inputs(seed: int = 0) -> dict:
    key = jax.random.key(seed)
    ks = jax.random.split(key, 24)
    f32 = jnp.float32
    D = D_MODEL

    def nrm(k, shape, fan_in):
        return jax.random.normal(k, shape, f32) * (fan_in ** -0.5)

    def gain(k, shape):
        return 1.0 + 0.05 * jax.random.normal(k, shape, f32)

    return {
        "x": jax.random.normal(ks[0], (BATCH, SEQ, D), f32),
        "mem": jax.random.normal(ks[1], (BATCH, MEM_LEN, D), f32),
        "g_mix": gain(ks[2], (DEPTH, D)),
        "w_in": nrm(ks[3], (DEPTH, D, IN_COLS), D),
        "b_forget": 3.0 + 0.5 * jax.random.normal(ks[4], (DEPTH, FOX_HEADS), f32),
        "g_q_fox": gain(ks[5], (DEPTH, FOX_HEAD_DIM)),
        "g_k_fox": gain(ks[6], (DEPTH, FOX_HEAD_DIM)),
        "w_pool": nrm(ks[7], (DEPTH, POOL_GROUPS, POOL_GROUP_DIM, POOL_GROUP_DIM), POOL_GROUP_DIM),
        "pool_scale": gain(ks[8], (DEPTH, POOL_WIDTH)),
        "w_out": nrm(ks[9], (DEPTH, D, D), D),
        "g_mem_q": gain(ks[10], (DEPTH, D)),
        "g_mem_kv": gain(ks[11], (DEPTH, D)),
        "w_mem_q": nrm(ks[12], (DEPTH, D, MEM_WIDTH), D),
        "w_mem_kv": nrm(ks[13], (DEPTH, D, 2 * MEM_WIDTH), D),
        "g_q_mem": gain(ks[14], (DEPTH, MEM_HEAD_DIM)),
        "g_k_mem": gain(ks[15], (DEPTH, MEM_HEAD_DIM)),
        "w_mem_out": nrm(ks[16], (DEPTH, MEM_WIDTH, D), MEM_WIDTH),
        "g_ffn": gain(ks[17], (DEPTH, D)),
        "w_gate_up": nrm(ks[18], (DEPTH, D, 2 * D_FF), D),
        "w_down": nrm(ks[19], (DEPTH, D_FF, D), D_FF),
    }

def first_block(x, mem, g_mix, w_in, b_forget, g_q_fox, g_k_fox, w_pool, pool_scale, w_out,
              g_mem_q, g_mem_kv, w_mem_q, w_mem_kv, g_q_mem, g_k_mem, w_mem_out,
              g_ffn, w_gate_up, w_down):
    B, S, _ = x.shape
    h = x
    for l in range(DEPTH):
        xn = rmsnorm(h, g_mix[l])
        z = jnp.einsum('bsd,dc->bsc', xn, w_in[l])
        q = z[..., :FOX_WIDTH]
        k = z[..., FOX_WIDTH:2 * FOX_WIDTH]
        v = z[..., 2 * FOX_WIDTH:3 * FOX_WIDTH]
        p_in = z[..., 3 * FOX_WIDTH:3 * FOX_WIDTH + POOL_WIDTH]
        f_logit = z[..., 3 * FOX_WIDTH + POOL_WIDTH:] + b_forget[l]
        q = rmsnorm(head_split(q, FOX_HEADS, FOX_HEAD_DIM), g_q_fox[l]).transpose(0, 2, 1, 3)
        k = rmsnorm(head_split(k, FOX_HEADS, FOX_HEAD_DIM), g_k_fox[l]).transpose(0, 2, 1, 3)
        v = head_split(v, FOX_HEADS, FOX_HEAD_DIM).transpose(0, 2, 1, 3)
        fox = forgetting_attention(q, k, v, f_logit.transpose(0, 2, 1))
        fox = fox.transpose(0, 2, 1, 3).reshape(B, S, FOX_WIDTH)
        pool = multiscale_pool(p_in, w_pool[l], pool_scale[l])
        h = h + jnp.einsum('bsc,cd->bsd', jnp.concatenate([fox, pool], axis=-1), w_out[l])

        hn = rmsnorm(h, g_mem_q[l])
        mn = rmsnorm(mem, g_mem_kv[l])
        mq = rmsnorm(head_split(jnp.einsum('bsd,dc->bsc', hn, w_mem_q[l]), MEM_HEADS, MEM_HEAD_DIM), g_q_mem[l])
        mkv = jnp.einsum('bmd,dc->bmc', mn, w_mem_kv[l])
        mk = rmsnorm(head_split(mkv[..., :MEM_WIDTH], MEM_HEADS, MEM_HEAD_DIM), g_k_mem[l])
        mv = head_split(mkv[..., MEM_WIDTH:], MEM_HEADS, MEM_HEAD_DIM)
        sc = jnp.einsum('bshd,bmhd->bhsm', mq, mk, preferred_element_type=jnp.float32) * (MEM_HEAD_DIM ** -0.5)
        pm = jax.nn.softmax(sc, axis=-1).astype(mv.dtype)
        mo = jnp.einsum('bhsm,bmhd->bshd', pm, mv).reshape(B, S, MEM_WIDTH)
        h = h + jnp.einsum('bsc,cd->bsd', mo, w_mem_out[l])

        hn = rmsnorm(h, g_ffn[l])
        gu = jnp.einsum('bsd,df->bsf', hn, w_gate_up[l])
        act = jax.nn.silu(gu[..., :D_FF]) * gu[..., D_FF:]
        h = h + jnp.einsum('bsf,fd->bsd', act, w_down[l])
    return h


DEPTH_2 = 2

N_A_LAYERS = DEPTH_2 // 2
N_B_LAYERS = DEPTH_2 - N_A_LAYERS
HEAD_DIM = 64
N_HEADS = D_MODEL // (2 * HEAD_DIM)
D_FF_2 = 2816
CONV_WIDTH = 3
NORM_EPS = 1e-6


def rmsnorm_2(x, g):
    xf = x.astype(jnp.float32)
    y = xf * lax.rsqrt(jnp.mean(xf * xf, axis=-1, keepdims=True) + NORM_EPS)
    return (y * g.astype(jnp.float32)).astype(x.dtype)

def swiglu(x, w_gu, w_down):
    gate, up = jnp.split(x @ w_gu, 2, axis=-1)
    return (jax.nn.silu(gate) * up) @ w_down

def short_gated_conv(xn, w_in, conv_k, w_out):
    b_gate, c_gate, z = jnp.split(xn @ w_in, 3, axis=-1)
    u = c_gate * z
    rhs = conv_k[:, None, :].astype(u.dtype)
    conv = lax.conv_general_dilated(
        u, rhs, window_strides=(1,), padding=[(CONV_WIDTH - 1, 0)],
        dimension_numbers=('NWC', 'WIO', 'NWC'), feature_group_count=u.shape[-1])
    return (b_gate * conv) @ w_out

def alibi_slopes(n_heads):
    return 2.0 ** (-8.0 * jnp.arange(1, n_heads + 1, dtype=jnp.float32) / n_heads)

def shared_kv(h, kv_norm_g, w_kv):
    Bsz, S, _ = h.shape
    k_flat, v_flat = jnp.split(rmsnorm_2(h, kv_norm_g) @ w_kv, 2, axis=-1)
    k = k_flat.reshape(Bsz, S, N_HEADS, 2, HEAD_DIM)
    v = v_flat.reshape(Bsz, S, N_HEADS, 2 * HEAD_DIM)
    return k, v

def diff_attention(xn, k, v, w_q, lam_params, subln_g, w_o, lambda_init):
    Bsz, S, _ = xn.shape
    q = (xn @ w_q).reshape(Bsz, S, N_HEADS, 2, HEAD_DIM)
    lp = lam_params.astype(jnp.float32)
    lam = jnp.exp(jnp.sum(lp[0] * lp[1])) - jnp.exp(jnp.sum(lp[2] * lp[3])) + lambda_init
    scale = HEAD_DIM ** -0.5
    n_blocks = S // Q_BLOCK
    q_blocks = q.reshape(Bsz, n_blocks, Q_BLOCK, N_HEADS, 2, HEAD_DIM).swapaxes(0, 1)
    slopes = alibi_slopes(N_HEADS)
    kpos = jnp.arange(S)

    def one_block(args):
        q_blk, start = args
        qpos = start + jnp.arange(Q_BLOCK)
        dist = (qpos[:, None] - kpos[None, :]).astype(jnp.float32)
        s = jnp.einsum('bqhcd,bkhcd->bhcqk', q_blk, k,
                       preferred_element_type=jnp.float32) * scale
        s = s - slopes[None, :, None, None, None] * dist
        s = jnp.where(dist >= 0, s, -jnp.inf)
        p = jax.nn.softmax(s, axis=-1)
        a = p[:, :, 0] - lam * p[:, :, 1]
        return jnp.einsum('bhqk,bkhe->bqhe', a, v)

    o = lax.map(one_block, (q_blocks, jnp.arange(n_blocks) * Q_BLOCK))
    o = o.swapaxes(0, 1).reshape(Bsz, S, N_HEADS, 2 * HEAD_DIM).astype(jnp.float32)
    o = o * lax.rsqrt(jnp.mean(o * o, axis=-1, keepdims=True) + NORM_EPS)
    o = o * subln_g.astype(jnp.float32) * (1.0 - lambda_init)
    return o.reshape(Bsz, S, N_HEADS * 2 * HEAD_DIM).astype(xn.dtype) @ w_o

def second_inputs(seed: int = 0) -> dict:
    key = jax.random.key(seed)
    ks = jax.random.split(key, 16)
    D = D_MODEL
    nrm = lambda k, shape, fan_in: jax.random.normal(k, shape, jnp.float32) * fan_in ** -0.5
    x = jax.random.normal(ks[0], (BATCH, SEQ, D), jnp.float32)
    ffn_w_gu = nrm(ks[1], (DEPTH_2, 2, D, 2 * D_FF_2), D)
    ffn_w_down = nrm(ks[2], (DEPTH_2, 2, D_FF_2, D), D_FF_2)
    norm_g = 1.0 + 0.05 * jax.random.normal(ks[3], (DEPTH_2, 6, D), jnp.float32)
    conv_w_in = nrm(ks[4], (N_A_LAYERS, D, 3 * D), D)
    conv_k = nrm(ks[5], (N_A_LAYERS, CONV_WIDTH, D), CONV_WIDTH)
    conv_w_out = nrm(ks[6], (N_A_LAYERS, D, D), D)
    kv_norm_g = 1.0 + 0.05 * jax.random.normal(ks[7], (D,), jnp.float32)
    w_kv = nrm(ks[8], (D, 2 * D), D)
    attn_w_q = nrm(ks[9], (N_B_LAYERS, D, D), D)
    attn_lambda = 0.1 * jax.random.normal(ks[10], (N_B_LAYERS, 4, HEAD_DIM), jnp.float32)
    attn_subln_g = 1.0 + 0.05 * jax.random.normal(ks[11], (N_B_LAYERS, 2 * HEAD_DIM), jnp.float32)
    attn_w_o = nrm(ks[12], (N_B_LAYERS, D, D), D)
    return {"x": x, "ffn_w_gu": ffn_w_gu, "ffn_w_down": ffn_w_down, "norm_g": norm_g,
            "conv_w_in": conv_w_in, "conv_k": conv_k, "conv_w_out": conv_w_out,
            "kv_norm_g": kv_norm_g, "w_kv": w_kv, "attn_w_q": attn_w_q,
            "attn_lambda": attn_lambda, "attn_subln_g": attn_subln_g, "attn_w_o": attn_w_o}

def second_block(x, ffn_w_gu, ffn_w_down, norm_g, conv_w_in, conv_k, conv_w_out,
              kv_norm_g, w_kv, attn_w_q, attn_lambda, attn_subln_g, attn_w_o):
    h = x
    k = v = None
    for l in range(DEPTH_2):
        g = norm_g[l]
        if l == N_A_LAYERS:
            k, v = shared_kv(h, kv_norm_g, w_kv)
        h = h + 0.5 * rmsnorm_2(swiglu(rmsnorm_2(h, g[0]), ffn_w_gu[l, 0], ffn_w_down[l, 0]), g[1])
        xn = rmsnorm_2(h, g[2])
        if l < N_A_LAYERS:
            mix = short_gated_conv(xn, conv_w_in[l], conv_k[l], conv_w_out[l])
        else:
            j = l - N_A_LAYERS
            lambda_init = 0.8 - 0.6 * math.exp(-0.3 * l)
            mix = diff_attention(xn, k, v, attn_w_q[j], attn_lambda[j],
                                 attn_subln_g[j], attn_w_o[j], lambda_init)
        h = h + rmsnorm_2(mix, g[3])
        h = h + 0.5 * rmsnorm_2(swiglu(rmsnorm_2(h, g[4]), ffn_w_gu[l, 1], ffn_w_down[l, 1]), g[5])
    return h


def setup_inputs(seed=0):
    out = dict(first_inputs(seed))
    for name, value in second_inputs(seed + 1).items():
        if name != "x":
            out[name + "_2"] = value
    return out


def reference(
    x, mem, g_mix, w_in, b_forget, g_q_fox, g_k_fox, w_pool, pool_scale, w_out, g_mem_q,
    g_mem_kv, w_mem_q, w_mem_kv, g_q_mem, g_k_mem, w_mem_out, g_ffn, w_gate_up, w_down,
    ffn_w_gu_2, ffn_w_down_2, norm_g_2, conv_w_in_2, conv_k_2, conv_w_out_2, kv_norm_g_2,
    w_kv_2, attn_w_q_2, attn_lambda_2, attn_subln_g_2, attn_w_o_2,
):
    x = first_block(
        x, mem, g_mix, w_in, b_forget, g_q_fox, g_k_fox, w_pool, pool_scale, w_out, g_mem_q,
        g_mem_kv, w_mem_q, w_mem_kv, g_q_mem, g_k_mem, w_mem_out, g_ffn, w_gate_up, w_down,
    )
    return second_block(
        x, ffn_w_gu_2, ffn_w_down_2, norm_g_2, conv_w_in_2, conv_k_2, conv_w_out_2, kv_norm_g_2,
        w_kv_2, attn_w_q_2, attn_lambda_2, attn_subln_g_2, attn_w_o_2,
    )


_drawn_inputs = setup_inputs


def setup_inputs(seed=0):
    import zlib

    import numpy as np

    out = dict(_drawn_inputs(seed))
    spreads = {}
    factors = {'g_q_fox': 3.135,
     'g_k_fox': 3.151,
     'g_mem_q': 6.713,
     'g_mem_kv': 4.337,
     'g_q_mem': 6.553,
     'g_k_mem': 6.325,
     'g_ffn': 5.26,
     'kv_norm_g_2': 28.392,
     'attn_subln_g_2': 39.512,
     'norm_g_2': 6.601,
     'attn_lambda_2': 8.0}
    for name, (base, spread) in spreads.items():
        noise = np.random.default_rng([zlib.crc32(name.encode()), seed]).standard_normal(out[name].shape)
        drawn = base * np.exp(spread * noise) if base else spread * noise
        out[name] = __import__('jax').numpy.asarray(drawn.astype(out[name].dtype))
    for name, factor in factors.items():
        out[name] = (out[name] * factor).astype(out[name].dtype)
    return out
```

```python
import math
from contextlib import ExitStack

import numpy as np
import concourse.bass as bass
from concourse import mybir

F32 = mybir.dt.float32
F32R = mybir.dt.float32r
ALU = mybir.AluOpType
ACT = mybir.ActivationFunctionType
AX = mybir.AxisListType

P = 128
S = 256
TOKS = S // P
D = 1024
KD = D // P
HALF = 512
FOX_H, FOX_DH = 8, 64
MEM_H, MEM_DH = 4, 128
DIFF_H, DIFF_DH = 8, 64
FF = 2816
FJ = FF // 256
WINDOWS = (2, 4, 8, 16)
EPS = 1e-6
NEG = -1.0e37
RING = 3
UNIT = 2048

U_MEMKV, U_IN, U_OUT, U_MQ, U_MO = 0, 4, 12, 16, 18
U_FFN = (20, 53, 102, 143, 184)
U_CIN, U_COUT, U_KV, U_Q, U_O = 86, 98, 135, 176, 180
UNITS = 217

XT_ORDER = [("mem", 8), ("x", 8), ("mix", 8), ("mq", 8), ("mo", 4), ("ffn0", 8), ("ffn1", 8), ("cin", 8),
            ("cout", 8), ("ffn2", 8), ("kv", 8), ("ffn3", 8), ("q", 8), ("ao", 8), ("ffn4", 8)]
XT = {}
TD = {}
_x = _t = 0
for _n, _c in XT_ORDER:
    XT[_n], TD[_n] = _x, _t
    _x += _c
    if _n != "cout":
        _t += _c

ST = {n: i for i, n in enumerate(["mem", "h0", "h1", "h2", "h3", "y0", "h4", "y1", "h5", "y2", "h6", "y3",
                                  "h7", "y4", "h8", "y5"])}
H_UP = {n: i for i, n in enumerate(["mq", "ffn0", "ffn1", "cin", "ffn2", "kv", "q", "ffn4", "out"])}
H_UP["ffn3"] = H_UP["kv"]

G_N2, G_CONV, G_ROWS1 = 0, 96, 120
G_MIX, G_MEMKV, G_MEMQ, G_FFN, G_KV, G_POOL, G_SUB, G_QF, G_KF, G_QM, G_KM = (
    120, 128, 136, 144, 152, 160, 164, 165, 166, 167, 168)
G_ROWS2 = 49
G_ONE = 169


def n2(layer, i):
    return G_N2 + (layer * 6 + i) * KD


def build(nc, a, out):
    lambda_init = 0.8 - 0.6 * math.exp(-0.3)
    slopes = [2.0 ** (-8.0 * (h + 1) / DIFF_H) for h in range(DIFF_H)]

    ctx = ExitStack()
    with ctx:
        def sb(name, shape, dt=F32):
            return ctx.enter_context(nc.sbuf_tensor(name, shape, dt))

        def sem(name):
            return ctx.enter_context(nc.semaphore(name))

        raw = [sb(f"w_raw{s}", [P, UNIT]) for s in range(RING)]
        whi = [sb(f"w_hi{s}", [P, UNIT], F32R) for s in range(RING)]
        wlo = [sb(f"w_lo{s}", [P, UNIT], F32R) for s in range(RING)]
        xhi = sb("xt_hi", [P, KD, S], F32R)
        xlo = sb("xt_lo", [P, KD, S], F32R)
        h = sb("h", [P, TOKS, D])
        nat = sb("nat", [P, TOKS, D])
        Z = sb("Z", [P, TOKS, 4 * HALF])
        QT = sb("QT", [P, 8, S])
        KT = sb("KT", [P, 8, S])
        VD = sb("VD", [P, TOKS, D])
        memKT = sb("memKT", [P, MEM_H, S])
        memV = sb("memV", [P, TOKS, HALF])
        ahi = sb("act_hi", [P, 2 * S], F32R)
        alo = sb("act_lo", [P, 2 * S], F32R)
        work = sb("work", [P, 4096])
        SQ = sb("SQ", [P, 2 * HALF])
        junk = sb("junk", [P, HALF])
        tmp = sb("tmp", [P, TOKS, HALF])
        gpost = sb("gpost", [P, 2, D])
        gains = sb("gains", [P, 176])
        grow1 = sb("grow1", [P, P])
        grow2 = sb("grow2", [P, P])
        ident = sb("ident", [P, P])
        tri = sb("tri", [P, TOKS, S])
        foxmask = sb("foxmask", [P, 384])
        dist = sb("dist", [P, 384])
        sel = tmp[0:FOX_H, :, :].rearrange("p t (h c) -> p (t h) c", c=P)
        cnt16 = sb("cnt16", [P, 4, 16])
        wpool = sb("wpool", [P, 4, P])
        wf = sb("wf", [P, KD, FOX_H])
        wfhi = sb("wf_hi", [P, KD, FOX_H], F32R)
        wflo = sb("wf_lo", [P, KD, FOX_H], F32R)
        bf = sb("b_forget", [P, FOX_H])
        lamp = sb("lamp", [P, 4, DIFF_DH])
        lam4 = sb("lam4", [P, 4])
        SS = sb("row_squares", [P, len(ST), TOKS, 2])
        SV = sb("row_var", [P, len(ST), TOKS])
        RS = sb("row_rstd", [P, len(ST), TOKS])
        HS = sb("head_squares", [P, 5, 16])
        HV = sb("head_var", [P, 5, 16])
        HR = sb("head_rstd", [P, 5, 16])
        mhalf = sb("minus_half", [P, 16])
        fl = sb("forget", [P, 4, 16])
        cn = sb("cum_nat", [P, TOKS, FOX_H])
        cT = sb("cum_T", [FOX_H, S])
        nmax = sb("neg_max", [P, 32])
        lsum = sb("exp_sum", [P, 32])
        linv = sb("exp_inv", [P, 32])

        scores = [work[:, 384 * i:384 * i + 384] for i in range(4)]
        probs = [work[:, 1536 + 384 * i:1920 + 384 * i] for i in range(4)]
        pT = [work[:, 3072 + 512 * i:3584 + 512 * i] for i in range(2)]
        gate = work[:, 0:512].rearrange("p (t c) -> p t c", t=2)
        actn = work[:, 512:1024].rearrange("p (t c) -> p t c", t=2)
        uT = [work[:, 1024 + 258 * i:1282 + 258 * i] for i in range(2)]
        taps = [work[:, 1600 + 256 * i:1856 + 256 * i] for i in range(2)]
        convx = [work[:, 2112 + 256 * i:2368 + 256 * i] for i in range(2)]
        mprobs = [work[:, 512 * i:512 * i + 512] for i in range(4)]
        PAD = 8
        poolT = VD[:, :, :].rearrange("p t c -> p (t c)")[:, 0:4 * (PAD + S)].rearrange("p (g t) -> p g t", g=4)
        kt_hi = KT[:, 4:8, :].rearrange("p c t -> p (c t)")
        win = [kt_hi[:, (PAD + S) * i:(PAD + S) * (i + 1)] for i in range(2)]
        wmean = kt_hi[:, 2 * (PAD + S):2 * (PAD + S) + S]
        mixT = QT[:, 4:8, :]

        osq = work[:, 0:2048].rearrange("p (t c) -> p t c", t=2)
        conv_places = [Z[:, :, 0:512], Z[:, :, 512:1024], Z[:, :, 1024:1536], Z[:, :, 1536:2048],
                       nat[:, :, 0:512], nat[:, :, 512:1024]]
        kv_places = [Z[:, :, 0:512], Z[:, :, 512:1024], VD[:, :, 0:512], VD[:, :, 512:1024]]

        B = [ctx.enter_context(nc.psum_tensor(f"B{i}", [P, HALF], F32)) for i in range(6)]
        T = [ctx.enter_context(nc.psum_tensor(f"T{i}", [P, HALF], F32)) for i in range(2)]
        PAIR = [(B[0], B[1]), (B[2], B[3]), (B[4], B[5])]
        GU = PAIR[2]

        w_loaded = [sem(f"w_loaded{s}") for s in range(RING)]
        w_hi, w_lo, w_used = sem("w_hi_written"), sem("w_lo_written"), sem("w_unit_used")
        in_mem, in_x, in_id, in_small, in_const = (sem("mem_in"), sem("x_in"), sem("ident_in"), sem("small_in"),
                                                   sem("const_in"))
        in_gain = sem("gain_rows_in")
        gain_T, gain_ok = sem("gains_turned"), sem("gains_ready")
        post_in = [sem(f"post_gain{i}_in") for i in range(2)]
        t_done, xt_hi, xt_lo = sem("chunk_turned"), sem("xt_hi_written"), sem("xt_lo_written")
        ssq, rstd = sem("row_squares_summed"), sem("row_rstd_ready")
        half_up = sem("h_half_updated")
        half0 = sem("down_half0_done")
        ev_a, ev_d = sem("group_evacuated_tok0"), sem("group_evacuated_tok1")
        hn_sq, hn_sum, hn_r, hn_x = sem("head_squared"), sem("head_summed"), sem("head_rstd"), sem("head_normed")
        ht, ht_a, ht_d = sem("heads_turned"), sem("heads_T_bank0_out"), sem("heads_T_bank1_out")
        wf_hi_s, wf_lo_s = sem("wf_hi_written"), sem("wf_lo_written")
        f_done, f_out, f_act, f_log = sem("f_product"), sem("f_logit_out"), sem("f_exp_ln"), sem("f_log_ready")
        c_done, c_out = sem("cumsum_done"), sem("cumsum_out")
        pt_done, pt_out = sem("pool_turned"), sem("pool_T_out")
        mixed_ok, py_done, py_out = sem("pool_mixed"), sem("pool_product"), sem("pool_out")
        at_s, at_m, at_x, at_e, at_r, at_c, at_v = (sem("scores_done"), sem("scores_masked"), sem("row_max_ready"),
                                                    sem("exp_done"), sem("probs_turned"), sem("probs_T_out"),
                                                    sem("values_done"))
        at_o, at_a = sem("attention_out"), sem("diff_probs_ready")
        pads_ok = sem("pool_pads_zero")
        lam_ok = sem("lambda_ready")
        gate_ok, act_ok, act_t, act_hi, act_lo = (sem("gate_ready"), sem("act_ready"), sem("act_turned"),
                                                  sem("act_hi_written"), sem("act_lo_written"))
        conv_p, conv_t, conv_u, conv_x = (sem("conv_product_ready"), sem("conv_turned"), sem("conv_u_out"),
                                          sem("conv_x_ready"))
        dve_step, act_step, pool_step = sem("dve_step"), sem("act_step"), sem("pool_step")
        out_done = sem("out_written")

        block = ctx.enter_context(nc.Block())

        M_S, M_X, M_E, M_R = FOX_H, 2 * FOX_H, 2 * FOX_H, FOX_H
        D_S, D_M, D_X, D_E, D_R = M_S + MEM_H, 2 * FOX_H, M_X + MEM_H, M_E + 2 * MEM_H, M_R + MEM_H
        HT_KM, HT_QF, HT_KF, HT_QM, HT_KD, HT_QD = 0, 1, 2, 3, 4, 6
        EV_MEMKV, EV_IN, EV_MQ, EV_CIN, EV_KV, EV_Q = 0, 2, 6, 7, 13, 17

        @block.sync
        def _(sp):
            def load(u, slot, parts):
                if not (isinstance(u, int) and u < RING):
                    sp.wait_ge(w_lo, u - RING + 1)
                for dst, src in parts:
                    sp.dma_start(dst, src).then_inc(w_loaded[slot], 16)

            def k_unit(u, w, k0, col):
                v = w.rearrange("(k p) f -> p k f", p=P)
                r = raw[u % RING][:, :].rearrange("p (k c) -> p k c", k=4)
                load(u, u % RING, [(r[:, i:i + 2, :], v[:, k0 + i:k0 + i + 2, col:col + HALF]) for i in (0, 2)])

            def ffn(u0, w_gu, w_dn):
                gu = w_gu.rearrange("(k p) f -> p k f", p=P)
                dn = w_dn.rearrange("(k p) f -> k p f", p=P)

                def up(j, u, slot, k0):
                    r = raw[slot][:, :].rearrange("p (k c) -> p k c", k=4)
                    load(u, slot, [(r[:, :, 0:256], gu[:, k0:k0 + 4, bass.ds(j * 256, 256)]),
                                   (r[:, :, 256:512], gu[:, k0:k0 + 4, bass.ds(j * 256 + FF, 256)])])

                def down(j, u, slot):
                    rows = w_dn[bass.ds(j * 256, 256), :].rearrange("(k p) f -> p k f", p=P)
                    load(u, slot, [(raw[slot][:, D * k:D * k + D], rows[:, k, :]) for k in range(2)])

                up(0, u0, u0 % RING, 0)
                up(0, u0 + 1, (u0 + 1) % RING, 4)

                def step(i):
                    up(i + 1, u0 + 2 + 3 * i, (u0 + 2) % RING, 0)
                    up(i + 1, u0 + 3 + 3 * i, (u0 + 3) % RING, 4)
                    down(i, u0 + 4 + 3 * i, (u0 + 4) % RING)

                with sp.Fori(0, FJ - 2) as i:
                    step(i)
                step(FJ - 2)
                down(FJ - 1, u0 + 32, (u0 + 32) % RING)

            def k_groups(u0, w, cols):
                for g, col in enumerate(cols):
                    k_unit(u0 + 2 * g, w, 0, col)
                    k_unit(u0 + 2 * g + 1, w, 4, col)

            k_groups(U_MEMKV, a["w_mem_kv"][0], (0, 512))
            k_groups(U_IN, a["w_in"][0], (0, 512, 1536, 1024))
            k_groups(U_OUT, a["w_out"][0], (0, 512))
            k_groups(U_MQ, a["w_mem_q"][0], (0,))
            k_unit(U_MO, a["w_mem_out"][0], 0, 0)
            k_unit(U_MO + 1, a["w_mem_out"][0], 0, 512)
            ffn(U_FFN[0], a["w_gate_up"][0], a["w_down"][0])
            ffn(U_FFN[1], a["ffn_w_gu_2"][0, 0], a["ffn_w_down_2"][0, 0])
            k_groups(U_CIN, a["conv_w_in_2"][0], (0, 1024, 2048, 512, 1536, 2560))
            k_groups(U_COUT, a["conv_w_out_2"][0], (0, 512))
            ffn(U_FFN[2], a["ffn_w_gu_2"][0, 1], a["ffn_w_down_2"][0, 1])
            k_groups(U_KV, a["w_kv_2"], (0, 512, 1024, 1536))
            ffn(U_FFN[3], a["ffn_w_gu_2"][1, 0], a["ffn_w_down_2"][1, 0])
            k_groups(U_Q, a["attn_w_q_2"][0], (0, 512))
            k_groups(U_O, a["attn_w_o_2"][0], (0, 512))
            ffn(U_FFN[4], a["ffn_w_gu_2"][1, 1], a["ffn_w_down_2"][1, 1])
            for half in range(2):
                sp.wait_ge(half_up, 2 * H_UP["out"] + half + 1)
                for t in range(TOKS):
                    sp.dma_start(out[0, t * P:t * P + P, half * HALF:half * HALF + HALF],
                                 h[:, t, half * HALF:half * HALF + HALF]).then_inc(out_done, 16)
            sp.wait_ge(out_done, 64)

        @block.gpsimd
        def _(pool):
            steps = [0]

            def link(ins):
                steps[0] += 1
                ins.then_inc(pool_step, 1)
                pool.wait_ge(pool_step, steps[0])

            for o, n in ((G_MIX, "g_mix"), (G_MEMKV, "g_mem_kv"), (G_MEMQ, "g_mem_q"), (G_FFN, "g_ffn")):
                pool.dma_start(grow2[o - G_ROWS1:o - G_ROWS1 + 8, :],
                               a[n][0].rearrange("(k c) -> k c", c=P)).then_inc(in_gain, 16)
            pool.dma_start(grow2[32:40, :], a["kv_norm_g_2"].rearrange("(k c) -> k c", c=P)).then_inc(in_gain, 16)
            pool.dma_start(grow2[40:44, :], a["pool_scale"][0].rearrange("(k c) -> k c", c=P)).then_inc(in_gain, 16)
            pool.dma_start(grow2[44:45, :], a["attn_subln_g_2"]).then_inc(in_gain, 16)
            for r, n in ((45, "g_q_fox"), (46, "g_k_fox")):
                for c in range(2):
                    pool.dma_start(grow2[r:r + 1, 64 * c:64 * c + 64], a[n]).then_inc(in_gain, 16)
            pool.dma_start(grow2[47:48, :], a["g_q_mem"]).then_inc(in_gain, 16)
            pool.dma_start(grow2[48:49, :], a["g_k_mem"]).then_inc(in_gain, 16)
            pool.dma_start(grow1[0:96, :], a["norm_g_2"].rearrange("l i (k c) -> (l i k) c", c=P)).then_inc(in_gain, 16)
            pool.dma_start(grow1[96:120, :], a["conv_k_2"].rearrange("l w (k c) -> (l w k) c", c=P)).then_inc(in_gain, 16)
            pool.memset(mhalf[:, :], -0.5).then_inc(pool_step, 1)
            steps[0] += 1
            pool.wait_ge(pool_step, steps[0])
            with nc.allow_non_contiguous_dma(reason="8 columns of w_in"):
                pool.dma_start(wf[:, :, :], a["w_in"][0].rearrange("(k p) f -> p k f", p=P)[:, :, 2048:2056])\
                    .then_inc(in_small, 16)
            pool.dma_start(bf[:, :], a["b_forget"][0].partition_broadcast(P)).then_inc(in_small, 16)
            pool.dma_start(wpool[:, :, :], a["w_pool"][0].rearrange("g c d -> c g d")).then_inc(in_small, 16)
            pool.dma_start(lamp[:, :, :], a["attn_lambda_2"][0].partition_broadcast(P)).then_inc(in_small, 16)
            for dst, name in ((tri, "c_tri"), (foxmask, "c_mask"), (dist, "c_dist"), (sel, "c_sel"), (cnt16, "c_cnt")):
                full = (slice(None),) * len(dst.shape)
                pool.dma_start(dst[full], a[name][full]).then_inc(in_const, 16)

            def post_gain(b, layer, i):
                if b >= 2:
                    pool.wait_ge(half_up, 2 * (3 + b - 2) + 2)
                pool.dma_start(gpost[:, b % 2, :], a["norm_g_2"][layer, i].partition_broadcast(P))\
                    .then_inc(post_in[b % 2], 16)

            def windows():
                pool.wait_ge(pt_out, 2)
                pool.wait_ge(in_const, 80)
                for g, w in enumerate(WINDOWS):
                    if g == 0:
                        pool.wait_ge(pads_ok, 3)
                    src = poolT[:, g, :]
                    for level in range(g + 1):
                        d = 1 << level
                        dst = win[level % 2]
                        link(pool.tensor_tensor(dst[:, PAD:PAD + S], src[:, PAD:PAD + S], src[:, PAD - d:PAD + S - d],
                                                ALU.add))
                        src = dst
                    link(pool.tensor_scalar(wmean, src[:, PAD:PAD + S], 1.0 / w, 0.0, ALU.mult, ALU.add))
                    link(pool.tensor_tensor(wmean[:, 0:16], src[:, PAD:PAD + 16], cnt16[:, g, :], ALU.mult))
                    pool.tensor_tensor(mixT[:, g, :], wmean, poolT[:, g, PAD:PAD + S], ALU.subtract)\
                        .then_inc(mixed_ok, 1)
                    pool.wait_ge(mixed_ok, g + 1)

            def rsqrt(dst, var, src, scale, eps, done):
                link(pool.tensor_scalar(var, src, scale, eps, ALU.mult, ALU.add))
                pool.tensor_tensor(dst, var, mhalf[:, 0:dst.shape[1]], ALU.pow).then_inc(done, 1)

            def row_stat(name, m=1.0):
                s = ST[name]
                pool.wait_ge(ssq, 4 * s + 4)
                link(pool.tensor_tensor(SV[:, s, :], SS[:, s, :, 0], SS[:, s, :, 1], ALU.add))
                rsqrt(RS[:, s, :], SV[:, s, :], SV[:, s, :], m / D, m * EPS, rstd)

            def head_stat(n, count, dh, m=1.0):
                pool.wait_ge(hn_sum, n + 1)
                rsqrt(HR[:, n, 0:count], HV[:, n, 0:count], HS[:, n, 0:count], m / dh, m * EPS, hn_r)

            post_gain(0, 0, 1)
            post_gain(1, 0, 3)
            row_stat("mem")
            head_stat(0, TOKS * MEM_H, MEM_DH)
            row_stat("h0")
            head_stat(1, TOKS * FOX_H, FOX_DH)
            head_stat(2, TOKS * FOX_H, FOX_DH)
            windows()
            row_stat("h1")
            head_stat(3, TOKS * MEM_H, MEM_DH)
            row_stat("h2")
            row_stat("h3")
            row_stat("y0", 4.0)
            row_stat("h4")
            row_stat("y1")
            post_gain(2, 0, 5)
            row_stat("h5")
            row_stat("y2", 4.0)
            post_gain(3, 1, 1)
            row_stat("h6")
            row_stat("y3", 4.0)
            post_gain(4, 1, 3)
            row_stat("h7")
            head_stat(4, TOKS * DIFF_H, 2 * DIFF_DH, 1.0 / (1.0 - lambda_init) ** 2)
            row_stat("y4")
            post_gain(5, 1, 5)
            row_stat("h8")
            row_stat("y5", 4.0)

        @block.scalar
        def _(act):
            act.dma_start(ident[:, :], a["c_ident"]).then_inc(in_id, 16)
            act.dma_start(nat[:, :, :], a["mem"][0].rearrange("(t p) d -> p t d", p=P)).then_inc(in_mem, 16)
            act.dma_start(h[:, :, :], a["x"][0].rearrange("(t p) d -> p t d", p=P)).then_inc(in_x, 16)

            def split(u, slot, n):
                act.wait_ge(w_loaded[slot], 32 * (n + 1))
                if not (isinstance(u, int) and u < RING):
                    act.wait_ge(w_used, u - RING + 1)
                act.activation(whi[slot][:, :], raw[slot][:, :], ACT.Copy).then_inc(w_hi, 1)

            def split_at(*units):
                for u in units:
                    if u < UNITS:
                        split(u, u % RING, u // RING)

            def turn_out(name, gain_cols, chunks=KD):
                for k in range(chunks):
                    act.wait_ge(t_done, TD[name] + k + 1)
                    g = gain_cols(k)
                    act.activation(xhi[:, k, :], T[k % 2][:, 0:S], ACT.Copy, scale=gains[:, g:g + 1])\
                        .then_inc(xt_hi, 1)

            def row_squares(stat, src, waits):
                for half in range(2):
                    act.wait_ge(*waits[half])
                    for t in range(TOKS):
                        if ST[stat] or half or t:
                            act.wait_ge(ssq, 4 * ST[stat] + 2 * half + t)
                        act.activation(junk[:, :], src(t, half), ACT.Square,
                                       accum_out=SS[:, ST[stat], t, half:half + 1]).then_inc(ssq, 1)

            def h_squares(stat, reader):
                m = H_UP[reader]
                row_squares(stat, lambda t, half: h[:, t, half * HALF:half * HALF + HALF],
                            [(half_up, 2 * m + 1), (half_up, 2 * m + 2)])

            def sum_squares(stat, waits):
                row_squares(stat, lambda t, half: PAIR[half][t][:, :], waits)

            def evac(e, u_last, dst, pair, stat):
                act.wait_ge(w_used, u_last + 1)
                act.wait_ge(rstd, ST[stat] + 1)
                act.activation(dst, pair[0][:, :], ACT.Copy, scale=RS[:, ST[stat], 0:1]).then_inc(ev_a, 1)

            def head_square(n, src, e):
                act.wait_ge(ev_a, e + 1)
                act.wait_ge(ev_d, e + 1)
                if n:
                    act.wait_ge(hn_sum, n)
                act.activation(SQ[:, :].rearrange("p (t c) -> p t c", t=2), src, ACT.Square).then_inc(hn_sq, 1)

            def heads_out(n, dst, gain_col=None, scale=1.0):
                act.wait_ge(ht, 2 * n + 1)
                g = scale if gain_col is None else gains[:, gain_col:gain_col + 1]
                act.activation(dst, T[0][:, :].rearrange("p (c t) -> p c t", c=2), ACT.Copy, scale=g)\
                    .then_inc(ht_a, 1)

            split_at(0, 1)
            act.wait_ge(gain_ok, 5)
            turn_out("mem", lambda k: G_MEMKV + k)
            row_squares("mem", lambda t, half: nat[:, t, half * HALF:half * HALF + HALF], [(in_mem, 16)] * 2)
            split_at(2, 3)
            evac(EV_MEMKV, 1, nat[:, 0, 0:HALF], PAIR[0], "mem")
            head_square(0, nat[:, :, 0:HALF], EV_MEMKV)
            split_at(4, 5)
            evac(EV_MEMKV + 1, 3, memV[:, 0, :], PAIR[1], "mem")
            turn_out("x", lambda k: G_MIX + k)
            row_squares("h0", lambda t, half: h[:, t, half * HALF:half * HALF + HALF], [(in_x, 16)] * 2)
            act.wait_ge(in_small, 64)
            act.activation(wfhi[:, :, :], wf[:, :, :], ACT.Copy).then_inc(wf_hi_s, 1)
            split_at(6, 7)
            evac(EV_IN, 5, Z[:, 0, 0:512], PAIR[2], "h0")
            head_square(1, Z[:, :, 0:512], EV_IN)
            split_at(8, 9)
            evac(EV_IN + 1, 7, Z[:, 0, 512:1024], PAIR[0], "h0")
            head_square(2, Z[:, :, 512:1024], EV_IN + 1)
            act.wait_ge(f_out, 3)
            act.activation(fl[:, 2, :], fl[:, 1, :], ACT.Exp, scale=-1.0).then_inc(f_act, 1)
            act.wait_ge(f_act, 1)
            act.activation(fl[:, 3, :], fl[:, 2, :], ACT.Ln, bias=1.0).then_inc(f_act, 1)
            act.wait_ge(lam_ok, 2)
            act.activation(lam4[:, 2:4], lam4[:, 0:2], ACT.Exp).then_inc(lam_ok, 1)
            split_at(10)
            heads_out(HT_KM, memKT[:, 0:2, :], G_KM)
            split_at(11)
            evac(EV_IN + 2, 9, Z[:, 0, 1024:1536], PAIR[1], "h0")
            heads_out(HT_QF, QT[:, 0:2, :], G_QF)
            split_at(12)
            heads_out(HT_KF, KT[:, 0:2, :], G_KF)
            split_at(13)
            evac(EV_IN + 3, 11, Z[:, 0, 1536:2048], PAIR[2], "h0")
            act.wait_ge(pt_done, 1)
            act.wait_ge(pads_ok, 3)
            act.activation(poolT[:, 0:2, PAD:PAD + S], T[0][:, :].rearrange("p (c t) -> p c t", c=2), ACT.Copy)\
                .then_inc(pt_out, 1)

            def probs_out(r0, i, cols):
                act.wait_ge(at_r, r0 + i + 1)
                if i >= 2:
                    act.wait_ge(at_v, r0 + i - 1)
                act.activation(pT[i % 2][:, 0:cols], T[i % 2][:, 0:cols], ACT.Copy).then_inc(at_c, 1)

            def causal_exp(x0, col0, i):
                act.wait_ge(at_x, x0 + 2 * i + 2)
                for t, c0, c1 in ((0, 0, 128), (1, 128, 384)):
                    col = col0 + 2 * i + t
                    act.activation(probs[i % 4][:, c0:c1], scores[i % 4][:, c0:c1], ACT.Exp,
                                   bias=nmax[:, col:col + 1], accum_out=lsum[:, col:col + 1]).then_inc(at_e, 1)

            for i in range(FOX_H + 1):
                if i < FOX_H:
                    if i >= 4:
                        act.wait_ge(at_r, i - 3)
                    causal_exp(0, 0, i)
                if i:
                    probs_out(0, i - 1, 384)
            act.wait_ge(py_done, 1)
            for t in range(TOKS):
                act.activation(nat[:, t, HALF:D], B[t][:, :], ACT.Copy).then_inc(py_out, 1)
            turn_out("mix", lambda k: G_ONE if k < 4 else G_POOL + k - 4)
            split_at(14, 15, 16, 17)
            turn_out("mq", lambda k: G_MEMQ + k)
            h_squares("h1", "mq")
            split_at(18, 19)
            evac(EV_MQ, 17, Z[:, 0, 0:512], PAIR[2], "h1")
            head_square(3, Z[:, :, 0:512], EV_MQ)
            heads_out(HT_QM, QT[:, 0:2, :], G_QM)
            for i in range(MEM_H + 1):
                if i < MEM_H:
                    act.wait_ge(at_x, M_X + i + 1)
                    for t in range(TOKS):
                        col = 2 * i + t
                        act.activation(mprobs[i][:, t * S:t * S + S], B[i][:, t * S:t * S + S], ACT.Exp,
                                       bias=nmax[:, col:col + 1], accum_out=lsum[:, col:col + 1]).then_inc(at_e, 1)
                if i:
                    probs_out(M_R, i - 1, 512)
            turn_out("mo", lambda k: G_ONE, chunks=4)
            split_at(20, 21)

            def ffn(f, stat, reader, gain, squares=True):
                u0 = U_FFN[f]
                v = u0 + 2
                turn_out(reader, lambda k: gain + k)
                if squares:
                    h_squares(stat, reader)

                def gate_of(j, u):
                    act.wait_ge(w_used, u + 1)
                    if not (isinstance(j, int) and j == 0 and f == 0):
                        act.wait_ge(act_ok, 2 * (FJ * f + j))
                    for t in range(TOKS):
                        act.activation(gate[:, t, :], GU[t][:, 0:256], ACT.Silu,
                                       scale=RS[:, ST[stat], t:t + 1]).then_inc(gate_ok, 1)

                def act_out(j):
                    act.wait_ge(act_t, FJ * f + j + 1)
                    act.activation(ahi[:, :], T[0][:, :], ACT.Copy).then_inc(act_hi, 1)

                split_at(u0 + 2, u0 + 3)
                act.wait_ge(rstd, ST[stat] + 1)
                gate_of(0, u0 + 1)

                def step(i, last):
                    split(v + 3 * i + 2, (v + 2) % RING, i + (v + 2) // RING)
                    act_out(i)
                    split(v + 3 * i + 3, (v + 3) % RING, i + (v + 3) // RING)
                    gate_of(i + 1, v + 3 * i + 1)
                    if not (last and v + 3 * i + 4 >= UNITS):
                        split(v + 3 * i + 4, (v + 4) % RING, i + (v + 4) // RING)

                with act.Fori(0, FJ - 2) as i:
                    step(i, False)
                step(FJ - 2, True)
                act_out(FJ - 1)
                split_at(u0 + 34)

            def down_waits(f):
                return [(half0, f + 1), (w_used, U_FFN[f] + 33)]

            ffn(0, "h2", "ffn0", G_FFN)
            ffn(1, "h3", "ffn1", n2(0, 0))
            sum_squares("y0", down_waits(1))
            turn_out("cin", lambda k: n2(0, 2) + k)
            h_squares("h4", "cin")
            for g in range(6):
                split_at(U_CIN + 2 * g + 2, U_CIN + 2 * g + 3)
                evac(EV_CIN + g, U_CIN + 2 * g + 1, conv_places[g][:, 0, :], PAIR[g % 3], "h4")

            def conv_hi(k):
                act.wait_ge(conv_x, k + 1)
                act.activation(xhi[:, k, :], convx[k % 2], ACT.Copy).then_inc(xt_hi, 1)

            for k in range(KD):
                act.wait_ge(conv_t, k + 1)
                if k >= 2:
                    act.wait_ge(conv_x, k - 1)
                act.activation(uT[k % 2][:, 2:2 + S], T[k % 2][:, 0:S], ACT.Copy).then_inc(conv_u, 1)
                if k:
                    conv_hi(k - 1)
            conv_hi(KD - 1)
            split_at(*range(U_COUT + 2, U_COUT + 6))
            sum_squares("y1", [(w_used, U_COUT + 2), (w_used, U_COUT + 4)])
            ffn(2, "h5", "ffn2", n2(0, 4))
            sum_squares("y2", down_waits(2))
            turn_out("kv", lambda k: G_KV + k)
            h_squares("h6", "kv")
            for g in range(4):
                split_at(U_KV + 2 * g + 2, U_KV + 2 * g + 3)
                evac(EV_KV + g, U_KV + 2 * g + 1, kv_places[g][:, 0, :], PAIR[(g + 2) % 3], "h6")
            heads_out(HT_KD, KT[:, 0:2, :])
            heads_out(HT_KD + 1, KT[:, 4:6, :])
            ffn(3, "h6", "ffn3", n2(1, 0), squares=False)
            sum_squares("y3", down_waits(3))
            turn_out("q", lambda k: n2(1, 2) + k)
            h_squares("h7", "q")
            for g in range(2):
                split_at(U_Q + 2 * g + 2, U_Q + 2 * g + 3)
                evac(EV_Q + g, U_Q + 2 * g + 1, Z[:, 0, 512 * g:512 * g + 512], PAIR[(g + 2) % 3], "h7")
            heads_out(HT_QD, QT[:, 0:2, :], scale=DIFF_DH ** -0.5)
            heads_out(HT_QD + 1, QT[:, 4:6, :], scale=DIFF_DH ** -0.5)
            for i in range(DIFF_H + 1):
                if i < DIFF_H:
                    for m in (2 * i, 2 * i + 1):
                        if m >= 4:
                            act.wait_ge(at_r, D_R + i - 1)
                        causal_exp(D_X, 0, m)
                if i:
                    probs_out(D_R, i - 1, 384)
            act.wait_ge(at_v, D_R + DIFF_H)
            for g in range(2):
                for t in range(TOKS):
                    act.activation(osq[:, t, g * HALF:g * HALF + HALF], PAIR[g][t][:, :], ACT.Square)\
                        .then_inc(hn_sq, 1)
            turn_out("ao", lambda k: G_SUB)
            split_at(*range(U_O + 2, U_O + 6))
            sum_squares("y4", [(w_used, U_O + 2), (w_used, U_O + 4)])
            ffn(4, "h8", "ffn4", n2(1, 4))
            sum_squares("y5", down_waits(4))

        @block.vector
        def _(dve):
            steps = [0]

            def link(ins):
                steps[0] += 1
                ins.then_inc(dve_step, 1)
                dve.wait_ge(dve_step, steps[0])

            def split(u, slot):
                dve.wait_ge(w_hi, u + 1)
                dve.tensor_tensor(wlo[slot][:, :], raw[slot][:, :], whi[slot][:, :].bitcast(F32), ALU.subtract)\
                    .then_inc(w_lo, 1)

            def split_at(*units):
                for u in units:
                    if u < UNITS:
                        split(u, u % RING)

            def turn_out(name, gain_cols, chunks=KD):
                for k in range(chunks):
                    dve.wait_ge(xt_hi, XT[name] + k + 1)
                    g = gain_cols(k)
                    dve.scalar_tensor_tensor(out=xlo[:, k, :], in0=T[k % 2][:, 0:S], scalar=gains[:, g:g + 1],
                                             in1=xhi[:, k, :].bitcast(F32), op0=ALU.mult, op1=ALU.subtract)\
                       .then_inc(xt_lo, 1)

            def evac(e, u_last, dst, pair, stat):
                dve.wait_ge(w_used, u_last + 1)
                dve.wait_ge(rstd, ST[stat] + 1)
                dve.tensor_scalar(dst, pair[1][:, :], RS[:, ST[stat], 1:2], None, ALU.mult).then_inc(ev_d, 1)

            def head_norm(n, x, heads, dh):
                dve.wait_ge(hn_sq, n + 1)
                dve.tensor_reduce(HS[:, n, 0:TOKS * heads], SQ[:, :].rearrange("p (h d) -> p h d", d=dh), AX.X, ALU.add)\
                    .then_inc(hn_sum, 1)
                dve.wait_ge(hn_r, n + 1)
                v = x.rearrange("p t (h d) -> p t h d", d=dh)
                for t in range(TOKS):
                    r = HR[:, n, t * heads:(t + 1) * heads].unsqueeze(2).to_broadcast([P, heads, dh])
                    dve.tensor_tensor(v[:, t], v[:, t], r, ALU.mult).then_inc(hn_x, 1)

            def heads_out(n, dst, gain_col=None, scale=1.0):
                dve.wait_ge(ht, 2 * n + 2)
                g = scale if gain_col is None else gains[:, gain_col:gain_col + 1]
                dve.tensor_scalar(dst, T[1][:, :].rearrange("p (c t) -> p c t", c=2), g, None, ALU.mult)\
                    .then_inc(ht_d, 1)

            def h_update(waits):
                for half in range(2):
                    dve.wait_ge(*waits[half])
                    for t in range(TOKS):
                        part = h[:, t, half * HALF:half * HALF + HALF]
                        ins = dve.tensor_tensor(part, part, PAIR[half][t][:, :], ALU.add)
                    ins.then_inc(half_up, 1)

            def post_update(b, stat):
                dve.wait_ge(rstd, ST[stat] + 1)
                dve.wait_ge(post_in[b % 2], 16 * (b // 2 + 1))
                for half in range(2):
                    c = slice(half * HALF, half * HALF + HALF)
                    for t in range(TOKS):
                        ins = dve.scalar_tensor_tensor(out=tmp[:, t, :], in0=PAIR[half][t][:, :],
                                                       scalar=RS[:, ST[stat], t:t + 1], in1=gpost[:, b % 2, c],
                                                       op0=ALU.mult, op1=ALU.mult)
                    link(ins)
                    for t in range(TOKS):
                        ins = dve.tensor_tensor(h[:, t, c], h[:, t, c], tmp[:, t, :], ALU.add)
                    ins.then_inc(half_up, 1)
                    dve.wait_ge(half_up, 2 * (b + 3) + half + 1)

            dve.memset(VD[:, :, :], 0.0).then_inc(pads_ok, 1)
            dve.memset(win[0], 0.0).then_inc(pads_ok, 1)
            dve.memset(win[1], 0.0).then_inc(pads_ok, 1)
            dve.memset(gains[:, G_ONE:G_ONE + 1], 1.0).then_inc(gain_ok, 1)
            dve.wait_ge(gain_T, 1)
            dve.tensor_copy(gains[:, 0:G_ROWS1], T[0][:, 0:G_ROWS1]).then_inc(gain_ok, 1)
            dve.tensor_copy(gains[:, G_ROWS1:G_ROWS1 + G_ROWS2], T[0][:, 128:128 + G_ROWS2]).then_inc(gain_ok, 1)
            dve.wait_ge(gain_ok, 3)
            for g, dh in ((G_QF, FOX_DH), (G_QM, MEM_DH)):
                dve.tensor_scalar(gains[:, g:g + 1], gains[:, g:g + 1], dh ** -0.5, None, ALU.mult).then_inc(gain_ok, 1)
            split_at(0, 1)
            turn_out("mem", lambda k: G_MEMKV + k)
            split_at(2, 3)
            evac(EV_MEMKV, 1, nat[:, 1, 0:HALF], PAIR[0], "mem")
            head_norm(0, nat[:, :, 0:HALF], MEM_H, MEM_DH)
            split_at(4, 5)
            evac(EV_MEMKV + 1, 3, memV[:, 1, :], PAIR[1], "mem")
            turn_out("x", lambda k: G_MIX + k)
            dve.wait_ge(wf_hi_s, 1)
            dve.tensor_tensor(wflo[:, :, :], wf[:, :, :], wfhi[:, :, :].bitcast(F32), ALU.subtract).then_inc(wf_lo_s, 1)
            for i in range(2):
                link(dve.tensor_tensor(work[:, 64 * i:64 * i + DIFF_DH], lamp[:, 2 * i, :], lamp[:, 2 * i + 1, :], ALU.mult))
                dve.reduce_sum(lam4[:, i:i + 1], work[:, 64 * i:64 * i + DIFF_DH], AX.X).then_inc(lam_ok, 1)
            split_at(6, 7)
            evac(EV_IN, 5, Z[:, 1, 0:512], PAIR[2], "h0")
            head_norm(1, Z[:, :, 0:512], FOX_H, FOX_DH)
            split_at(8, 9)
            evac(EV_IN + 1, 7, Z[:, 1, 512:1024], PAIR[0], "h0")
            head_norm(2, Z[:, :, 512:1024], FOX_H, FOX_DH)
            dve.wait_ge(f_done, 1)
            f2 = fl[:, 0, :].rearrange("p (t c) -> p t c", t=2)
            for t in range(TOKS):
                dve.scalar_tensor_tensor(out=f2[:, t, :], in0=T[0][:, 8 * t:8 * t + 8], scalar=RS[:, ST["h0"], t:t + 1],
                                         in1=bf[:, :], op0=ALU.mult, op1=ALU.add).then_inc(f_out, 1)
            dve.wait_ge(f_out, 2)
            dve.scalar_tensor_tensor(out=fl[:, 1, :], in0=fl[:, 0, :], scalar=-1.0, in1=fl[:, 0, :], op0=ALU.mult,
                                     op1=ALU.max).then_inc(f_out, 1)
            dve.wait_ge(f_act, 2)
            dve.scalar_tensor_tensor(out=fl[:, 0, :], in0=fl[:, 0, :], scalar=0.0, in1=fl[:, 3, :], op0=ALU.min,
                                     op1=ALU.subtract).then_inc(f_log, 1)
            dve.wait_ge(lam_ok, 3)
            dve.scalar_tensor_tensor(out=lam4[:, 0:1], in0=lam4[:, 2:3], scalar=lambda_init, in1=lam4[:, 3:4],
                                     op0=ALU.add, op1=ALU.subtract).then_inc(lam_ok, 1)
            split_at(10)
            heads_out(HT_KM, memKT[:, 2:4, :], G_KM)
            split_at(11)
            evac(EV_IN + 2, 9, Z[:, 1, 1024:1536], PAIR[1], "h0")
            heads_out(HT_QF, QT[:, 2:4, :], G_QF)
            split_at(12)
            heads_out(HT_KF, KT[:, 2:4, :], G_KF)
            dve.wait_ge(c_done, 1)
            dve.tensor_copy(cn[:, :, :], B[0][:, 0:16].rearrange("p (t c) -> p t c", t=2)).then_inc(c_out, 1)
            dve.tensor_copy(cT[:, :], B[1][0:FOX_H, 0:S]).then_inc(c_out, 1)
            split_at(13)
            evac(EV_IN + 3, 11, Z[:, 1, 1536:2048], PAIR[2], "h0")
            dve.wait_ge(pt_done, 2)
            dve.tensor_copy(poolT[:, 2:4, PAD:PAD + S], T[1][:, :].rearrange("p (c t) -> p c t", c=2)).then_inc(pt_out, 1)

            def row_max(i, col0):
                for t, c0, c1 in ((0, 0, 128), (1, 128, 384)):
                    col = col0 + 2 * i + t
                    dve.tensor_reduce(nmax[:, col:col + 1], scores[i % 4][:, c0:c1], AX.X, ALU.max, negate=True)\
                        .then_inc(at_x, 1)

            dve.wait_ge(in_const, 80)
            dve.wait_ge(c_out, 2)
            for i in range(FOX_H):
                dve.wait_ge(at_s, i + 1)
                if i >= 4:
                    dve.wait_ge(at_e, 2 * (i - 3))
                for t, c0, c1 in ((0, 0, 128), (1, 128, 384)):
                    dve.scalar_tensor_tensor(out=scores[i % 4][:, c0:c1], in0=B[i % 4][:, c0:c1],
                                             scalar=cn[:, t, i:i + 1], in1=foxmask[:, c0:c1], op0=ALU.add,
                                             op1=ALU.add).then_inc(at_m, 1)
                dve.wait_ge(at_m, 2 * i + 2)
                row_max(i, 0)

            def values_out(e0, count, v0, heads, dh):
                dve.wait_ge(at_e, e0 + count)
                link(dve.reciprocal(linv[:, 0:count], lsum[:, 0:count]))
                dve.wait_ge(at_v, v0 + heads)
                r = linv[:, 0:count].rearrange("p (h t) -> p t h", t=2)
                for t in range(TOKS):
                    dve.tensor_tensor(nat[:, t, 0:HALF].rearrange("p (h d) -> p h d", d=dh),
                                      B[4 + t][:, :].rearrange("p (h d) -> p h d", d=dh),
                                      r[:, t].unsqueeze(2).to_broadcast([P, heads, dh]), ALU.mult).then_inc(at_o, 1)

            values_out(0, 16, 0, FOX_H, FOX_DH)
            turn_out("mix", lambda k: G_ONE if k < 4 else G_POOL + k - 4)
            split_at(14, 15, 16, 17)
            h_update([(w_used, U_OUT + 2), (w_used, U_OUT + 4)])
            turn_out("mq", lambda k: G_MEMQ + k)
            split_at(18, 19)
            evac(EV_MQ, 17, Z[:, 1, 0:512], PAIR[2], "h1")
            head_norm(3, Z[:, :, 0:512], MEM_H, MEM_DH)
            heads_out(HT_QM, QT[:, 2:4, :], G_QM)
            for i in range(MEM_H):
                dve.wait_ge(at_s, M_S + i + 1)
                dve.tensor_reduce(nmax[:, 2 * i:2 * i + 2], B[i][:, :].rearrange("p (t c) -> p t c", t=2), AX.X,
                                  ALU.max, negate=True).then_inc(at_x, 1)
            values_out(M_E, 8, M_R, MEM_H, MEM_DH)
            turn_out("mo", lambda k: G_ONE, chunks=4)
            split_at(20, 21)
            h_update([(w_used, U_MO + 1), (w_used, U_MO + 2)])

            def ffn(f, stat, reader, gain):
                u0 = U_FFN[f]
                v = u0 + 2
                turn_out(reader, lambda k: gain + k)

                def act_of(j):
                    for t in range(TOKS):
                        dve.wait_ge(gate_ok, 2 * (FJ * f + j) + t + 1)
                        dve.scalar_tensor_tensor(out=actn[:, t, :], in0=GU[t][:, 256:512],
                                                 scalar=RS[:, ST[stat], t:t + 1], in1=gate[:, t, :],
                                                 op0=ALU.mult, op1=ALU.mult).then_inc(act_ok, 1)

                def act_out(j):
                    dve.wait_ge(act_hi, FJ * f + j + 1)
                    dve.tensor_tensor(alo[:, :], T[0][:, :], ahi[:, :].bitcast(F32), ALU.subtract).then_inc(act_lo, 1)

                split_at(u0 + 2, u0 + 3)
                dve.wait_ge(rstd, ST[stat] + 1)
                act_of(0)

                def step(i, last):
                    split(v + 3 * i + 2, (v + 2) % RING)
                    act_out(i)
                    split(v + 3 * i + 3, (v + 3) % RING)
                    act_of(i + 1)
                    if not (last and v + 3 * i + 4 >= UNITS):
                        split(v + 3 * i + 4, (v + 4) % RING)

                with dve.Fori(0, FJ - 2) as i:
                    step(i, False)
                step(FJ - 2, True)
                act_out(FJ - 1)
                split_at(u0 + 34)

            ffn(0, "h2", "ffn0", G_FFN)
            h_update([(half0, 1), (w_used, U_FFN[0] + 33)])
            ffn(1, "h3", "ffn1", n2(0, 0))
            post_update(0, "y0")
            turn_out("cin", lambda k: n2(0, 2) + k)
            for i in range(2):
                dve.memset(uT[i][:, 0:2], 0.0).then_inc(pads_ok, 1)
            for g in range(6):
                split_at(U_CIN + 2 * g + 2, U_CIN + 2 * g + 3)
                evac(EV_CIN + g, U_CIN + 2 * g + 1, conv_places[g][:, 1, :], PAIR[g % 3], "h4")
                if g % 3 == 2:
                    dve.wait_ge(ev_a, EV_CIN + g + 1)
                    dve.wait_ge(ev_d, EV_CIN + g + 1)
                    dve.tensor_tensor(conv_places[g - 1], conv_places[g - 1], conv_places[g], ALU.mult)\
                        .then_inc(conv_p, 1)

            def conv_lo(k):
                dve.wait_ge(xt_hi, XT["cout"] + k + 1)
                dve.tensor_tensor(xlo[:, k, :], convx[k % 2], xhi[:, k, :].bitcast(F32), ALU.subtract)\
                    .then_inc(xt_lo, 1)

            dve.wait_ge(pads_ok, 5)
            for k in range(KD):
                dve.wait_ge(conv_u, k + 1)
                g = [gains[:, G_CONV + 8 * w + k:G_CONV + 8 * w + k + 1] for w in range(3)]
                u = uT[k % 2]
                if k:
                    dve.wait_ge(conv_x, k)
                link(dve.tensor_scalar(taps[0], u[:, 2:2 + S], g[2], None, ALU.mult))
                link(dve.scalar_tensor_tensor(out=taps[1], in0=u[:, 1:1 + S], scalar=g[1], in1=taps[0], op0=ALU.mult,
                                              op1=ALU.add))
                link(dve.scalar_tensor_tensor(out=taps[0], in0=u[:, 0:S], scalar=g[0], in1=taps[1], op0=ALU.mult,
                                              op1=ALU.add))
                dve.tensor_tensor(convx[k % 2], T[k % 2][:, S:2 * S], taps[0], ALU.mult).then_inc(conv_x, 1)
                if k:
                    conv_lo(k - 1)
            conv_lo(KD - 1)
            split_at(*range(U_COUT + 2, U_COUT + 6))
            post_update(1, "y1")
            ffn(2, "h5", "ffn2", n2(0, 4))
            post_update(2, "y2")
            turn_out("kv", lambda k: G_KV + k)
            for g in range(4):
                split_at(U_KV + 2 * g + 2, U_KV + 2 * g + 3)
                evac(EV_KV + g, U_KV + 2 * g + 1, kv_places[g][:, 1, :], PAIR[(g + 2) % 3], "h6")
            heads_out(HT_KD, KT[:, 2:4, :])
            heads_out(HT_KD + 1, KT[:, 6:8, :])
            ffn(3, "h6", "ffn3", n2(1, 0))
            post_update(3, "y3")
            turn_out("q", lambda k: n2(1, 2) + k)
            for g in range(2):
                split_at(U_Q + 2 * g + 2, U_Q + 2 * g + 3)
                evac(EV_Q + g, U_Q + 2 * g + 1, Z[:, 1, 512 * g:512 * g + 512], PAIR[(g + 2) % 3], "h7")
            heads_out(HT_QD, QT[:, 2:4, :], scale=DIFF_DH ** -0.5)
            heads_out(HT_QD + 1, QT[:, 6:8, :], scale=DIFF_DH ** -0.5)

            def combine(i):
                p0, p1 = probs[2 * i % 4], probs[(2 * i + 1) % 4]
                dve.wait_ge(at_e, D_E + 4 * i + 4)
                link(dve.reciprocal(linv[:, 4 * i:4 * i + 4], lsum[:, 4 * i:4 * i + 4]))
                link(dve.tensor_scalar(linv[:, 4 * i + 2:4 * i + 4], linv[:, 4 * i + 2:4 * i + 4], lam4[:, 0:1], None,
                                       ALU.mult))
                for t, c0, c1 in ((0, 0, 128), (1, 128, 384)):
                    ins = dve.tensor_scalar(p1[:, c0:c1], p1[:, c0:c1], linv[:, 4 * i + 2 + t:4 * i + 3 + t], None,
                                            ALU.mult)
                link(ins)
                for t, c0, c1 in ((0, 0, 128), (1, 128, 384)):
                    dve.scalar_tensor_tensor(out=p0[:, c0:c1], in0=p0[:, c0:c1],
                                             scalar=linv[:, 4 * i + t:4 * i + t + 1], in1=p1[:, c0:c1],
                                             op0=ALU.mult, op1=ALU.subtract).then_inc(at_a, 1)

            for i in range(DIFF_H + 1):
                if i < DIFF_H:
                    for m in (2 * i, 2 * i + 1):
                        dve.wait_ge(at_s, D_S + m + 1)
                        if m >= 4:
                            dve.wait_ge(at_e, D_E + 2 * (m - 3))
                        dve.scalar_tensor_tensor(out=scores[m % 4], in0=dist[:, :], scalar=slopes[i],
                                                 in1=B[4 + m % 2][:, 0:384], op0=ALU.mult, op1=ALU.add)\
                            .then_inc(at_m, 1)
                        dve.wait_ge(at_m, D_M + m + 1)
                        row_max(m, 0)
                if i:
                    combine(i - 1)
            dve.wait_ge(hn_sq, 8)
            dve.tensor_reduce(HS[:, 4, :], osq[:, :, :].rearrange("p t (h d) -> p (t h) d", d=2 * DIFF_DH), AX.X, ALU.add)\
                .then_inc(hn_sum, 1)
            dve.wait_ge(hn_r, 5)
            for g in range(2):
                for t in range(TOKS):
                    r = HR[:, 4, 8 * t + 4 * g:8 * t + 4 * g + 4].unsqueeze(2).to_broadcast([P, 4, 128])
                    dve.tensor_tensor(nat[:, t, g * HALF:g * HALF + HALF].rearrange("p (h d) -> p h d", d=128),
                                      PAIR[g][t][:, :].rearrange("p (h d) -> p h d", d=128), r, ALU.mult)\
                        .then_inc(at_o, 1)
            turn_out("ao", lambda k: G_SUB)
            split_at(*range(U_O + 2, U_O + 6))
            post_update(4, "y4")
            ffn(4, "h8", "ffn4", n2(1, 4))
            post_update(5, "y5")

        @block.tensor
        def _(pe):
            def turn(name, k, src, waits):
                if waits:
                    for w in waits[k // 4]:
                        pe.wait_ge(*w)
                if k >= 2:
                    pe.wait_ge(xt_lo, XT[name] + k - 1)
                for t in range(TOKS):
                    ins = pe.transpose(T[k % 2][:, t * P:t * P + P], src[:, t, k * P:k * P + P], ident[:, :])
                ins.then_inc(t_done, 1)

            def k_unit(u, name, k0, banks, first, last, feed=None):
                pe.wait_ge(w_lo, u + 1)
                s = u % RING
                for kk in range(4):
                    k = k0 + kk
                    pe.wait_ge(xt_lo, XT[name] + k + 1)
                    c = slice(kk * HALF, kk * HALF + HALF)
                    for t in range(TOKS):
                        x = slice(t * P, t * P + P)
                        pe.matmul(banks[t][:, :], xlo[:, k, x], whi[s][:, c], start=first and kk == 0, stop=False)
                        pe.matmul(banks[t][:, :], xhi[:, k, x], wlo[s][:, c], start=False, stop=False)
                        ins = pe.matmul(banks[t][:, :], xhi[:, k, x], whi[s][:, c], start=False,
                                        stop=last and kk == 3)
                    if kk == 3:
                        ins.then_inc(w_used, 1)
                    if feed:
                        feed(k + 2)

            def group(u, name, banks, feed=None):
                k_unit(u, name, 0, banks, True, False, feed)
                k_unit(u + 1, name, 4, banks, False, True, feed)

            def feeder(name, src, waits, chunks=KD):
                def feed(k):
                    if k < chunks:
                        turn(name, k, src, waits)
                feed(0)
                feed(1)
                return feed

            def evacuated(e):
                pe.wait_ge(ev_a, e + 1)
                pe.wait_ge(ev_d, e + 1)

            def heads_turn(n, src):
                for b in range(2):
                    for c in range(2):
                        for t in range(TOKS):
                            col = (2 * b + c) * P
                            ins = pe.transpose(T[b][:, (2 * c + t) * P:(2 * c + t) * P + P], src[:, t, col:col + P],
                                               ident[:, :])
                    ins.then_inc(ht, 1)

            def t_free_heads(n):
                pe.wait_ge(ht_a, n + 1)
                pe.wait_ge(ht_d, n + 1)

            pe.wait_ge(in_id, 16)
            pe.wait_ge(in_gain, 15 * 16)
            pe.transpose(T[0][:, 0:G_ROWS1], grow1[0:G_ROWS1, :], ident[0:G_ROWS1, 0:G_ROWS1])
            pe.transpose(T[0][:, 128:128 + G_ROWS2], grow2[0:G_ROWS2, :], ident[0:G_ROWS2, 0:G_ROWS2])\
                .then_inc(gain_T, 1)
            pe.wait_ge(gain_ok, 3)
            feed = feeder("mem", nat, [[(in_mem, 16)]] * 2)
            group(U_MEMKV, "mem", PAIR[0], feed)
            group(U_MEMKV + 2, "mem", PAIR[1])
            feed = feeder("x", h, [[(in_x, 16)]] * 2)
            group(U_IN, "x", PAIR[2], feed)
            evacuated(EV_MEMKV)
            group(U_IN + 2, "x", PAIR[0])
            pe.wait_ge(wf_lo_s, 1)
            for t in range(TOKS):
                x = slice(t * P, t * P + P)
                for k in range(KD):
                    o = T[0][:, 8 * t:8 * t + 8]
                    pe.matmul(o, xlo[:, k, x], wfhi[:, k, :], start=k == 0, stop=False)
                    pe.matmul(o, xhi[:, k, x], wflo[:, k, :], start=False, stop=False)
                    ins = pe.matmul(o, xhi[:, k, x], wfhi[:, k, :], start=False, stop=k == KD - 1)
            ins.then_inc(f_done, 1)
            evacuated(EV_MEMKV + 1)
            k_unit(U_IN + 4, "x", 0, PAIR[1], True, False)
            pe.wait_ge(f_out, 2)
            pe.wait_ge(hn_x, 2)
            heads_turn(HT_KM, nat)
            k_unit(U_IN + 5, "x", 4, PAIR[1], False, True)
            t_free_heads(HT_KM)
            pe.wait_ge(hn_x, 4)
            heads_turn(HT_QF, Z[:, :, 0:512])
            evacuated(EV_IN)
            k_unit(U_IN + 6, "x", 0, PAIR[2], True, False)
            t_free_heads(HT_QF)
            pe.wait_ge(hn_x, 6)
            heads_turn(HT_KF, Z[:, :, 512:1024])
            pe.wait_ge(f_log, 1)
            pe.wait_ge(in_const, 80)
            evacuated(EV_IN + 1)
            for t in range(TOKS):
                for j in range(t + 1):
                    pe.matmul(B[0][:, 8 * t:8 * t + 8], tri[:, j, t * P:t * P + P], fl[:, 0, 8 * j:8 * j + 8],
                              start=j == 0, stop=j == t)
            for j in range(TOKS):
                ins = pe.matmul(B[1][0:FOX_H, 0:S], fl[:, 0, 8 * j:8 * j + 8], tri[:, j, :], start=j == 0, stop=j == 1)
            ins.then_inc(c_done, 1)
            k_unit(U_IN + 7, "x", 4, PAIR[2], False, True)
            t_free_heads(HT_KF)
            evacuated(EV_IN + 2)
            for b in range(2):
                for c in range(2):
                    for t in range(TOKS):
                        col = 1024 + (2 * b + c) * P
                        ins = pe.transpose(T[b][:, (2 * c + t) * P:(2 * c + t) * P + P], Z[:, t, col:col + P],
                                           ident[:, :])
                ins.then_inc(pt_done, 1)

            def causal_turn(i, src, done):
                for b in range(3):
                    ins = pe.transpose(T[i % 2][:, b * P:b * P + P], src[:, b * P:b * P + P], ident[:, :])
                ins.then_inc(done, 1)

            def causal_values(i, out0, out1, v):
                pe.matmul(out0, pT[i % 2][:, 0:P], v[:, 0, :], start=True, stop=True)
                pe.matmul(out1, pT[i % 2][:, P:2 * P], v[:, 0, :], start=True, stop=False)
                pe.matmul(out1, pT[i % 2][:, 2 * P:3 * P], v[:, 1, :], start=False, stop=True).then_inc(at_v, 1)

            def fox_scores(i):
                c, r = i // 2, slice(64 * (i % 2), 64 * (i % 2) + 64)
                if i >= 4:
                    pe.wait_ge(at_m, 2 * (i - 3))
                b = B[i % 4]
                for q, lo, width in ((0, 0, P), (1, P, S)):
                    pe.matmul(b[:, lo:lo + width], QT[r, c, q * P:q * P + P], KT[r, c, 0:width], start=True, stop=False)
                    ins = pe.matmul(b[:, lo:lo + width], sel[:, i, :], cT[:, 0:width], start=False, stop=True)
                ins.then_inc(at_s, 1)

            pe.wait_ge(c_out, 2)
            evacuated(EV_IN + 3)
            fox_scores(0)
            fox_scores(1)
            fox_scores(2)
            for i in range(FOX_H):
                pe.wait_ge(at_e, 2 * i + 2)
                if i < 2:
                    pe.wait_ge(pt_out, 2)
                else:
                    pe.wait_ge(at_c, i - 1)
                causal_turn(i, probs[i % 4], at_r)
                if i + 3 < FOX_H:
                    fox_scores(i + 3)
                pe.wait_ge(at_c, i + 1)
                d = slice(64 * i, 64 * i + 64)
                causal_values(i, B[4][:, d], B[5][:, d], Z[:, :, 1536 + 64 * i:1600 + 64 * i])
            pe.wait_ge(mixed_ok, 4)
            pe.wait_ge(in_small, 64)
            pe.wait_ge(at_m, 16)
            for g in range(4):
                for t in range(TOKS):
                    ins = pe.matmul(B[t][:, g * P:g * P + P], mixT[:, g, t * P:t * P + P], wpool[:, g, :],
                                    start=True, stop=True)
            ins.then_inc(py_done, 1)
            feed = feeder("mix", nat, [[(at_o, 2)], [(py_out, 2)]])
            pe.wait_ge(py_out, 2)
            group(U_OUT, "mix", PAIR[0], feed)
            group(U_OUT + 2, "mix", PAIR[1])

            def h_waits(reader):
                m = H_UP[reader]
                return [[(half_up, 2 * m + 1)], [(half_up, 2 * m + 2)]]

            feed = feeder("mq", h, h_waits("mq"))
            group(U_MQ, "mq", PAIR[2], feed)
            pe.wait_ge(hn_x, 8)
            pe.wait_ge(xt_lo, XT["mq"] + KD)
            heads_turn(HT_QM, Z[:, :, 0:512])
            t_free_heads(HT_QM)
            pe.wait_ge(half_up, 2)

            def mem_scores(i):
                for t in range(TOKS):
                    ins = pe.matmul(B[i][:, t * S:t * S + S], QT[:, i, t * P:t * P + P], memKT[:, i, :],
                                    start=True, stop=True)
                ins.then_inc(at_s, 1)

            for i in range(3):
                mem_scores(i)
            for i in range(MEM_H):
                pe.wait_ge(at_e, M_E + 2 * i + 2)
                if i >= 2:
                    pe.wait_ge(at_c, M_R + i - 1)
                for t in range(TOKS):
                    for b in range(2):
                        c = (2 * t + b) * P
                        ins = pe.transpose(T[i % 2][:, c:c + P], mprobs[i][:, c:c + P], ident[:, :])
                ins.then_inc(at_r, 1)
                if i + 3 < MEM_H:
                    mem_scores(i + 3)
                pe.wait_ge(at_c, M_R + i + 1)
                for t in range(TOKS):
                    for b in range(2):
                        c = (2 * t + b) * P
                        ins = pe.matmul(B[4 + t][:, i * P:i * P + P], pT[i % 2][:, c:c + P],
                                        memV[:, b, i * P:i * P + P], start=b == 0, stop=b == 1)
                ins.then_inc(at_v, 1)
            feed = feeder("mo", nat, [[(at_o, 4)]], chunks=4)
            k_unit(U_MO, "mo", 0, PAIR[0], True, True, feed)
            k_unit(U_MO + 1, "mo", 0, PAIR[1], True, True)

            def ffn(f, reader, waits, before=None):
                u0 = U_FFN[f]
                feed = feeder(reader, h, waits)
                if before:
                    before()
                group(u0, reader, GU, feed)

                def up_unit(u, slot, k0):
                    pe.wait_ge(w_lo, u + 1)
                    for kk in range(4):
                        c = slice(kk * HALF, kk * HALF + HALF)
                        for t in range(TOKS):
                            x, k = slice(t * P, t * P + P), k0 + kk
                            pe.matmul(GU[t][:, :], xlo[:, k, x], whi[slot][:, c], start=k == 0, stop=False)
                            pe.matmul(GU[t][:, :], xhi[:, k, x], wlo[slot][:, c], start=False, stop=False)
                            ins = pe.matmul(GU[t][:, :], xhi[:, k, x], whi[slot][:, c], start=False, stop=k == KD - 1)
                    ins.then_inc(w_used, 1)

                def down_unit(u, slot, j, first, last):
                    pe.wait_ge(w_lo, u + 1)
                    pe.wait_ge(act_lo, FJ * f + j + 1)
                    for half in range(2):
                        for k in range(2):
                            c = slice(k * D + half * HALF, k * D + half * HALF + HALF)
                            for t in range(TOKS):
                                x = slice((2 * k + t) * P, (2 * k + t) * P + P)
                                o = PAIR[half][t][:, :]
                                pe.matmul(o, alo[:, x], whi[slot][:, c], start=first and k == 0, stop=False)
                                pe.matmul(o, ahi[:, x], wlo[slot][:, c], start=False, stop=False)
                                ins = pe.matmul(o, ahi[:, x], whi[slot][:, c], start=False, stop=last and k == 1)
                        if last and half == 0:
                            ins.then_inc(half0, 1)
                    ins.then_inc(w_used, 1)

                def turn_act(j):
                    pe.wait_ge(act_ok, 2 * (FJ * f + j) + 2)
                    for k in range(2):
                        for t in range(TOKS):
                            ins = pe.transpose(T[0][:, (2 * k + t) * P:(2 * k + t) * P + P],
                                               actn[:, t, k * P:k * P + P], ident[:, :])
                    ins.then_inc(act_t, 1)

                def step(i, first):
                    v = u0 + 2
                    pe.wait_ge(act_ok, 2 * (FJ * f + i) + 2)
                    up_unit(v + 3 * i, v % RING, 0)
                    turn_act(i)
                    up_unit(v + 3 * i + 1, (v + 1) % RING, 4)
                    down_unit(v + 3 * i + 2, (v + 2) % RING, i, first, False)

                step(0, True)
                with pe.Fori(1, FJ - 1) as i:
                    step(i, False)
                turn_act(FJ - 1)
                down_unit(u0 + 32, (u0 + 32) % RING, FJ - 1, False, True)

            ffn(0, "ffn0", h_waits("ffn0"))
            ffn(1, "ffn1", h_waits("ffn1"))
            feed = feeder("cin", h, h_waits("cin"))
            for g in range(6):
                if g == 1:
                    pe.wait_ge(half_up, 2 * H_UP["cin"] + 2)
                if g >= 3:
                    evacuated(EV_CIN + g - 3)
                group(U_CIN + 2 * g, "cin", PAIR[g % 3], feed if g == 0 else None)
            evacuated(EV_CIN + 5)

            def conv_feed(k):
                if k >= KD:
                    return
                pe.wait_ge(conv_p, k // 4 + 1)
                if k >= 2:
                    pe.wait_ge(conv_x, k - 1)
                b = Z[:, :, 0:512] if k < 4 else Z[:, :, 1536:2048]
                u = Z[:, :, 512:1024] if k < 4 else nat[:, :, 0:512]
                c = slice((k % 4) * P, (k % 4) * P + P)
                for src, lo in ((u, 0), (b, S)):
                    for t in range(TOKS):
                        ins = pe.transpose(T[k % 2][:, lo + t * P:lo + t * P + P], src[:, t, c], ident[:, :])
                ins.then_inc(conv_t, 1)

            conv_feed(0)
            conv_feed(1)
            group(U_COUT, "cout", PAIR[0], conv_feed)
            group(U_COUT + 2, "cout", PAIR[1])
            ffn(2, "ffn2", h_waits("ffn2"))
            feed = feeder("kv", h, h_waits("kv"))
            for g in range(4):
                if g == 1:
                    pe.wait_ge(half_up, 2 * H_UP["kv"] + 2)
                if g == 3:
                    evacuated(EV_KV)
                group(U_KV + 2 * g, "kv", PAIR[(g + 2) % 3], feed if g == 0 else None)
            evacuated(EV_KV + 1)
            heads_turn(HT_KD, Z[:, :, 0:512])
            t_free_heads(HT_KD)
            heads_turn(HT_KD + 1, Z[:, :, 512:1024])
            t_free_heads(HT_KD + 1)
            evacuated(EV_KV + 3)
            ffn(3, "ffn3", None)
            feed = feeder("q", h, h_waits("q"))
            group(U_Q, "q", PAIR[2], feed)
            pe.wait_ge(half_up, 2 * H_UP["q"] + 2)
            group(U_Q + 2, "q", PAIR[0])
            evacuated(EV_Q)
            heads_turn(HT_QD, Z[:, :, 0:512])
            t_free_heads(HT_QD)
            evacuated(EV_Q + 1)
            heads_turn(HT_QD + 1, Z[:, :, 512:1024])
            t_free_heads(HT_QD + 1)

            def diff_scores(m):
                c, r = m // 2, slice(64 * (m % 2), 64 * (m % 2) + 64)
                if m >= 2:
                    pe.wait_ge(at_m, D_M + m - 1)
                b = B[4 + m % 2]
                pe.matmul(b[:, 0:P], QT[r, c, 0:P], KT[r, c, 0:P], start=True, stop=True)
                pe.matmul(b[:, P:3 * P], QT[r, c, P:2 * P], KT[r, c, 0:S], start=True, stop=True).then_inc(at_s, 1)

            diff_scores(0)
            diff_scores(1)
            for i in range(DIFF_H + 1):
                if i + 1 < DIFF_H:
                    diff_scores(2 * i + 2)
                    diff_scores(2 * i + 3)
                if i < DIFF_H:
                    pe.wait_ge(at_a, 2 * i + 2)
                    if i >= 2:
                        pe.wait_ge(at_c, D_R + i - 1)
                    causal_turn(i, probs[2 * i % 4], at_r)
                    pe.wait_ge(at_c, D_R + i + 1)
                    d = slice((i % 4) * P, (i % 4) * P + P)
                    causal_values(i, PAIR[i // 4][0][:, d], PAIR[i // 4][1][:, d], VD[:, :, i * P:i * P + P])
            feed = feeder("ao", nat, [[(at_o, 6)], [(at_o, 8)]])
            pe.wait_ge(at_o, 8)
            group(U_O, "ao", PAIR[0], feed)
            group(U_O + 2, "ao", PAIR[1])
            ffn(4, "ffn4", h_waits("ffn4"))


_INS = ["x", "mem", "g_mix", "w_in", "b_forget", "g_q_fox", "g_k_fox", "w_pool", "pool_scale", "w_out", "g_mem_q",
        "g_mem_kv", "w_mem_q", "w_mem_kv", "g_q_mem", "g_k_mem", "w_mem_out", "g_ffn", "w_gate_up", "w_down",
        "ffn_w_gu_2", "ffn_w_down_2", "norm_g_2", "conv_w_in_2", "conv_k_2", "conv_w_out_2", "kv_norm_g_2",
        "w_kv_2", "attn_w_q_2", "attn_lambda_2", "attn_subln_g_2", "attn_w_o_2"]


def constants():
    p, t = np.arange(P), np.arange(S)
    ones = np.float32(1.0)
    tri = np.stack([(j * P + p[:, None] <= t[None, :]) for j in range(TOKS)], axis=1).astype(np.float32)
    q = np.concatenate([np.zeros(P), np.full(S, P)])
    k = np.concatenate([np.arange(P), np.arange(S)])
    gap = (q[None, :] + p[:, None] - k[None, :]).astype(np.float32)
    sel = np.zeros((FOX_H, FOX_H, P), np.float32)
    for i in range(FOX_H):
        sel[i, i, :] = -ones
    cnt = np.stack([1.0 / np.minimum(np.arange(16) + 1, w) for w in WINDOWS]).astype(np.float32)
    return {
        "c_ident": np.eye(P, dtype=np.float32),
        "c_tri": tri,
        "c_mask": np.where(gap >= 0, 0.0, NEG).astype(np.float32),
        "c_dist": np.where(gap >= 0, -gap, NEG).astype(np.float32),
        "c_sel": sel,
        "c_cnt": np.ascontiguousarray(np.broadcast_to(cnt, (P, 4, 16))),
    }


def kernel(**inputs):
    import concourse.bacc as bacc
    from concourse.bass_utils import run_bass_kernel_spmd

    nc = bacc.Bacc("TRN2", target_bir_lowering=False, num_devices=1)
    arrays, args = {}, {}
    for name, value in [(n, inputs[n]) for n in _INS] + list(constants().items()):
        v = np.ascontiguousarray(value)
        arrays[f"in_{name}"] = v
        args[name] = nc.dram_tensor(f"in_{name}", v.shape, mybir.dt.from_np(v.dtype), kind="ExternalInput").ap()
    out = nc.dram_tensor("out_0", (1, S, D), F32, kind="ExternalOutput").ap()
    build(nc, args, out)
    r = run_bass_kernel_spmd(nc, [arrays], core_ids=[0])
    return r.results[0]["out_0"]
```

```python
import math
from contextlib import ExitStack

import numpy as np
import concourse.bass as bass
from concourse import mybir

F32 = mybir.dt.float32
F32R = mybir.dt.float32r
ALU = mybir.AluOpType
ACT = mybir.ActivationFunctionType
AX = mybir.AxisListType

P = 128
S = 256
TOKS = S // P
D = 1024
KD = D // P
HALF = 512
FOX_H, FOX_DH = 8, 64
MEM_H, MEM_DH = 4, 128
DIFF_H, DIFF_DH = 8, 64
FF = 2816
FJ = FF // 256
WINDOWS = (2, 4, 8, 16)
EPS = 1e-6
NEG = -1.0e37
RING = 3
UNIT = 2048

U_MEMKV, U_IN, U_OUT, U_MQ, U_MO = 0, 4, 12, 16, 18
U_FFN = (20, 53, 102, 143, 184)
U_CIN, U_COUT, U_KV, U_Q, U_O = 86, 98, 135, 176, 180
UNITS = 217

XT_ORDER = [("mem", 8), ("x", 8), ("mix", 8), ("mq", 8), ("mo", 4), ("ffn0", 8), ("ffn1", 8), ("cin", 8),
            ("cout", 8), ("ffn2", 8), ("kv", 8), ("ffn3", 8), ("q", 8), ("ao", 8), ("ffn4", 8)]
XT = {}
TD = {}
_x = _t = 0
for _n, _c in XT_ORDER:
    XT[_n], TD[_n] = _x, _t
    if _n == "cout":
        _x += _c
    else:
        _x += TOKS * _c
        _t += TOKS * _c // 2
CHUNKS = dict(XT_ORDER)

ST = {n: i for i, n in enumerate(["mem", "h0", "h1", "h2", "h3", "y0", "h4", "y1", "h5", "y2", "h6", "y3",
                                  "h7", "y4", "h8", "y5"])}
H_UP = {n: i for i, n in enumerate(["mq", "ffn0", "ffn1", "cin", "ffn2", "kv", "q", "ffn4", "out"])}
H_UP["ffn3"] = H_UP["kv"]


def h_ready(reader, t, half):
    return 4 * H_UP[reader] + 2 * t + half + 1


G_N2, G_CONV, G_ROWS1 = 0, 96, 120
G_MEMKV, G_MIX, G_MEMQ, G_FFN, G_KV, G_POOL, G_SUB, G_QF, G_KF, G_QM, G_KM = (
    120, 128, 136, 144, 152, 160, 164, 165, 166, 167, 168)
G_ROWS2 = 49
G_ONE = 169


def n2(layer, i):
    return G_N2 + (layer * 6 + i) * KD


def build(nc, a, out):
    lambda_init = 0.8 - 0.6 * math.exp(-0.3)
    SUB_M = 1.0 / (1.0 - lambda_init) ** 2
    slopes = [2.0 ** (-8.0 * (h + 1) / DIFF_H) for h in range(DIFF_H)]

    ctx = ExitStack()
    with ctx:
        def sb(name, shape, dt=F32):
            return ctx.enter_context(nc.sbuf_tensor(name, shape, dt))

        def sem(name):
            return ctx.enter_context(nc.semaphore(name))

        raw = [sb(f"w_raw{s}", [P, UNIT]) for s in range(RING)]
        whi = [sb(f"w_hi{s}", [P, UNIT], F32R) for s in range(RING)]
        wlo = [sb(f"w_lo{s}", [P, UNIT], F32R) for s in range(RING)]
        xhi = sb("xt_hi", [P, KD, S], F32R)
        xlo = sb("xt_lo", [P, KD, S], F32R)
        h = sb("h", [P, TOKS, D])
        nat = sb("nat", [P, TOKS, D])
        Z = sb("Z", [P, TOKS, 4 * HALF])
        QT = sb("QT", [P, 8, S])
        KT = sb("KT", [P, 8, S])
        VD = sb("VD", [P, TOKS, D])
        memKT = sb("memKT", [P, MEM_H, S])
        memV = sb("memV", [P, TOKS, HALF])
        ahi = sb("act_hi", [P, 2 * S], F32R)
        alo = sb("act_lo", [P, 2 * S], F32R)
        last_hi = xhi[:, KD - 2:KD, :].rearrange("p k t -> p (k t)")
        last_lo = xlo[:, KD - 2:KD, :].rearrange("p k t -> p (k t)")
        work = sb("work", [P, 4096])
        SQ = sb("SQ", [P, 2 * HALF])
        junk = sb("junk", [P, HALF])
        tmp = sb("tmp", [P, TOKS, HALF])
        gpost = sb("gpost", [P, 2, D])
        gains = sb("gains", [P, 176])
        grow1 = sb("grow1", [P, P])
        grow2 = sb("grow2", [P, P])
        ident = sb("ident", [P, P])
        tri = sb("tri", [P, TOKS, S])
        foxmask = sb("foxmask", [P, 384])
        dist = sb("dist", [P, 384])
        sel = tmp[0:FOX_H, :, :].rearrange("p t (h c) -> p (t h) c", c=P)
        cnt16 = sb("cnt16", [P, 4, 16])
        wpool = sb("wpool", [P, 4, P])
        wf = sb("wf", [P, KD, FOX_H])
        wfhi = sb("wf_hi", [P, KD, FOX_H], F32R)
        wflo = sb("wf_lo", [P, KD, FOX_H], F32R)
        bf = sb("b_forget", [P, FOX_H])
        lamp = sb("lamp", [P, 4, DIFF_DH])
        lam4 = sb("lam4", [P, 4])
        SS = sb("row_squares", [P, len(ST), TOKS, 2])
        SV = sb("row_var", [P, len(ST), TOKS])
        RS = sb("row_rstd", [P, len(ST), TOKS])
        HS = sb("head_squares", [P, 5, 16])
        HV = sb("head_var", [P, 5, 16])
        HR = sb("head_rstd", [P, 5, 16])
        mhalf = sb("minus_half", [P, 16])
        fl = sb("forget", [P, 4, 16])
        cn = sb("cum_nat", [P, TOKS, FOX_H])
        cT = sb("cum_T", [FOX_H, S])
        nmax = sb("neg_max", [P, 32])
        lsum = sb("exp_sum", [P, 32])
        epsl = sb("eps_sum2", [P, 16])
        linv = sb("exp_inv", [P, 32])

        scores = [work[:, 384 * i:384 * i + 384] for i in range(4)]
        probs = [work[:, 1536 + 384 * i:1920 + 384 * i] for i in range(4)]
        pT = [work[:, 3072 + 512 * i:3584 + 512 * i] for i in range(2)]
        gate = work[:, 0:512].rearrange("p (t c) -> p t c", t=2)
        actn = work[:, 512:1024].rearrange("p (t c) -> p t c", t=2)
        uT = work[:, 1024:1024 + 4 * (S + 2)].rearrange("p (k t) -> p k t", k=4)
        convx = QT
        mprobs = [work[:, 512 * i:512 * i + 512] for i in range(4)]
        PAD = 8
        poolT = VD[:, :, :].rearrange("p t c -> p (t c)")[:, 0:4 * (PAD + S)].rearrange("p (g t) -> p g t", g=4)
        kt_hi = KT[:, 4:8, :].rearrange("p c t -> p (c t)")
        win = [kt_hi[:, (PAD + S) * i:(PAD + S) * (i + 1)] for i in range(2)]
        wmean = kt_hi[:, 2 * (PAD + S):2 * (PAD + S) + S]
        mixT = QT[:, 4:8, :]

        osq = Z[:, :, 2 * HALF:4 * HALF]
        conv_places = [Z[:, :, 0:512], Z[:, :, 512:1024], Z[:, :, 1024:1536], Z[:, :, 1536:2048],
                       nat[:, :, 0:512], nat[:, :, 512:1024]]
        KV_PAIR = (0, 1, 2, 1)
        kv_places = [Z[:, :, 0:512], Z[:, :, 512:1024], VD[:, :, 0:512], VD[:, :, 512:1024]]

        B = [ctx.enter_context(nc.psum_tensor(f"B{i}", [P, HALF], F32)) for i in range(6)]
        T = [ctx.enter_context(nc.psum_tensor(f"T{i}", [P, HALF], F32)) for i in range(2)]
        PAIR = [(B[0], B[1]), (B[2], B[3]), (B[4], B[5])]
        TURN = [T[0], T[1], B[4], B[5]]
        GU = PAIR[2]

        w_loaded = [sem(f"w_loaded{s}") for s in range(RING)]
        w_hi, w_lo, w_used = sem("w_hi_written"), sem("w_lo_written"), sem("w_unit_used")
        in_mem = [sem(f"mem_tok{t}_in") for t in range(TOKS)]
        in_x, in_id, in_small, in_const = sem("x_in"), sem("ident_in"), sem("small_in"), sem("const_in")
        in_gain, in_mgain = sem("gain_rows_in"), sem("memory_gain_row_in")
        gain_T, gain_ok = sem("gains_turned"), sem("gains_ready")
        post_in = [sem(f"post_gain{i}_in") for i in range(2)]
        t_done, xt_hi, xt_lo = sem("chunk_turned"), sem("xt_hi_written"), sem("xt_lo_written")
        ssq, rstd = sem("row_squares_summed"), sem("row_rstd_ready")
        h_up = sem("h_part_updated")
        tok0_done = sem("sum_tok0_half_done")
        mq_tok0 = sem("memory_queries_tok0_done")
        ev_a, ev_d = sem("group_evacuated_tok0"), sem("group_evacuated_tok1")
        hn_sq, hn_sum, hn_r, hn_x = sem("head_squared"), sem("head_summed"), sem("head_rstd"), sem("head_normed")
        ht, ht_a, ht_d = sem("heads_turned"), sem("heads_T_bank0_out"), sem("heads_T_bank1_out")
        wf_hi_s, wf_lo_s = sem("wf_hi_written"), sem("wf_lo_written")
        f_done, f_out, f_act, f_log = sem("f_product"), sem("f_logit_out"), sem("f_exp_ln"), sem("f_log_ready")
        c_done, c_out = sem("cumsum_done"), sem("cumsum_out")
        pt_done, pt_out = sem("pool_turned"), sem("pool_T_out")
        mixed_ok, py_done, py_out = sem("pool_mixed"), sem("pool_product"), sem("pool_out")
        at_s, at_m, at_x, at_e, at_r, at_c, at_v = (sem("scores_done"), sem("scores_masked"), sem("row_max_ready"),
                                                    sem("exp_done"), sem("probs_turned"), sem("probs_T_out"),
                                                    sem("values_done"))
        at_o, at_a = sem("attention_out"), sem("diff_probs_ready")
        pads_ok = sem("pool_pads_zero")
        eps_l = sem("eps_sum2_ready")
        lam_ok = sem("lambda_ready")
        gate_ok, act_ok, act_t, act_hi, act_lo = (sem("gate_ready"), sem("act_ready"), sem("act_turned"),
                                                  sem("act_hi_written"), sem("act_lo_written"))
        conv_p, conv_t, conv_u, conv_c, conv_x = (sem("conv_product_ready"), sem("conv_turned"), sem("conv_u_out"),
                                                  sem("conv_taps_summed"), sem("conv_x_ready"))
        dve_step, act_step, pool_step = sem("dve_step"), sem("act_step"), sem("pool_step")
        out_done = sem("out_written")

        block = ctx.enter_context(nc.Block())

        M_S, M_X, M_E, M_R = FOX_H, 2 * FOX_H, 2 * FOX_H, FOX_H
        D_S, D_M, D_X, D_E, D_R = M_S + MEM_H, 2 * FOX_H, M_X + MEM_H, M_E + 2 * MEM_H, M_R + MEM_H
        HT_KM, HT_QF, HT_KF, HT_QM, HT_KD, HT_QD = 0, 1, 2, 3, 4, 6
        FEED_U, FEED_B = (1, 2, 5, 6), (3, 4, 7, 8)
        EV_MEMKV, EV_IN, EV_CIN, EV_KV, EV_Q = 0, 2, 6, 12, 16
        HN_D = 5

        @block.sync
        def _(sp):
            def load(u, slot, parts):
                if not (isinstance(u, int) and u < RING):
                    sp.wait_ge(w_lo, u - RING + 1)
                for dst, src in parts:
                    sp.dma_start(dst, src).then_inc(w_loaded[slot], 16)

            def k_unit(u, w, k0, col):
                v = w.rearrange("(k p) f -> p k f", p=P)
                r = raw[u % RING][:, :].rearrange("p (k c) -> p k c", k=4)
                load(u, u % RING, [(r[:, i:i + 2, :], v[:, k0 + i:k0 + i + 2, col:col + HALF]) for i in (0, 2)])

            def ffn(u0, w_gu, w_dn):
                gu = w_gu.rearrange("(k p) f -> p k f", p=P)
                dn = w_dn.rearrange("(k p) f -> k p f", p=P)

                def up(j, u, slot, k0):
                    r = raw[slot][:, :].rearrange("p (k c) -> p k c", k=4)
                    load(u, slot, [(r[:, :, 0:256], gu[:, k0:k0 + 4, bass.ds(j * 256, 256)]),
                                   (r[:, :, 256:512], gu[:, k0:k0 + 4, bass.ds(j * 256 + FF, 256)])])

                def down(j, u, slot):
                    rows = w_dn[bass.ds(j * 256, 256), :].rearrange("(k p) f -> p k f", p=P)
                    load(u, slot, [(raw[slot][:, D * k:D * k + D], rows[:, k, :]) for k in range(2)])

                up(0, u0, u0 % RING, 0)
                up(0, u0 + 1, (u0 + 1) % RING, 4)

                def step(i):
                    up(i + 1, u0 + 2 + 3 * i, (u0 + 2) % RING, 0)
                    up(i + 1, u0 + 3 + 3 * i, (u0 + 3) % RING, 4)
                    down(i, u0 + 4 + 3 * i, (u0 + 4) % RING)

                with sp.Fori(0, FJ - 2) as i:
                    step(i)
                step(FJ - 2)
                down(FJ - 1, u0 + 32, (u0 + 32) % RING)

            def k_groups(u0, w, cols):
                for g, col in enumerate(cols):
                    k_unit(u0 + 2 * g, w, 0, col)
                    k_unit(u0 + 2 * g + 1, w, 4, col)

            k_groups(U_MEMKV, a["w_mem_kv"][0], (0, 512))
            k_groups(U_IN, a["w_in"][0], (0, 512, 1536, 1024))
            k_groups(U_OUT, a["w_out"][0], (0, 512))
            k_groups(U_MQ, a["w_mem_q"][0], (0,))
            k_unit(U_MO, a["w_mem_out"][0], 0, 0)
            k_unit(U_MO + 1, a["w_mem_out"][0], 0, 512)
            ffn(U_FFN[0], a["w_gate_up"][0], a["w_down"][0])
            ffn(U_FFN[1], a["ffn_w_gu_2"][0, 0], a["ffn_w_down_2"][0, 0])
            k_groups(U_CIN, a["conv_w_in_2"][0], (0, 1024, 2048, 1536, 2560, 512))
            k_groups(U_COUT, a["conv_w_out_2"][0], (0, 512))
            ffn(U_FFN[2], a["ffn_w_gu_2"][0, 1], a["ffn_w_down_2"][0, 1])
            k_groups(U_KV, a["w_kv_2"], (0, 512, 1024, 1536))
            ffn(U_FFN[3], a["ffn_w_gu_2"][1, 0], a["ffn_w_down_2"][1, 0])
            k_groups(U_Q, a["attn_w_q_2"][0], (0, 512))
            k_groups(U_O, a["attn_w_o_2"][0], (0, 512))
            ffn(U_FFN[4], a["ffn_w_gu_2"][1, 1], a["ffn_w_down_2"][1, 1])
            for t in range(TOKS):
                for half in range(2):
                    sp.wait_ge(h_up, h_ready("out", t, half))
                    sp.dma_start(out[0, t * P:t * P + P, half * HALF:half * HALF + HALF],
                                 h[:, t, half * HALF:half * HALF + HALF]).then_inc(out_done, 16)
            sp.wait_ge(out_done, 64)

        @block.gpsimd
        def _(pool):
            steps = [0]

            def link(ins):
                steps[0] += 1
                ins.then_inc(pool_step, 1)
                pool.wait_ge(pool_step, steps[0])

            for o, n in ((G_MIX, "g_mix"), (G_MEMQ, "g_mem_q"), (G_FFN, "g_ffn")):
                pool.dma_start(grow2[o - G_ROWS1:o - G_ROWS1 + 8, :],
                               a[n][0].rearrange("(k c) -> k c", c=P)).then_inc(in_gain, 16)
            pool.dma_start(grow2[32:40, :], a["kv_norm_g_2"].rearrange("(k c) -> k c", c=P)).then_inc(in_gain, 16)
            pool.dma_start(grow2[40:44, :], a["pool_scale"][0].rearrange("(k c) -> k c", c=P)).then_inc(in_gain, 16)
            pool.dma_start(grow2[44:45, :], a["attn_subln_g_2"]).then_inc(in_gain, 16)
            for r, n in ((45, "g_q_fox"), (46, "g_k_fox")):
                for c in range(2):
                    pool.dma_start(grow2[r:r + 1, 64 * c:64 * c + 64], a[n]).then_inc(in_gain, 16)
            pool.dma_start(grow2[47:48, :], a["g_q_mem"]).then_inc(in_gain, 16)
            pool.dma_start(grow2[48:49, :], a["g_k_mem"]).then_inc(in_gain, 16)
            pool.dma_start(grow1[0:96, :], a["norm_g_2"].rearrange("l i (k c) -> (l i k) c", c=P)).then_inc(in_gain, 16)
            pool.dma_start(grow1[96:120, :], a["conv_k_2"].rearrange("l w (k c) -> (l w k) c", c=P)).then_inc(in_gain, 16)
            pool.memset(mhalf[:, :], -0.5).then_inc(pool_step, 1)
            steps[0] += 1
            pool.wait_ge(pool_step, steps[0])
            with nc.allow_non_contiguous_dma(reason="8 columns of w_in"):
                pool.dma_start(wf[:, :, :], a["w_in"][0].rearrange("(k p) f -> p k f", p=P)[:, :, 2048:2056])\
                    .then_inc(in_small, 16)
            pool.dma_start(bf[:, :], a["b_forget"][0].partition_broadcast(P)).then_inc(in_small, 16)
            pool.dma_start(wpool[:, :, :], a["w_pool"][0].rearrange("g c d -> c g d")).then_inc(in_small, 16)
            pool.dma_start(lamp[:, :, :], a["attn_lambda_2"][0].partition_broadcast(P)).then_inc(in_small, 16)
            for dst, name in ((tri, "c_tri"), (foxmask, "c_mask"), (dist, "c_dist"), (sel, "c_sel"), (cnt16, "c_cnt")):
                full = (slice(None),) * len(dst.shape)
                pool.dma_start(dst[full], a[name][full]).then_inc(in_const, 16)

            def post_gain(b, layer, i):
                if b >= 2:
                    pool.wait_ge(h_up, 4 * (3 + b - 2) + 4)
                pool.dma_start(gpost[:, b % 2, :], a["norm_g_2"][layer, i].partition_broadcast(P))\
                    .then_inc(post_in[b % 2], 16)

            def windows():
                pool.wait_ge(pt_out, 2)
                pool.wait_ge(in_const, 80)
                for g, w in enumerate(WINDOWS):
                    if g == 0:
                        pool.wait_ge(pads_ok, 3)
                    src = poolT[:, g, :]
                    for level in range(g + 1):
                        d = 1 << level
                        dst = win[level % 2]
                        link(pool.tensor_tensor(dst[:, PAD:PAD + S], src[:, PAD:PAD + S], src[:, PAD - d:PAD + S - d],
                                                ALU.add))
                        src = dst
                    link(pool.tensor_scalar(wmean, src[:, PAD:PAD + S], 1.0 / w, 0.0, ALU.mult, ALU.add))
                    link(pool.tensor_tensor(wmean[:, 0:16], src[:, PAD:PAD + 16], cnt16[:, g, :], ALU.mult))
                    pool.tensor_tensor(mixT[:, g, :], wmean, poolT[:, g, PAD:PAD + S], ALU.subtract)\
                        .then_inc(mixed_ok, 1)
                    pool.wait_ge(mixed_ok, g + 1)

            def rsqrt(dst, var, src, scale, eps, done):
                link(pool.tensor_scalar(var, src, scale, eps, ALU.mult, ALU.add))
                pool.tensor_tensor(dst, var, mhalf[:, 0:dst.shape[1]], ALU.pow).then_inc(done, 1)

            def row_stat(name, m=1.0):
                s = ST[name]
                for t in range(TOKS):
                    pool.wait_ge(ssq, 4 * s + 2 * t + 2)
                    v = SV[:, s, t:t + 1]
                    link(pool.tensor_tensor(v, SS[:, s, t, 0:1], SS[:, s, t, 1:2], ALU.add))
                    rsqrt(RS[:, s, t:t + 1], v, v, m / D, m * EPS, rstd)

            def head_stat(n, count, dh, m=1.0):
                pool.wait_ge(hn_sum, n + 1)
                rsqrt(HR[:, n, 0:count], HV[:, n, 0:count], HS[:, n, 0:count], m / dh, m * EPS, hn_r)

            post_gain(0, 0, 1)
            post_gain(1, 0, 3)
            row_stat("mem")
            head_stat(0, TOKS * MEM_H, MEM_DH)
            row_stat("h0")
            head_stat(1, TOKS * FOX_H, FOX_DH)
            head_stat(2, TOKS * FOX_H, FOX_DH)
            windows()
            row_stat("h1")
            for t in range(TOKS):
                c = slice(t * MEM_H, t * MEM_H + MEM_H)
                pool.wait_ge(hn_sum, 3 + t + 1)
                link(pool.tensor_scalar(HV[:, 3, c], HS[:, 3, c], 1.0 / MEM_DH, EPS, ALU.mult, ALU.add))
                link(pool.tensor_tensor(HV[:, 3, c], HV[:, 3, c], mhalf[:, 0:MEM_H], ALU.pow))
                pool.tensor_tensor(HR[:, 3, c], HV[:, 3, c], RS[:, ST["h1"], t:t + 1].to_broadcast([P, MEM_H]),
                                   ALU.mult).then_inc(hn_r, 1)
            row_stat("h2")
            row_stat("h3")
            row_stat("y0", 4.0)
            row_stat("h4")
            for n, g in enumerate((2, 4)):
                pool.wait_ge(ev_a, EV_CIN + g + 1)
                pool.wait_ge(ev_d, EV_CIN + g + 1)
                pool.tensor_tensor(conv_places[g - 1], conv_places[g - 1], conv_places[g], ALU.mult).then_inc(conv_p, 1)
            row_stat("y1")
            post_gain(2, 0, 5)
            row_stat("h5")
            row_stat("y2", 4.0)
            post_gain(3, 1, 1)
            row_stat("h6")
            row_stat("y3", 4.0)
            post_gain(4, 1, 3)
            row_stat("h7")
            for g in range(2):
                c = slice(8 * g, 8 * g + 8)
                l0 = lsum[:, 16 * g:16 * g + 16].rearrange("p (h c t) -> p c t h", c=2, t=2)[:, 0]
                pool.wait_ge(at_e, D_E + 16 * (g + 1))
                e = epsl[:, c].rearrange("p (t h) -> p t h", t=2)
                link(pool.tensor_tensor(e, l0, l0, ALU.mult))
                pool.tensor_scalar(epsl[:, c], epsl[:, c], SUB_M * EPS, 0.0, ALU.mult, ALU.add).then_inc(eps_l, 1)
                for t in range(TOKS):
                    n = 2 * g + t
                    pool.wait_ge(hn_sum, HN_D + n + 1)
                    pool.tensor_tensor(HR[:, 4, 4 * n:4 * n + 4], HV[:, 4, 4 * n:4 * n + 4], mhalf[:, 0:4], ALU.pow)\
                        .then_inc(hn_r, 1)
            row_stat("y4")
            post_gain(5, 1, 5)
            row_stat("h8")
            row_stat("y5", 4.0)

        @block.scalar
        def _(act):
            act.dma_start(ident[:, :], a["c_ident"]).then_inc(in_id, 16)
            act.dma_start(grow2[0:8, :], a["g_mem_kv"][0].rearrange("(k c) -> k c", c=P)).then_inc(in_mgain, 16)
            for t in range(TOKS):
                act.dma_start(nat[:, t, :], a["mem"][0, t * P:t * P + P, :]).then_inc(in_mem[t], 16)

            def split(u, slot, n):
                act.wait_ge(w_loaded[slot], 32 * (n + 1))
                if not (isinstance(u, int) and u < RING):
                    act.wait_ge(w_used, u - RING + 1)
                act.activation(whi[slot][:, :], raw[slot][:, :], ACT.Copy).then_inc(w_hi, 1)

            def split_at(*units):
                for u in units:
                    if u < UNITS:
                        split(u, u % RING, u // RING)

            def turned_hi(name, gain_cols, t):
                for k in range(CHUNKS[name]):
                    if k % 2 == 0:
                        act.wait_ge(t_done, TD[name] + (t * CHUNKS[name] + k) // 2 + 1)
                    g = gain_cols(k)
                    act.activation(xhi[:, k, t * P:t * P + P], TURN[k // 2][:, (k % 2) * P:(k % 2) * P + P], ACT.Copy,
                                   scale=gains[:, g:g + 1]).then_inc(xt_hi, 1)

            def tok_squares(stat, src, t, waits):
                for half in range(2):
                    if waits:
                        act.wait_ge(*waits[half])
                    if ST[stat] or half or t:
                        act.wait_ge(ssq, 4 * ST[stat] + 2 * t + half)
                    act.activation(junk[:, :], src(t, half), ACT.Square,
                                   accum_out=SS[:, ST[stat], t, half:half + 1]).then_inc(ssq, 1)

            def h_squares(stat, reader, t):
                waits = [(in_x, 16)] * 2 if reader == "x" else [(h_up, h_ready(reader, t, half)) for half in range(2)]
                tok_squares(stat, lambda t, half: h[:, t, half * HALF:half * HALF + HALF], t, waits)

            def sum_squares(stat, reader, u_last, late_split=None):
                tok_squares(stat, lambda t, half: PAIR[half][t][:, :], 0,
                            [(tok0_done, 2 * H_UP[reader] + half + 1) for half in range(2)])
                if late_split is not None:
                    split_at(late_split)
                tok_squares(stat, lambda t, half: PAIR[half][t][:, :], 1, [(w_used, u_last + 1)] * 2)

            def turned(name, gain_cols, u0, squares=lambda t: None):
                turned_hi(name, gain_cols, 0)
                squares(0)
                turned_hi(name, gain_cols, 1)
                split_at(u0 + 2)
                squares(1)

            def evac(e, u_last, dst, pair, stat):
                act.wait_ge(w_used, u_last + 1)
                act.wait_ge(rstd, 2 * ST[stat] + 1)
                act.activation(dst, pair[0][:, :], ACT.Copy, scale=RS[:, ST[stat], 0:1]).then_inc(ev_a, 1)

            def head_square(n, src, e):
                act.wait_ge(ev_a, e + 1)
                act.wait_ge(ev_d, e + 1)
                if n:
                    act.wait_ge(hn_sum, n)
                act.activation(SQ[:, :].rearrange("p (t c) -> p t c", t=2), src, ACT.Square).then_inc(hn_sq, 1)

            def heads_out(n, dst, gain_col=None, scale=1.0):
                act.wait_ge(ht, 2 * n + 1)
                g = scale if gain_col is None else gains[:, gain_col:gain_col + 1]
                act.activation(dst, T[0][:, :].rearrange("p (c t) -> p c t", c=2), ACT.Copy, scale=g)\
                    .then_inc(ht_a, 1)

            split_at(0)
            act.dma_start(h[:, :, :], a["x"][0].rearrange("(t p) d -> p t d", p=P)).then_inc(in_x, 16)
            act.wait_ge(gain_ok, 2)
            turned_hi("mem", lambda k: G_MEMKV + k, 0)
            split_at(1)
            tok_squares("mem", lambda t, half: nat[:, t, half * HALF:half * HALF + HALF], 0, [(in_mem[0], 16)] * 2)
            turned_hi("mem", lambda k: G_MEMKV + k, 1)
            split_at(2)
            tok_squares("mem", lambda t, half: nat[:, t, half * HALF:half * HALF + HALF], 1, [(in_mem[1], 16)] * 2)
            split_at(3)
            evac(EV_MEMKV, 1, nat[:, 0, 0:HALF], PAIR[0], "mem")
            head_square(0, nat[:, :, 0:HALF], EV_MEMKV)
            split_at(4, 5)
            evac(EV_MEMKV + 1, 3, memV[:, 0, :], PAIR[1], "mem")
            act.wait_ge(gain_ok, 6)
            turned("x", lambda k: G_MIX + k, U_IN, lambda t: h_squares("h0", "x", t))
            act.wait_ge(in_small, 64)
            act.activation(wfhi[:, :, :], wf[:, :, :], ACT.Copy).then_inc(wf_hi_s, 1)
            split_at(7)
            evac(EV_IN, 5, Z[:, 0, 0:512], PAIR[0], "h0")
            head_square(1, Z[:, :, 0:512], EV_IN)
            split_at(8, 9)
            evac(EV_IN + 1, 7, Z[:, 0, 512:1024], PAIR[1], "h0")
            head_square(2, Z[:, :, 512:1024], EV_IN + 1)
            act.wait_ge(f_out, 3)
            act.activation(fl[:, 2, :], fl[:, 1, :], ACT.Exp, scale=-1.0).then_inc(f_act, 1)
            act.wait_ge(f_act, 1)
            act.activation(fl[:, 3, :], fl[:, 2, :], ACT.Ln, bias=1.0).then_inc(f_act, 1)
            act.wait_ge(lam_ok, 2)
            act.activation(lam4[:, 2:4], lam4[:, 0:2], ACT.Exp).then_inc(lam_ok, 1)
            split_at(10)
            heads_out(HT_KM, memKT[:, 0:2, :], G_KM)
            split_at(11)
            evac(EV_IN + 2, 9, Z[:, 0, 1024:1536], PAIR[2], "h0")
            heads_out(HT_QF, QT[:, 0:2, :], G_QF)
            split_at(12)
            heads_out(HT_KF, KT[:, 0:2, :], G_KF)
            split_at(13)
            evac(EV_IN + 3, 11, Z[:, 0, 1536:2048], PAIR[0], "h0")
            act.wait_ge(pt_done, 1)
            act.wait_ge(pads_ok, 3)
            act.activation(poolT[:, 0:2, PAD:PAD + S], T[0][:, :].rearrange("p (c t) -> p c t", c=2), ACT.Copy)\
                .then_inc(pt_out, 1)

            def probs_out(r0, i, cols):
                act.wait_ge(at_r, r0 + i + 1)
                if i >= 2:
                    act.wait_ge(at_v, r0 + i - 1)
                act.activation(pT[i % 2][:, 0:cols], T[i % 2][:, 0:cols], ACT.Copy).then_inc(at_c, 1)

            def causal_exp(x0, col0, i):
                act.wait_ge(at_x, x0 + 2 * i + 2)
                for t, c0, c1 in ((0, 0, 128), (1, 128, 384)):
                    col = col0 + 2 * i + t
                    act.activation(probs[i % 4][:, c0:c1], scores[i % 4][:, c0:c1], ACT.Exp,
                                   bias=nmax[:, col:col + 1], accum_out=lsum[:, col:col + 1]).then_inc(at_e, 1)

            for i in range(FOX_H + 1):
                if i < FOX_H:
                    if i >= 4:
                        act.wait_ge(at_r, i - 3)
                    causal_exp(0, 0, i)
                if i:
                    probs_out(0, i - 1, 384)
            act.wait_ge(py_done, 1)
            for t in range(TOKS):
                act.activation(nat[:, t, HALF:D], B[t][:, :], ACT.Copy).then_inc(py_out, 1)
            turned("mix", lambda k: G_ONE if k < 4 else G_POOL + k - 4, U_OUT)
            split_at(15, 16, 17)
            for t in range(TOKS):
                turned_hi("mq", lambda k: G_MEMQ + k, t)
                h_squares("h1", "mq", t)
            for t in range(TOKS):
                act.wait_ge(*((w_used, U_MQ + 2) if t else (mq_tok0, 1)))
                act.wait_ge(rstd, 2 * ST["h1"] + t + 1)
                act.wait_ge(hn_sum, 3)
                act.activation(SQ[:, t * HALF:t * HALF + HALF], PAIR[0][t][:, :], ACT.Square,
                               scale=RS[:, ST["h1"], t:t + 1]).then_inc(hn_sq, 1)
                if t == 0:
                    split_at(18)
            heads_out(HT_QM, QT[:, 0:2, :], G_QM)
            for i in range(MEM_H + 1):
                if i < MEM_H:
                    act.wait_ge(at_x, M_X + i + 1)
                    for t in range(TOKS):
                        col = 2 * i + t
                        act.activation(mprobs[i][:, t * S:t * S + S], B[i][:, t * S:t * S + S], ACT.Exp,
                                       bias=nmax[:, col:col + 1], accum_out=lsum[:, col:col + 1]).then_inc(at_e, 1)
                if i:
                    probs_out(M_R, i - 1, 512)
                if i == 2:
                    split_at(19)
            turned("mo", lambda k: G_ONE, U_MO)
            split_at(21)

            def ffn(f, stat, reader, gain, squares=True):
                u0 = U_FFN[f]
                v = u0 + 2
                turned(reader, lambda k: gain + k, u0, (lambda t: h_squares(stat, reader, t)) if squares else lambda t: None)

                def gate_of(j, u, pair):
                    act.wait_ge(w_used, u + 1)
                    if not (isinstance(j, int) and j == 0 and f == 0):
                        act.wait_ge(act_ok, 2 * (FJ * f + j))
                    for t in range(TOKS):
                        act.activation(gate[:, t, :], pair[t][:, 0:256], ACT.Silu,
                                       scale=RS[:, ST[stat], t:t + 1]).then_inc(gate_ok, 1)

                def act_out(j, hi=ahi[:, :]):
                    act.wait_ge(act_t, FJ * f + j + 1)
                    act.activation(hi, T[0][:, :], ACT.Copy).then_inc(act_hi, 1)

                split_at(u0 + 3)
                act.wait_ge(rstd, 2 * ST[stat] + 2)
                gate_of(0, u0 + 1, PAIR[0])

                def step(i, last):
                    split(v + 3 * i + 2, (v + 2) % RING, i + (v + 2) // RING)
                    act_out(i)
                    split(v + 3 * i + 3, (v + 3) % RING, i + (v + 3) // RING)
                    gate_of(i + 1, v + 3 * i + 1, GU)
                    if not (last and v + 3 * i + 4 >= UNITS):
                        split(v + 3 * i + 4, (v + 4) % RING, i + (v + 4) // RING)

                with act.Fori(0, FJ - 2) as i:
                    step(i, False)
                step(FJ - 2, True)
                act_out(FJ - 1, last_hi)
                split_at(u0 + 34)

            ffn(0, "h2", "ffn0", G_FFN)
            ffn(1, "h3", "ffn1", n2(0, 0))
            sum_squares("y0", "cin", U_FFN[1] + 32)
            turned("cin", lambda k: n2(0, 2) + k, U_CIN, lambda t: h_squares("h4", "cin", t))
            def conv_evac(g):
                evac(EV_CIN + g, U_CIN + 2 * g + 1, conv_places[g][:, 0, :], PAIR[g % 3], "h4")

            def conv_u_out(p):
                act.wait_ge(conv_t, FEED_U[p])
                if p >= 2:
                    act.wait_ge(conv_c, p - 1)
                else:
                    act.wait_ge(pads_ok, 4)
                u = T[p % 2][:, :].rearrange("p (k t) -> p k t", k=2)
                act.activation(uT[:, 2 * p % 4:2 * p % 4 + 2, 2:2 + S], u, ACT.Copy)
                for k in (2 * p, 2 * p + 1):
                    ins = act.activation(convx[:, k, :], u[:, k % 2, :], ACT.Copy,
                                         scale=gains[:, G_CONV + 16 + k:G_CONV + 17 + k])
                ins.then_inc(conv_u, 1)

            def conv_hi(p):
                act.wait_ge(conv_x, p + 1)
                act.wait_ge(w_used, U_CIN + 11 if p < 2 else U_CIN + 12)
                act.activation(xhi[:, 2 * p:2 * p + 2, :], convx[:, 2 * p:2 * p + 2, :], ACT.Copy).then_inc(xt_hi, 2)

            split_at(U_CIN + 3)
            conv_evac(0)
            for g in (1, 2, 3):
                split_at(U_CIN + 2 * g + 2, U_CIN + 2 * g + 3)
                if g == 3:
                    conv_u_out(0)
                conv_evac(g)
            split_at(U_CIN + 10)
            conv_u_out(1)
            split_at(U_CIN + 11)
            conv_evac(4)
            split_at(U_COUT, U_COUT + 1)
            conv_u_out(2)
            conv_hi(0)
            conv_hi(1)
            conv_u_out(3)
            conv_evac(5)
            conv_hi(2)
            conv_hi(3)
            split_at(*range(U_COUT + 2, U_COUT + 5))
            sum_squares("y1", "ffn2", U_COUT + 3, U_COUT + 5)
            ffn(2, "h5", "ffn2", n2(0, 4))
            sum_squares("y2", "kv", U_FFN[2] + 32)
            turned("kv", lambda k: G_KV + k, U_KV, lambda t: h_squares("h6", "kv", t))
            for g in range(4):
                split_at(*range(U_KV + 2 * g + (3 if g == 0 else 2), U_KV + 2 * g + 4))
                evac(EV_KV + g, U_KV + 2 * g + 1, kv_places[g][:, 0, :], PAIR[KV_PAIR[g]], "h6")
            heads_out(HT_KD, KT[:, 0:2, :])
            heads_out(HT_KD + 1, KT[:, 4:6, :])
            ffn(3, "h6", "ffn3", n2(1, 0), squares=False)
            sum_squares("y3", "q", U_FFN[3] + 32)
            turned("q", lambda k: n2(1, 2) + k, U_Q, lambda t: h_squares("h7", "q", t))
            for g in range(2):
                split_at(*range(U_Q + 2 * g + (3 if g == 0 else 2), U_Q + 2 * g + 4))
                evac(EV_Q + g, U_Q + 2 * g + 1, Z[:, 0, 512 * g:512 * g + 512], PAIR[g], "h7")
            heads_out(HT_QD, QT[:, 0:2, :], scale=DIFF_DH ** -0.5)
            heads_out(HT_QD + 1, QT[:, 4:6, :], scale=DIFF_DH ** -0.5)

            def o_squares(g):
                act.wait_ge(at_v, D_R + 4 * g + 4)
                for t in range(TOKS):
                    act.activation(osq[:, t, g * HALF:g * HALF + HALF], PAIR[g][t][:, :], ACT.Square)\
                        .then_inc(hn_sq, 1)

            for i in range(DIFF_H + 1):
                if i < DIFF_H:
                    for m in (2 * i, 2 * i + 1):
                        if m >= 4:
                            act.wait_ge(at_r, D_R + i - 1)
                        causal_exp(D_X, 0, m)
                if i:
                    probs_out(D_R, i - 1, 384)
                if i == 5:
                    o_squares(0)
            o_squares(1)
            turned("ao", lambda k: G_SUB, U_O)
            split_at(*range(U_O + 3, U_O + 5))
            sum_squares("y4", "ffn4", U_O + 3, U_O + 5)
            ffn(4, "h8", "ffn4", n2(1, 4))
            sum_squares("y5", "out", U_FFN[4] + 32)

        @block.vector
        def _(dve):
            steps = [0]

            def link(ins):
                steps[0] += 1
                ins.then_inc(dve_step, 1)
                dve.wait_ge(dve_step, steps[0])

            def split(u, slot):
                dve.wait_ge(w_hi, u + 1)
                dve.tensor_tensor(wlo[slot][:, :], raw[slot][:, :], whi[slot][:, :].bitcast(F32), ALU.subtract)\
                    .then_inc(w_lo, 1)

            def split_at(*units):
                for u in units:
                    if u < UNITS:
                        split(u, u % RING)

            def turned_lo(name, gain_cols, t, k0=0, k1=KD):
                for k in range(k0, min(k1, CHUNKS[name])):
                    if k % 2 == 0:
                        dve.wait_ge(xt_hi, XT[name] + t * CHUNKS[name] + k + 2)
                    g = gain_cols(k)
                    x = slice(t * P, t * P + P)
                    dve.scalar_tensor_tensor(out=xlo[:, k, x], in0=TURN[k // 2][:, (k % 2) * P:(k % 2) * P + P],
                                             scalar=gains[:, g:g + 1], in1=xhi[:, k, x].bitcast(F32),
                                             op0=ALU.mult, op1=ALU.subtract).then_inc(xt_lo, 1)

            def turned(name, gain_cols, u0, update=lambda t: None, late_split=False):
                update(0)
                turned_lo(name, gain_cols, 0, 0, 4)
                if late_split:
                    split_at(u0 + 1)
                turned_lo(name, gain_cols, 0, 4)
                update(1)
                turned_lo(name, gain_cols, 1)
                split_at(u0 + 2)

            def evac(e, u_last, dst, pair, stat):
                dve.wait_ge(w_used, u_last + 1)
                dve.wait_ge(rstd, 2 * ST[stat] + 2)
                dve.tensor_scalar(dst, pair[1][:, :], RS[:, ST[stat], 1:2], None, ALU.mult).then_inc(ev_d, 1)

            def head_norm(n, x, heads, dh):
                dve.wait_ge(hn_sq, n + 1)
                dve.tensor_reduce(HS[:, n, 0:TOKS * heads], SQ[:, :].rearrange("p (h d) -> p h d", d=dh), AX.X, ALU.add)\
                    .then_inc(hn_sum, 1)
                dve.wait_ge(hn_r, n + 1)
                v = x.rearrange("p t (h d) -> p t h d", d=dh)
                for t in range(TOKS):
                    r = HR[:, n, t * heads:(t + 1) * heads].unsqueeze(2).to_broadcast([P, heads, dh])
                    dve.tensor_tensor(v[:, t], v[:, t], r, ALU.mult).then_inc(hn_x, 1)

            def heads_out(n, dst, gain_col=None, scale=1.0):
                dve.wait_ge(ht, 2 * n + 2)
                g = scale if gain_col is None else gains[:, gain_col:gain_col + 1]
                dve.tensor_scalar(dst, T[1][:, :].rearrange("p (c t) -> p c t", c=2), g, None, ALU.mult)\
                    .then_inc(ht_d, 1)

            def h_update(reader, u_last, t):
                for half in range(2):
                    dve.wait_ge(*((w_used, u_last + 1) if t else (tok0_done, 2 * H_UP[reader] + half + 1)))
                    part = h[:, t, half * HALF:half * HALF + HALF]
                    dve.tensor_tensor(part, part, PAIR[half][t][:, :], ALU.add).then_inc(h_up, 1)

            def post_update(b, stat, reader, t):
                if t == 0:
                    dve.wait_ge(post_in[b % 2], 16 * (b // 2 + 1))
                dve.wait_ge(rstd, 2 * ST[stat] + t + 1)
                for half in range(2):
                    c = slice(half * HALF, half * HALF + HALF)
                    if half or t:
                        dve.wait_ge(h_up, h_ready(reader, t, half) - 1)
                    link(dve.scalar_tensor_tensor(out=tmp[:, half, :], in0=PAIR[half][t][:, :],
                                                  scalar=RS[:, ST[stat], t:t + 1], in1=gpost[:, b % 2, c],
                                                  op0=ALU.mult, op1=ALU.mult))
                    dve.tensor_tensor(h[:, t, c], h[:, t, c], tmp[:, half, :], ALU.add).then_inc(h_up, 1)

            dve.memset(VD[:, :, :], 0.0).then_inc(pads_ok, 1)
            dve.memset(win[0], 0.0).then_inc(pads_ok, 1)
            dve.memset(win[1], 0.0).then_inc(pads_ok, 1)
            dve.memset(gains[:, G_ONE:G_ONE + 1], 1.0).then_inc(gain_ok, 1)
            dve.wait_ge(gain_T, 1)
            dve.tensor_copy(gains[:, G_MEMKV:G_MEMKV + 8], T[0][:, 0:8]).then_inc(gain_ok, 1)
            dve.wait_ge(gain_ok, 2)
            split_at(0)
            turned("mem", lambda k: G_MEMKV + k, U_MEMKV, late_split=True)
            split_at(3)
            dve.wait_ge(gain_T, 2)
            dve.tensor_copy(gains[:, 0:G_ROWS1], T[0][:, 0:G_ROWS1]).then_inc(gain_ok, 1)
            dve.tensor_copy(gains[:, G_ROWS1 + 8:G_ROWS1 + G_ROWS2], T[0][:, 136:128 + G_ROWS2]).then_inc(gain_ok, 1)
            dve.wait_ge(gain_ok, 4)
            for g, dh in ((G_QF, FOX_DH), (G_QM, MEM_DH)):
                dve.tensor_scalar(gains[:, g:g + 1], gains[:, g:g + 1], dh ** -0.5, None, ALU.mult).then_inc(gain_ok, 1)
            dve.wait_ge(gain_ok, 6)
            evac(EV_MEMKV, 1, nat[:, 1, 0:HALF], PAIR[0], "mem")
            head_norm(0, nat[:, :, 0:HALF], MEM_H, MEM_DH)
            split_at(4, 5)
            evac(EV_MEMKV + 1, 3, memV[:, 1, :], PAIR[1], "mem")
            turned("x", lambda k: G_MIX + k, U_IN)
            dve.wait_ge(wf_hi_s, 1)
            dve.tensor_tensor(wflo[:, :, :], wf[:, :, :], wfhi[:, :, :].bitcast(F32), ALU.subtract).then_inc(wf_lo_s, 1)
            for i in range(2):
                link(dve.tensor_tensor(work[:, 64 * i:64 * i + DIFF_DH], lamp[:, 2 * i, :], lamp[:, 2 * i + 1, :], ALU.mult))
                dve.reduce_sum(lam4[:, i:i + 1], work[:, 64 * i:64 * i + DIFF_DH], AX.X).then_inc(lam_ok, 1)
            split_at(7)
            evac(EV_IN, 5, Z[:, 1, 0:512], PAIR[0], "h0")
            head_norm(1, Z[:, :, 0:512], FOX_H, FOX_DH)
            split_at(8, 9)
            evac(EV_IN + 1, 7, Z[:, 1, 512:1024], PAIR[1], "h0")
            head_norm(2, Z[:, :, 512:1024], FOX_H, FOX_DH)
            dve.wait_ge(f_done, 1)
            f2 = fl[:, 0, :].rearrange("p (t c) -> p t c", t=2)
            for t in range(TOKS):
                dve.scalar_tensor_tensor(out=f2[:, t, :], in0=T[0][:, 8 * t:8 * t + 8], scalar=RS[:, ST["h0"], t:t + 1],
                                         in1=bf[:, :], op0=ALU.mult, op1=ALU.add).then_inc(f_out, 1)
            dve.wait_ge(f_out, 2)
            dve.scalar_tensor_tensor(out=fl[:, 1, :], in0=fl[:, 0, :], scalar=-1.0, in1=fl[:, 0, :], op0=ALU.mult,
                                     op1=ALU.max).then_inc(f_out, 1)
            dve.wait_ge(f_act, 2)
            dve.scalar_tensor_tensor(out=fl[:, 0, :], in0=fl[:, 0, :], scalar=0.0, in1=fl[:, 3, :], op0=ALU.min,
                                     op1=ALU.subtract).then_inc(f_log, 1)
            dve.wait_ge(lam_ok, 3)
            dve.scalar_tensor_tensor(out=lam4[:, 0:1], in0=lam4[:, 3:4], scalar=-lambda_init, in1=lam4[:, 2:3],
                                     op0=ALU.add, op1=ALU.subtract).then_inc(lam_ok, 1)
            split_at(10)
            heads_out(HT_KM, memKT[:, 2:4, :], G_KM)
            split_at(11)
            evac(EV_IN + 2, 9, Z[:, 1, 1024:1536], PAIR[2], "h0")
            heads_out(HT_QF, QT[:, 2:4, :], G_QF)
            split_at(12)
            heads_out(HT_KF, KT[:, 2:4, :], G_KF)
            dve.wait_ge(c_done, 1)
            dve.tensor_copy(cn[:, :, :], B[2][:, 0:16].rearrange("p (t c) -> p t c", t=2)).then_inc(c_out, 1)
            dve.tensor_copy(cT[:, :], B[3][0:FOX_H, 0:S]).then_inc(c_out, 1)
            split_at(13)
            evac(EV_IN + 3, 11, Z[:, 1, 1536:2048], PAIR[0], "h0")
            dve.wait_ge(pt_done, 2)
            dve.tensor_copy(poolT[:, 2:4, PAD:PAD + S], T[1][:, :].rearrange("p (c t) -> p c t", c=2)).then_inc(pt_out, 1)

            def row_max(i, col0):
                for t, c0, c1 in ((0, 0, 128), (1, 128, 384)):
                    col = col0 + 2 * i + t
                    dve.tensor_reduce(nmax[:, col:col + 1], scores[i % 4][:, c0:c1], AX.X, ALU.max, negate=True)\
                        .then_inc(at_x, 1)

            dve.wait_ge(in_const, 80)
            dve.wait_ge(c_out, 2)
            for i in range(FOX_H):
                dve.wait_ge(at_s, i + 1)
                if i >= 4:
                    dve.wait_ge(at_e, 2 * (i - 3))
                for t, c0, c1 in ((0, 0, 128), (1, 128, 384)):
                    dve.scalar_tensor_tensor(out=scores[i % 4][:, c0:c1], in0=B[i % 4][:, c0:c1],
                                             scalar=cn[:, t, i:i + 1], in1=foxmask[:, c0:c1], op0=ALU.add,
                                             op1=ALU.add).then_inc(at_m, 1)
                dve.wait_ge(at_m, 2 * i + 2)
                row_max(i, 0)

            def values_out(e0, count, v0, heads, dh):
                dve.wait_ge(at_e, e0 + count)
                link(dve.reciprocal(linv[:, 0:count], lsum[:, 0:count]))
                dve.wait_ge(at_v, v0 + heads)
                r = linv[:, 0:count].rearrange("p (h t) -> p t h", t=2)
                for t in range(TOKS):
                    dve.tensor_tensor(nat[:, t, 0:HALF].rearrange("p (h d) -> p h d", d=dh),
                                      B[4 + t][:, :].rearrange("p (h d) -> p h d", d=dh),
                                      r[:, t].unsqueeze(2).to_broadcast([P, heads, dh]), ALU.mult).then_inc(at_o, 1)

            values_out(0, 16, 0, FOX_H, FOX_DH)
            turned("mix", lambda k: G_ONE if k < 4 else G_POOL + k - 4, U_OUT)
            split_at(15, 16)
            for t in range(TOKS):
                h_update("mq", U_OUT + 3, t)
                if t == 0:
                    split_at(17)
                turned_lo("mq", lambda k: G_MEMQ + k, t)
            for t in range(TOKS):
                c = slice(t * MEM_H, t * MEM_H + MEM_H)
                dve.wait_ge(hn_sq, 3 + t + 1)
                dve.tensor_reduce(HS[:, 3, c], SQ[:, t * HALF:t * HALF + HALF].rearrange("p (h d) -> p h d", d=MEM_DH),
                                  AX.X, ALU.add).then_inc(hn_sum, 1)
                dve.wait_ge(hn_r, 3 + t + 1)
                dve.tensor_tensor(Z[:, t, 0:HALF].rearrange("p (h d) -> p h d", d=MEM_DH),
                                  PAIR[0][t][:, :].rearrange("p (h d) -> p h d", d=MEM_DH),
                                  HR[:, 3, c].unsqueeze(2).to_broadcast([P, MEM_H, MEM_DH]), ALU.mult).then_inc(hn_x, 1)
                if t == 0:
                    split_at(18)
            heads_out(HT_QM, QT[:, 2:4, :], G_QM)
            for i in range(MEM_H):
                dve.wait_ge(at_s, M_S + i + 1)
                dve.tensor_reduce(nmax[:, 2 * i:2 * i + 2], B[i][:, :].rearrange("p (t c) -> p t c", t=2), AX.X,
                                  ALU.max, negate=True).then_inc(at_x, 1)
            split_at(19)
            values_out(M_E, 8, M_R, MEM_H, MEM_DH)
            turned("mo", lambda k: G_ONE, U_MO)

            def ffn(f, stat, reader, gain, update=lambda t: None, late_split=False):
                u0 = U_FFN[f]
                v = u0 + 2
                turned(reader, lambda k: gain + k, u0, update, late_split)

                def act_of(j, pair):
                    for t in range(TOKS):
                        dve.wait_ge(gate_ok, 2 * (FJ * f + j) + t + 1)
                        dve.scalar_tensor_tensor(out=actn[:, t, :], in0=pair[t][:, 256:512],
                                                 scalar=RS[:, ST[stat], t:t + 1], in1=gate[:, t, :],
                                                 op0=ALU.mult, op1=ALU.mult).then_inc(act_ok, 1)

                def act_out(j, hi=ahi[:, :], lo=alo[:, :]):
                    dve.wait_ge(act_hi, FJ * f + j + 1)
                    dve.tensor_tensor(lo, T[0][:, :], hi.bitcast(F32), ALU.subtract).then_inc(act_lo, 1)

                split_at(u0 + 3)
                dve.wait_ge(rstd, 2 * ST[stat] + 2)
                act_of(0, PAIR[0])

                def step(i, last):
                    split(v + 3 * i + 2, (v + 2) % RING)
                    act_out(i)
                    split(v + 3 * i + 3, (v + 3) % RING)
                    act_of(i + 1, GU)
                    if not (last and v + 3 * i + 4 >= UNITS):
                        split(v + 3 * i + 4, (v + 4) % RING)

                with dve.Fori(0, FJ - 2) as i:
                    step(i, False)
                step(FJ - 2, True)
                act_out(FJ - 1, last_hi, last_lo)
                split_at(u0 + 34)

            ffn(0, "h2", "ffn0", G_FFN, lambda t: h_update("ffn0", U_MO + 1, t), late_split=True)
            ffn(1, "h3", "ffn1", n2(0, 0), lambda t: h_update("ffn1", U_FFN[0] + 32, t))
            turned("cin", lambda k: n2(0, 2) + k, U_CIN, lambda t: post_update(0, "y0", "cin", t))
            def conv_evac(g):
                evac(EV_CIN + g, U_CIN + 2 * g + 1, conv_places[g][:, 1, :], PAIR[g % 3], "h4")

            def conv_taps(p):
                dve.wait_ge(conv_u, p + 1)
                for w in (1, 0):
                    for k in (2 * p, 2 * p + 1):
                        if w == 0 and k == 2 * p:
                            dve.wait_ge(dve_step, steps[0])
                        g = gains[:, G_CONV + 8 * w + k:G_CONV + 8 * w + k + 1]
                        ins = dve.scalar_tensor_tensor(out=convx[:, k, :], in0=uT[:, k % 4, w:w + S], scalar=g,
                                                       in1=convx[:, k, :], op0=ALU.mult, op1=ALU.add)
                    if w:
                        steps[0] += 1
                        ins.then_inc(dve_step, 1)
                ins.then_inc(conv_c, 1)

            def conv_gate(p):
                dve.wait_ge(conv_t, FEED_B[p])
                dve.wait_ge(conv_c, p + 1)
                x = convx[:, 2 * p:2 * p + 2, :]
                dve.tensor_tensor(x, T[p % 2][:, :].rearrange("p (k t) -> p k t", k=2), x, ALU.mult).then_inc(conv_x, 1)

            def conv_lo(p):
                k = slice(2 * p, 2 * p + 2)
                dve.wait_ge(xt_hi, XT["cout"] + 2 * p + 2)
                dve.tensor_tensor(xlo[:, k, :], convx[:, k, :], xhi[:, k, :].bitcast(F32), ALU.subtract)\
                    .then_inc(xt_lo, 2)

            split_at(U_CIN + 3)
            conv_evac(0)
            for g in (1, 2, 3):
                split_at(U_CIN + 2 * g + 2, U_CIN + 2 * g + 3)
                if g == 1:
                    dve.memset(uT[:, :, 0:2], 0.0).then_inc(pads_ok, 1)
                if g == 3:
                    conv_taps(0)
                conv_evac(g)
            split_at(U_CIN + 10)
            conv_taps(1)
            conv_gate(0)
            split_at(U_CIN + 11)
            conv_gate(1)
            conv_evac(4)
            split_at(U_COUT, U_COUT + 1)
            conv_taps(2)
            conv_lo(0)
            conv_lo(1)
            conv_evac(5)
            conv_taps(3)
            conv_gate(2)
            conv_gate(3)
            conv_lo(2)
            conv_lo(3)
            split_at(*range(U_COUT + 2, U_COUT + 5))
            ffn(2, "h5", "ffn2", n2(0, 4), lambda t: post_update(1, "y1", "ffn2", t), late_split=True)
            turned("kv", lambda k: G_KV + k, U_KV, lambda t: post_update(2, "y2", "kv", t))
            for g in range(4):
                split_at(*range(U_KV + 2 * g + (3 if g == 0 else 2), U_KV + 2 * g + 4))
                evac(EV_KV + g, U_KV + 2 * g + 1, kv_places[g][:, 1, :], PAIR[KV_PAIR[g]], "h6")
            heads_out(HT_KD, KT[:, 2:4, :])
            heads_out(HT_KD + 1, KT[:, 6:8, :])
            ffn(3, "h6", "ffn3", n2(1, 0))
            turned("q", lambda k: n2(1, 2) + k, U_Q, lambda t: post_update(3, "y3", "q", t))
            for g in range(2):
                split_at(*range(U_Q + 2 * g + (3 if g == 0 else 2), U_Q + 2 * g + 4))
                evac(EV_Q + g, U_Q + 2 * g + 1, Z[:, 1, 512 * g:512 * g + 512], PAIR[g], "h7")
            heads_out(HT_QD, QT[:, 2:4, :], scale=DIFF_DH ** -0.5)
            heads_out(HT_QD + 1, QT[:, 6:8, :], scale=DIFF_DH ** -0.5)

            def combine(i):
                p0, p1 = probs[2 * i % 4], probs[(2 * i + 1) % 4]
                l0, l1 = slice(4 * i, 4 * i + 2), slice(4 * i + 2, 4 * i + 4)
                dve.wait_ge(at_e, D_E + 4 * i + 4)
                link(dve.reciprocal(linv[:, l1], lsum[:, l1]))
                link(dve.scalar_tensor_tensor(out=linv[:, l0], in0=lsum[:, l0], scalar=lam4[:, 0:1], in1=linv[:, l1],
                                              op0=ALU.mult, op1=ALU.mult))
                for t, c0, c1 in ((0, 0, 128), (1, 128, 384)):
                    dve.scalar_tensor_tensor(out=p0[:, c0:c1], in0=p1[:, c0:c1],
                                             scalar=linv[:, 4 * i + t:4 * i + t + 1], in1=p0[:, c0:c1],
                                             op0=ALU.mult, op1=ALU.add).then_inc(at_a, 1)

            def o_sum(g, t):
                c = slice(8 * g + 4 * t, 8 * g + 4 * t + 4)
                dve.wait_ge(hn_sq, HN_D + 2 * g + t + 1)
                link(dve.tensor_reduce(HS[:, 4, c], osq[:, t, g * HALF:g * HALF + HALF].rearrange(
                    "p (h d) -> p h d", d=2 * DIFF_DH), AX.X, ALU.add))
                dve.wait_ge(eps_l, g + 1)
                dve.scalar_tensor_tensor(out=HV[:, 4, c], in0=HS[:, 4, c], scalar=SUB_M / (2 * DIFF_DH),
                                         in1=epsl[:, c], op0=ALU.mult, op1=ALU.add).then_inc(hn_sum, 1)

            def o_norm(g, t):
                c = slice(8 * g + 4 * t, 8 * g + 4 * t + 4)
                dve.wait_ge(hn_r, HN_D + 2 * g + t + 1)
                r = HR[:, 4, c].unsqueeze(2).to_broadcast([P, 4, 128])
                dve.tensor_tensor(nat[:, t, g * HALF:g * HALF + HALF].rearrange("p (h d) -> p h d", d=128),
                                  PAIR[g][t][:, :].rearrange("p (h d) -> p h d", d=128), r, ALU.mult).then_inc(at_o, 1)

            for i in range(DIFF_H + 1):
                if i < DIFF_H:
                    for m in (2 * i, 2 * i + 1):
                        dve.wait_ge(at_s, D_S + m + 1)
                        if m >= 4:
                            dve.wait_ge(at_e, D_E + 2 * (m - 3))
                        dve.scalar_tensor_tensor(out=scores[m % 4], in0=dist[:, :], scalar=slopes[i],
                                                 in1=B[4 + m % 2][:, 0:384], op0=ALU.mult, op1=ALU.add)\
                            .then_inc(at_m, 1)
                        dve.wait_ge(at_m, D_M + m + 1)
                        row_max(m, 0)
                if i:
                    combine(i - 1)
                if i == 5:
                    o_sum(0, 0)
                    o_sum(0, 1)
                if i == 6:
                    o_norm(0, 0)
                    o_norm(0, 1)
            o_sum(1, 0)
            o_sum(1, 1)
            o_norm(1, 0)
            o_norm(1, 1)
            turned("ao", lambda k: G_SUB, U_O)
            split_at(*range(U_O + 3, U_O + 5))
            ffn(4, "h8", "ffn4", n2(1, 4), lambda t: post_update(4, "y4", "ffn4", t), late_split=True)
            for t in range(TOKS):
                post_update(5, "y5", "out", t)

        @block.tensor
        def _(pe):
            def turn(name, t, j, src, waits):
                for w in waits(t, j // 2):
                    pe.wait_ge(*w)
                if t:
                    pe.wait_ge(xt_lo, XT[name] + 2 * j + 2)
                for k in (2 * j, 2 * j + 1):
                    ins = pe.transpose(TURN[j][:, (k % 2) * P:(k % 2) * P + P], src[:, t, k * P:k * P + P], ident[:, :])
                ins.then_inc(t_done, 1)

            def product(bank, s, c, k, t, first, last):
                x = slice(t * P, t * P + P)
                pe.matmul(bank[:, :], xlo[:, k, x], whi[s][:, c], start=first, stop=False)
                pe.matmul(bank[:, :], xhi[:, k, x], wlo[s][:, c], start=False, stop=False)
                return pe.matmul(bank[:, :], xhi[:, k, x], whi[s][:, c], start=False, stop=last)

            def columns(k):
                return slice(k % 4 * HALF, k % 4 * HALF + HALF)

            def k_unit(u, banks, k0):
                pe.wait_ge(w_lo, u + 1)
                for k in range(k0, k0 + 4):
                    for t in range(TOKS):
                        ins = product(banks[t], u % RING, columns(k), k, t, k == 0, k == KD - 1)
                ins.then_inc(w_used, 1)

            def group(u, banks):
                k_unit(u, banks, 0)
                k_unit(u + 1, banks, 4)

            def first_group(u, name, banks, src, waits, halves=False, tok0=None):
                for j in range(2 if halves else 4):
                    turn(name, 0, j, src, waits)
                for t in range(TOKS):
                    for k in range(KD):
                        if t == 0 and k % 4 == 0:
                            pe.wait_ge(w_lo, u + k // 4 + 1)
                        pe.wait_ge(xt_lo, XT[name] + t * KD + k + 1)
                        ins = product(banks[t], (u + k // 4) % RING, columns(k), k, t, k == 0, k == KD - 1)
                        if t and k % 4 == 3:
                            ins.then_inc(w_used, 1)
                        if tok0 and t == 0 and k == KD - 1:
                            ins.then_inc(tok0, 1)
                        if halves and t == 0 and k == 3:
                            turn(name, 0, 2, src, waits)
                            turn(name, 0, 3, src, waits)
                        if t == 0 and k in (5, 7):
                            turn(name, 1, k - 5, src, waits)
                            turn(name, 1, k - 4, src, waits)

            def last_group(u, banks):
                for t in range(TOKS):
                    for k in range(KD):
                        if t == 0 and k % 4 == 0:
                            pe.wait_ge(w_lo, u + k // 4 + 1)
                        ins = product(banks[t], (u + k // 4) % RING, columns(k), k, t, k == 0, k == KD - 1)
                        if t and k % 4 == 3:
                            ins.then_inc(w_used, 1)
                        if t == 0 and k in (0, KD - 1):
                            ins.then_inc(tok0_done, 1)

            def h_waits(reader):
                return lambda t, half: [(h_up, h_ready(reader, t, half))]

            def evacuated(e):
                pe.wait_ge(ev_a, e + 1)
                pe.wait_ge(ev_d, e + 1)

            def heads_turn(n, src):
                for b in range(2):
                    for c in range(2):
                        for t in range(TOKS):
                            col = (2 * b + c) * P
                            ins = pe.transpose(T[b][:, (2 * c + t) * P:(2 * c + t) * P + P], src[:, t, col:col + P],
                                               ident[:, :])
                    ins.then_inc(ht, 1)

            def t_free_heads(n):
                pe.wait_ge(ht_a, n + 1)
                pe.wait_ge(ht_d, n + 1)

            pe.wait_ge(in_id, 16)
            pe.wait_ge(in_mgain, 16)
            pe.transpose(T[0][:, 0:8], grow2[0:8, :], ident[0:8, 0:8]).then_inc(gain_T, 1)
            pe.wait_ge(gain_ok, 2)
            first_group(U_MEMKV, "mem", PAIR[0], nat, lambda t, half: [(in_mem[t], 16)])
            k_unit(U_MEMKV + 2, PAIR[1], 0)
            pe.wait_ge(in_gain, 14 * 16)
            pe.transpose(T[0][:, 0:G_ROWS1], grow1[0:G_ROWS1, :], ident[0:G_ROWS1, 0:G_ROWS1])
            pe.transpose(T[0][:, 128:128 + G_ROWS2], grow2[0:G_ROWS2, :], ident[0:G_ROWS2, 0:G_ROWS2])\
                .then_inc(gain_T, 1)
            k_unit(U_MEMKV + 3, PAIR[1], 4)
            pe.wait_ge(gain_ok, 4)
            evacuated(EV_MEMKV)
            first_group(U_IN, "x", PAIR[0], h, lambda t, half: [(in_x, 16)])
            evacuated(EV_MEMKV + 1)
            group(U_IN + 2, PAIR[1])
            pe.wait_ge(wf_lo_s, 1)
            for t in range(TOKS):
                x = slice(t * P, t * P + P)
                for k in range(KD):
                    o = T[0][:, 8 * t:8 * t + 8]
                    pe.matmul(o, xlo[:, k, x], wfhi[:, k, :], start=k == 0, stop=False)
                    pe.matmul(o, xhi[:, k, x], wflo[:, k, :], start=False, stop=False)
                    ins = pe.matmul(o, xhi[:, k, x], wfhi[:, k, :], start=False, stop=k == KD - 1)
            ins.then_inc(f_done, 1)
            k_unit(U_IN + 4, PAIR[2], 0)
            pe.wait_ge(f_out, 2)
            pe.wait_ge(hn_x, 2)
            heads_turn(HT_KM, nat)
            k_unit(U_IN + 5, PAIR[2], 4)
            t_free_heads(HT_KM)
            pe.wait_ge(hn_x, 4)
            heads_turn(HT_QF, Z[:, :, 0:512])
            evacuated(EV_IN)
            k_unit(U_IN + 6, PAIR[0], 0)
            t_free_heads(HT_QF)
            pe.wait_ge(hn_x, 6)
            heads_turn(HT_KF, Z[:, :, 512:1024])
            pe.wait_ge(f_log, 1)
            pe.wait_ge(in_const, 80)
            evacuated(EV_IN + 1)
            for t in range(TOKS):
                for j in range(t + 1):
                    pe.matmul(B[2][:, 8 * t:8 * t + 8], tri[:, j, t * P:t * P + P], fl[:, 0, 8 * j:8 * j + 8],
                              start=j == 0, stop=j == t)
            for j in range(TOKS):
                ins = pe.matmul(B[3][0:FOX_H, 0:S], fl[:, 0, 8 * j:8 * j + 8], tri[:, j, :], start=j == 0, stop=j == 1)
            ins.then_inc(c_done, 1)
            k_unit(U_IN + 7, PAIR[0], 4)
            t_free_heads(HT_KF)
            evacuated(EV_IN + 2)
            for b in range(2):
                for c in range(2):
                    for t in range(TOKS):
                        col = 1024 + (2 * b + c) * P
                        ins = pe.transpose(T[b][:, (2 * c + t) * P:(2 * c + t) * P + P], Z[:, t, col:col + P],
                                           ident[:, :])
                ins.then_inc(pt_done, 1)

            def causal_turn(i, src, done):
                for b in range(3):
                    ins = pe.transpose(T[i % 2][:, b * P:b * P + P], src[:, b * P:b * P + P], ident[:, :])
                ins.then_inc(done, 1)

            def causal_values(i, out0, out1, v):
                pe.matmul(out0, pT[i % 2][:, 0:P], v[:, 0, :], start=True, stop=True)
                pe.matmul(out1, pT[i % 2][:, P:2 * P], v[:, 0, :], start=True, stop=False)
                pe.matmul(out1, pT[i % 2][:, 2 * P:3 * P], v[:, 1, :], start=False, stop=True).then_inc(at_v, 1)

            def fox_scores(i):
                c, r = i // 2, slice(64 * (i % 2), 64 * (i % 2) + 64)
                if i >= 4:
                    pe.wait_ge(at_m, 2 * (i - 3))
                b = B[i % 4]
                for q, lo, width in ((0, 0, P), (1, P, S)):
                    pe.matmul(b[:, lo:lo + width], QT[r, c, q * P:q * P + P], KT[r, c, 0:width], start=True, stop=False)
                    ins = pe.matmul(b[:, lo:lo + width], sel[:, i, :], cT[:, 0:width], start=False, stop=True)
                ins.then_inc(at_s, 1)

            pe.wait_ge(c_out, 2)
            evacuated(EV_IN + 3)
            fox_scores(0)
            fox_scores(1)
            fox_scores(2)
            for i in range(FOX_H):
                pe.wait_ge(at_e, 2 * i + 2)
                if i < 2:
                    pe.wait_ge(pt_out, 2)
                else:
                    pe.wait_ge(at_c, i - 1)
                causal_turn(i, probs[i % 4], at_r)
                if i + 3 < FOX_H:
                    fox_scores(i + 3)
                pe.wait_ge(at_c, i + 1)
                d = slice(64 * i, 64 * i + 64)
                causal_values(i, B[4][:, d], B[5][:, d], Z[:, :, 1536 + 64 * i:1600 + 64 * i])
            pe.wait_ge(mixed_ok, 4)
            pe.wait_ge(in_small, 64)
            pe.wait_ge(at_m, 16)
            for g in range(4):
                for t in range(TOKS):
                    ins = pe.matmul(B[t][:, g * P:g * P + P], mixT[:, g, t * P:t * P + P], wpool[:, g, :],
                                    start=True, stop=True)
            ins.then_inc(py_done, 1)
            pe.wait_ge(at_o, 2)
            first_group(U_OUT, "mix", PAIR[0], nat, lambda t, half: [(py_out, 2)] if half else [(at_o, 2)])
            last_group(U_OUT + 2, PAIR[1])
            first_group(U_MQ, "mq", PAIR[0], h, h_waits("mq"), tok0=mq_tok0)
            pe.wait_ge(hn_x, 8)
            heads_turn(HT_QM, Z[:, :, 0:512])
            t_free_heads(HT_QM)

            def mem_scores(i):
                for t in range(TOKS):
                    ins = pe.matmul(B[i][:, t * S:t * S + S], QT[:, i, t * P:t * P + P], memKT[:, i, :],
                                    start=True, stop=True)
                ins.then_inc(at_s, 1)

            for i in range(3):
                mem_scores(i)
            for i in range(MEM_H):
                pe.wait_ge(at_e, M_E + 2 * i + 2)
                if i >= 2:
                    pe.wait_ge(at_c, M_R + i - 1)
                for t in range(TOKS):
                    for b in range(2):
                        c = (2 * t + b) * P
                        ins = pe.transpose(T[i % 2][:, c:c + P], mprobs[i][:, c:c + P], ident[:, :])
                ins.then_inc(at_r, 1)
                if i + 3 < MEM_H:
                    mem_scores(i + 3)
                pe.wait_ge(at_c, M_R + i + 1)
                for t in range(TOKS):
                    for b in range(2):
                        c = (2 * t + b) * P
                        ins = pe.matmul(B[4 + t][:, i * P:i * P + P], pT[i % 2][:, c:c + P],
                                        memV[:, b, i * P:i * P + P], start=b == 0, stop=b == 1)
                ins.then_inc(at_v, 1)
            for j in range(2):
                turn("mo", 0, j, nat, lambda t, half: [(at_o, 3)])
            for j in range(2):
                turn("mo", 1, j, nat, lambda t, half: [(at_o, 4)])
            for t in range(TOKS):
                for half in range(2):
                    for k in range(4):
                        if t == 0:
                            pe.wait_ge(w_lo, U_MO + half + 1)
                        pe.wait_ge(xt_lo, XT["mo"] + 4 * t + k + 1)
                        ins = product(PAIR[half][t], (U_MO + half) % RING, columns(k), k, t, k == 0, k == 3)
                    ins.then_inc(w_used if t else tok0_done, 1)

            def ffn(f, reader, waits):
                u0 = U_FFN[f]
                first_group(u0, reader, PAIR[0], h, waits)

                def up_unit(u, slot, k0):
                    pe.wait_ge(w_lo, u + 1)
                    for k in range(k0, k0 + 4):
                        for t in range(TOKS):
                            ins = product(GU[t], slot, columns(k), k, t, k == 0, k == KD - 1)
                    ins.then_inc(w_used, 1)

                def down(slot, t, half, first=False, last=False):
                    hi, lo = (last_hi, last_lo) if last else (ahi, alo)
                    for k in range(2):
                        c = slice(k * D + half * HALF, k * D + half * HALF + HALF)
                        x = slice((2 * k + t) * P, (2 * k + t) * P + P)
                        o = PAIR[half][t][:, :]
                        pe.matmul(o, lo[:, x], whi[slot][:, c], start=first and k == 0, stop=False)
                        pe.matmul(o, hi[:, x], wlo[slot][:, c], start=False, stop=False)
                        ins = pe.matmul(o, hi[:, x], whi[slot][:, c], start=False, stop=last and k == 1)
                    return ins

                def down_ready(u, j):
                    pe.wait_ge(w_lo, u + 1)
                    pe.wait_ge(act_lo, FJ * f + j + 1)

                def turn_act(j):
                    pe.wait_ge(act_ok, 2 * (FJ * f + j) + 2)
                    for k in range(2):
                        for t in range(TOKS):
                            ins = pe.transpose(T[0][:, (2 * k + t) * P:(2 * k + t) * P + P],
                                               actn[:, t, k * P:k * P + P], ident[:, :])
                    ins.then_inc(act_t, 1)

                v = u0 + 2

                def up(i, first):
                    if not first:
                        pe.wait_ge(act_ok, 2 * (FJ * f + i) + 2)
                    up_unit(v + 3 * i, v % RING, 0)
                    turn_act(i)
                    up_unit(v + 3 * i + 1, (v + 1) % RING, 4)

                def step(i, first):
                    up(i, first)
                    down_ready(v + 3 * i + 2, i)
                    for t in range(TOKS):
                        for half in range(2):
                            ins = down((v + 2) % RING, t, half, first)
                    ins.then_inc(w_used, 1)

                step(0, True)
                with pe.Fori(1, FJ - 2) as i:
                    step(i, False)
                up(FJ - 2, False)
                u, last = u0 + 31, u0 + 32
                down_ready(u, FJ - 2)
                down(u % RING, 0, 0)
                down(u % RING, 0, 1)
                turn_act(FJ - 1)
                down(u % RING, 1, 0)
                down(u % RING, 1, 1).then_inc(w_used, 1)
                down_ready(last, FJ - 1)
                down(last % RING, 0, 0, last=True).then_inc(tok0_done, 1)
                down(last % RING, 0, 1, last=True).then_inc(tok0_done, 1)
                down(last % RING, 1, 0, last=True)
                down(last % RING, 1, 1, last=True).then_inc(w_used, 1)

            ffn(0, "ffn0", h_waits("ffn0"))
            ffn(1, "ffn1", h_waits("ffn1"))
            first_group(U_CIN, "cin", PAIR[0], h, h_waits("cin"))
            def conv_feed(p, is_b):
                if not is_b:
                    pe.wait_ge(conv_p, p // 2 + 1)
                    src = Z[:, :, 512:1024] if p < 2 else Z[:, :, 1536:2048]
                    if p >= 2:
                        pe.wait_ge(conv_x, p - 1)
                else:
                    evacuated(EV_CIN + (0 if p < 2 else 5))
                    src = Z[:, :, 0:512] if p < 2 else nat[:, :, 512:1024]
                    pe.wait_ge(conv_u, p + 1)
                for k in range(2):
                    c = (2 * p + k) % 4 * P
                    for t in range(TOKS):
                        ins = pe.transpose(T[p % 2][:, (2 * k + t) * P:(2 * k + t) * P + P], src[:, t, c:c + P],
                                           ident[:, :])
                ins.then_inc(conv_t, 1)

            group(U_CIN + 2, PAIR[1])
            group(U_CIN + 4, PAIR[2])
            evacuated(EV_CIN)
            k_unit(U_CIN + 6, PAIR[0], 0)
            conv_feed(0, False)
            k_unit(U_CIN + 7, PAIR[0], 4)
            conv_feed(1, False)
            conv_feed(0, True)
            evacuated(EV_CIN + 1)
            k_unit(U_CIN + 8, PAIR[1], 0)
            conv_feed(1, True)
            k_unit(U_CIN + 9, PAIR[1], 4)
            evacuated(EV_CIN + 2)
            k_unit(U_CIN + 10, PAIR[2], 0)
            conv_feed(2, False)
            conv_feed(3, False)
            k_unit(U_CIN + 11, PAIR[2], 4)
            evacuated(EV_CIN + 3)
            for k in range(KD):
                if k % 4 == 0:
                    pe.wait_ge(w_lo, U_COUT + k // 4 + 1)
                if k % 2 == 0:
                    pe.wait_ge(xt_lo, XT["cout"] + k + 2)
                for t in range(TOKS):
                    ins = product(PAIR[0][t], (U_COUT + k // 4) % RING, columns(k), k, t, k == 0, k == KD - 1)
                if k % 4 == 3:
                    ins.then_inc(w_used, 1)
                if k < 2:
                    conv_feed(k + 2, True)
            last_group(U_COUT + 2, PAIR[1])
            ffn(2, "ffn2", h_waits("ffn2"))
            first_group(U_KV, "kv", PAIR[KV_PAIR[0]], h, h_waits("kv"))
            for g in range(1, 4):
                if g == 3:
                    evacuated(EV_KV + 1)
                group(U_KV + 2 * g, PAIR[KV_PAIR[g]])
            heads_turn(HT_KD, Z[:, :, 0:512])
            t_free_heads(HT_KD)
            heads_turn(HT_KD + 1, Z[:, :, 512:1024])
            t_free_heads(HT_KD + 1)
            evacuated(EV_KV + 2)
            ffn(3, "ffn3", lambda t, half: [])
            first_group(U_Q, "q", PAIR[0], h, h_waits("q"))
            group(U_Q + 2, PAIR[1])
            evacuated(EV_Q)
            heads_turn(HT_QD, Z[:, :, 0:512])
            t_free_heads(HT_QD)
            evacuated(EV_Q + 1)
            heads_turn(HT_QD + 1, Z[:, :, 512:1024])
            t_free_heads(HT_QD + 1)

            def diff_scores(m):
                c, r = m // 2, slice(64 * (m % 2), 64 * (m % 2) + 64)
                if m >= 2:
                    pe.wait_ge(at_m, D_M + m - 1)
                b = B[4 + m % 2]
                pe.matmul(b[:, 0:P], QT[r, c, 0:P], KT[r, c, 0:P], start=True, stop=True)
                pe.matmul(b[:, P:3 * P], QT[r, c, P:2 * P], KT[r, c, 0:S], start=True, stop=True).then_inc(at_s, 1)

            diff_scores(0)
            diff_scores(1)
            diff_scores(2)
            diff_scores(3)
            for i in range(DIFF_H):
                if i + 2 < DIFF_H:
                    diff_scores(2 * i + 4)
                pe.wait_ge(at_a, 2 * i + 2)
                if i >= 2:
                    pe.wait_ge(at_c, D_R + i - 1)
                causal_turn(i, probs[2 * i % 4], at_r)
                if i + 2 < DIFF_H:
                    diff_scores(2 * i + 5)
                pe.wait_ge(at_c, D_R + i + 1)
                d = slice((i % 4) * P, (i % 4) * P + P)
                causal_values(i, PAIR[i // 4][0][:, d], PAIR[i // 4][1][:, d], VD[:, :, i * P:i * P + P])
            first_group(U_O, "ao", PAIR[0], nat, lambda t, half: [(at_o, 4 + 2 * (half + 1) if half == 0 else 7 + t)],
                        halves=True)
            last_group(U_O + 2, PAIR[1])
            ffn(4, "ffn4", h_waits("ffn4"))


_INS = ["x", "mem", "g_mix", "w_in", "b_forget", "g_q_fox", "g_k_fox", "w_pool", "pool_scale", "w_out", "g_mem_q",
        "g_mem_kv", "w_mem_q", "w_mem_kv", "g_q_mem", "g_k_mem", "w_mem_out", "g_ffn", "w_gate_up", "w_down",
        "ffn_w_gu_2", "ffn_w_down_2", "norm_g_2", "conv_w_in_2", "conv_k_2", "conv_w_out_2", "kv_norm_g_2",
        "w_kv_2", "attn_w_q_2", "attn_lambda_2", "attn_subln_g_2", "attn_w_o_2"]


def constants():
    p, t = np.arange(P), np.arange(S)
    ones = np.float32(1.0)
    tri = np.stack([(j * P + p[:, None] <= t[None, :]) for j in range(TOKS)], axis=1).astype(np.float32)
    q = np.concatenate([np.zeros(P), np.full(S, P)])
    k = np.concatenate([np.arange(P), np.arange(S)])
    gap = (q[None, :] + p[:, None] - k[None, :]).astype(np.float32)
    sel = np.zeros((FOX_H, FOX_H, P), np.float32)
    for i in range(FOX_H):
        sel[i, i, :] = -ones
    cnt = np.stack([1.0 / np.minimum(np.arange(16) + 1, w) for w in WINDOWS]).astype(np.float32)
    return {
        "c_ident": np.eye(P, dtype=np.float32),
        "c_tri": tri,
        "c_mask": np.where(gap >= 0, 0.0, NEG).astype(np.float32),
        "c_dist": np.where(gap >= 0, -gap, NEG).astype(np.float32),
        "c_sel": sel,
        "c_cnt": np.ascontiguousarray(np.broadcast_to(cnt, (P, 4, 16))),
    }


def kernel(**inputs):
    import concourse.bacc as bacc
    from concourse.bass_utils import run_bass_kernel_spmd

    nc = bacc.Bacc("TRN2", target_bir_lowering=False, num_devices=1)
    arrays, args = {}, {}
    for name, value in [(n, inputs[n]) for n in _INS] + list(constants().items()):
        v = np.ascontiguousarray(value)
        arrays[f"in_{name}"] = v
        args[name] = nc.dram_tensor(f"in_{name}", v.shape, mybir.dt.from_np(v.dtype), kind="ExternalInput").ap()
    out = nc.dram_tensor("out_0", (1, S, D), F32, kind="ExternalOutput").ap()
    build(nc, args, out)
    r = run_bass_kernel_spmd(nc, [arrays], core_ids=[0])
    return r.results[0]["out_0"]
```

```python
import math
from contextlib import ExitStack

import numpy as np
import concourse.bass as bass
from concourse import mybir

F32 = mybir.dt.float32
F32R = mybir.dt.float32r
ALU = mybir.AluOpType
ACT = mybir.ActivationFunctionType
AX = mybir.AxisListType

P = 128
S = 256
TOKS = S // P
D = 1024
KD = D // P
HALF = 512
FOX_H, FOX_DH = 8, 64
MEM_H, MEM_DH = 4, 128
DIFF_H, DIFF_DH = 8, 64
FF = 2816
FJ = FF // 256
WINDOWS = (2, 4, 8, 16)
EPS = 1e-6
NEG = -1.0e37
RING = 3
UNIT = 2048

U_MEMKV, U_IN, U_OUT, U_MQ, U_MO = 0, 4, 12, 16, 18
U_FFN = (20, 53, 102, 143, 184)
U_CIN, U_COUT, U_KV, U_Q, U_O = 86, 98, 135, 176, 180
UNITS = 217

XT_ORDER = [("mem", 8), ("x", 8), ("mix", 8), ("mq", 8), ("mo", 4), ("ffn0", 8), ("ffn1", 8), ("cin", 8),
            ("cout", 8), ("ffn2", 8), ("kv", 8), ("ffn3", 8), ("q", 8), ("ao", 8), ("ffn4", 8)]
XT = {}
TD = {}
_x = _t = 0
for _n, _c in XT_ORDER:
    XT[_n], TD[_n] = _x, _t
    if _n == "cout":
        _x += _c
    else:
        _x += TOKS * _c
        _t += TOKS * _c // 2
CHUNKS = dict(XT_ORDER)

ST = {n: i for i, n in enumerate(["mem", "h0", "h1", "h2", "h3", "y0", "h4", "y1", "h5", "y2", "h6", "y3",
                                  "h7", "y4", "h8", "y5"])}
MEAN = {n: 4.0 if n in ("y0", "y2", "y3", "y5") else 1.0 for n in ST}
H_UP = {n: i for i, n in enumerate(["mq", "ffn0", "ffn1", "cin", "ffn2", "kv", "q", "ffn4", "out"])}
H_UP["ffn3"] = H_UP["kv"]


def h_ready(reader, t, half):
    return 4 * H_UP[reader] + 2 * t + half + 1


G_N2, G_CONV, G_ROWS1 = 0, 96, 120
G_MEMKV, G_MIX, G_MEMQ, G_FFN, G_KV, G_POOL, G_SUB, G_QF, G_KF, G_QM, G_KM = (
    120, 128, 136, 144, 152, 160, 164, 165, 166, 167, 168)
G_ROWS2 = 49
G_ONE = 169


def n2(layer, i):
    return G_N2 + (layer * 6 + i) * KD


def build(nc, a, out):
    lambda_init = 0.8 - 0.6 * math.exp(-0.3)
    SUB_M = 1.0 / (1.0 - lambda_init) ** 2
    slopes = [2.0 ** (-8.0 * (h + 1) / DIFF_H) for h in range(DIFF_H)]

    ctx = ExitStack()
    with ctx:
        def sb(name, shape, dt=F32):
            return ctx.enter_context(nc.sbuf_tensor(name, shape, dt))

        def sem(name):
            return ctx.enter_context(nc.semaphore(name))

        raw = [sb(f"w_raw{s}", [P, UNIT]) for s in range(RING)]
        whi = [sb(f"w_hi{s}", [P, UNIT], F32R) for s in range(RING)]
        wlo = [sb(f"w_lo{s}", [P, UNIT], F32R) for s in range(RING)]
        xhi = sb("xt_hi", [P, KD, S], F32R)
        xlo = sb("xt_lo", [P, KD, S], F32R)
        h = sb("h", [P, TOKS, D])
        nat = sb("nat", [P, TOKS, D])
        Z = sb("Z", [P, TOKS, 4 * HALF])
        QT = sb("QT", [P, 8, S])
        KT = sb("KT", [P, 8, S])
        VD = sb("VD", [P, TOKS, D])
        memKT = sb("memKT", [P, MEM_H, S])
        memV = sb("memV", [P, TOKS, HALF])
        ahi = sb("act_hi", [P, 2 * S], F32R)
        alo = sb("act_lo", [P, 2 * S], F32R)
        last_hi = xhi[:, KD - 2:KD, :].rearrange("p k t -> p (k t)")
        last_lo = xlo[:, KD - 2:KD, :].rearrange("p k t -> p (k t)")
        work = sb("work", [P, 4096])
        SQ = sb("SQ", [P, 2 * HALF])
        junk = sb("junk", [P, HALF])
        tmp = sb("tmp", [P, TOKS, HALF])
        gpost = sb("gpost", [P, 2, D])
        gains = sb("gains", [P, 176])
        grow1 = sb("grow1", [P, P])
        grow2 = sb("grow2", [P, P])
        ident = sb("ident", [P, P])
        tri = sb("tri", [P, TOKS, S])
        foxmask = sb("foxmask", [P, 384])
        dist = sb("dist", [P, 384])
        distr = sb("dist_rounded", [P, 384], F32R)
        CK = 64 + FOX_H
        sel = tmp[0:CK, :, :].rearrange("p t (h c) -> p (t h) c", c=P)
        selr = [t[0:CK, :].rearrange("p (h c) -> p h c", c=P) for t in (ahi, alo)]
        slopeI = [t[:, :].rearrange("p (h c) -> p h c", c=P) for t in (ahi, alo)]
        cnt16 = sb("cnt16", [P, 4, 16])
        wpool = sb("wpool", [P, 4, P])
        wf = sb("wf", [P, KD, FOX_H])
        wfhi = sb("wf_hi", [P, KD, FOX_H], F32R)
        wflo = sb("wf_lo", [P, KD, FOX_H], F32R)
        bf = sb("b_forget", [P, FOX_H])
        lamp = sb("lamp", [P, 4, DIFF_DH])
        lam4 = sb("lam4", [P, 4])
        SS = sb("row_squares", [P, len(ST), TOKS, 2])
        SV = sb("row_var", [P, len(ST), TOKS])
        RS = sb("row_rstd", [P, len(ST), TOKS])
        HS = sb("head_squares", [P, 5, 16])
        HV = sb("head_var", [P, 5, 16])
        HR = sb("head_rstd", [P, 5, 16])
        mhalf = sb("minus_half", [P, 16])
        fl = sb("forget", [P, 4, 16])
        cn = sb("cum_nat", [P, TOKS, FOX_H])
        fT = sb("forget_T", [FOX_H, S])
        logf = sb("log_f", [P, TOKS, CK])
        cT = sb("cum_T", [CK, S], F32R)
        nmax = sb("neg_max", [P, 32])
        lsum = sb("exp_sum", [P, 32])
        epsl = sb("eps_sum2", [P, 16])
        linv = sb("exp_inv", [P, 32])

        scores = [work[:, 384 * i:384 * i + 384] for i in range(4)]
        probs = [work[:, 1536 + 384 * i:1920 + 384 * i] for i in range(4)]
        pT = [work[:, 3072 + 512 * i:3584 + 512 * i] for i in range(2)]
        gate = work[:, 0:512].rearrange("p (t c) -> p t c", t=2)
        actn = work[:, 512:1024].rearrange("p (t c) -> p t c", t=2)
        uT = work[:, 1024:1024 + 4 * (S + 2)].rearrange("p (k t) -> p k t", k=4)
        convx = QT
        mprobs = [work[:, 512 * i:512 * i + 512] for i in range(4)]
        PAD = 8
        poolT = VD[:, :, :].rearrange("p t c -> p (t c)")[:, 0:4 * (PAD + S)].rearrange("p (g t) -> p g t", g=4)
        kt_hi = KT[:, 4:8, :].rearrange("p c t -> p (c t)")
        win = [kt_hi[:, (PAD + S) * i:(PAD + S) * (i + 1)] for i in range(2)]
        wmean = kt_hi[:, 2 * (PAD + S):2 * (PAD + S) + S]
        mixT = QT[:, 4:8, :]

        osq = Z[:, :, 2 * HALF:4 * HALF]
        conv_places = [Z[:, :, 0:512], Z[:, :, 512:1024], Z[:, :, 1024:1536], Z[:, :, 1536:2048],
                       nat[:, :, 0:512], nat[:, :, 512:1024]]
        KV_PAIR = (0, 1, 2, 1)
        kv_places = [Z[:, :, 0:512], Z[:, :, 512:1024], VD[:, :, 0:512], VD[:, :, 512:1024]]

        B = [ctx.enter_context(nc.psum_tensor(f"B{i}", [P, HALF], F32)) for i in range(6)]
        T = [ctx.enter_context(nc.psum_tensor(f"T{i}", [P, HALF], F32)) for i in range(2)]
        PAIR = [(B[0], B[1]), (B[2], B[3]), (B[4], B[5])]
        TURN = [T[0], T[1], B[4], B[5]]
        GU = PAIR[2]

        w_loaded = [sem(f"w_loaded{s}") for s in range(RING)]
        w_hi, w_lo, w_used = sem("w_hi_written"), sem("w_lo_written"), sem("w_unit_used")
        in_mem = [sem(f"mem_tok{t}_in") for t in range(TOKS)]
        in_x, in_id, in_small, in_const = sem("x_in"), sem("ident_in"), sem("small_in"), sem("const_in")
        in_gain, in_mgain = sem("gain_rows_in"), sem("memory_gain_row_in")
        gain_T, gain_ok = sem("gains_turned"), sem("gains_ready")
        post_in = [sem(f"post_gain{i}_in") for i in range(2)]
        t_done, xt_hi, xt_lo = sem("chunk_turned"), sem("xt_hi_written"), sem("xt_lo_written")
        ssq, rstd = sem("row_squares_summed"), sem("row_rstd_ready")
        h_up = sem("h_part_updated")
        tok0_done = sem("sum_tok0_half_done")
        mq_tok0 = sem("memory_queries_tok0_done")
        ev_a, ev_d = sem("group_evacuated_tok0"), sem("group_evacuated_tok1")
        hn_sq, hn_sum, hn_r, hn_x = sem("head_squared"), sem("head_summed"), sem("head_rstd"), sem("head_normed")
        ht, ht_a, ht_d = sem("heads_turned"), sem("heads_T_bank0_out"), sem("heads_T_bank1_out")
        wf_hi_s, wf_lo_s = sem("wf_hi_written"), sem("wf_lo_written")
        f_done, f_raw, f_out = sem("f_product"), sem("f_product_out"), sem("f_logit_out")
        f_act, f_log = sem("f_exp_ln"), sem("f_log_ready")
        c_done, c_out, c_hi = sem("cumsum_done"), sem("cumsum_out"), sem("cumsum_hi_written")
        logf_0, sel_ok = sem("log_f_zeroed"), sem("selectors_ready")
        pt_done, pt_out = sem("pool_turned"), sem("pool_T_out")
        mixed_ok, py_done, py_out = sem("pool_mixed"), sem("pool_product"), sem("pool_out")
        at_s, at_m, at_x, at_e, at_r, at_c, at_v = (sem("scores_done"), sem("scores_masked"), sem("row_max_ready"),
                                                    sem("exp_done"), sem("probs_turned"), sem("probs_T_out"),
                                                    sem("values_done"))
        at_o, at_a = sem("attention_out"), sem("diff_probs_ready")
        pads_ok = sem("pool_pads_zero")
        alibi_ok = sem("alibi_ready")
        eps_l = sem("eps_sum2_ready")
        lam_ok = sem("lambda_ready")
        gate_ok, act_ok, act_t, act_hi, act_lo = (sem("gate_ready"), sem("act_ready"), sem("act_turned"),
                                                  sem("act_hi_written"), sem("act_lo_written"))
        conv_p, conv_t, conv_u, conv_c, conv_x = (sem("conv_product_ready"), sem("conv_turned"), sem("conv_u_out"),
                                                  sem("conv_taps_summed"), sem("conv_x_ready"))
        dve_step, pool_step = sem("dve_step"), sem("pool_step")
        out_done = sem("out_written")

        block = ctx.enter_context(nc.Block())

        M_S, M_X, M_E, M_R = FOX_H, 2 * FOX_H, 2 * FOX_H, FOX_H
        D_S, D_X, D_E, D_R = M_S + MEM_H, M_X + MEM_H, M_E + 2 * MEM_H, M_R + MEM_H
        HT_KM, HT_QF, HT_KF, HT_QM, HT_KD, HT_QD = 0, 1, 2, 3, 4, 6
        FEED_U, FEED_B = (1, 2, 5, 6), (3, 4, 7, 8)
        EV_MEMKV, EV_IN, EV_CIN, EV_KV, EV_Q = 0, 2, 6, 12, 16
        HN_D = 5

        @block.sync
        def _(sp):
            def load(u, slot, parts):
                if not (isinstance(u, int) and u < RING):
                    sp.wait_ge(w_lo, u - RING + 1)
                for dst, src in parts:
                    sp.dma_start(dst, src).then_inc(w_loaded[slot], 16)

            def k_unit(u, w, k0, col):
                v = w.rearrange("(k p) f -> p k f", p=P)
                r = raw[u % RING][:, :].rearrange("p (k c) -> p k c", k=4)
                load(u, u % RING, [(r[:, i:i + 2, :], v[:, k0 + i:k0 + i + 2, col:col + HALF]) for i in (0, 2)])

            def ffn(u0, w_gu, w_dn):
                gu = w_gu.rearrange("(k p) f -> p k f", p=P)

                def up(j, u, slot, k0):
                    r = raw[slot][:, :].rearrange("p (k c) -> p k c", k=4)
                    load(u, slot, [(r[:, :, 0:256], gu[:, k0:k0 + 4, bass.ds(j * 256, 256)]),
                                   (r[:, :, 256:512], gu[:, k0:k0 + 4, bass.ds(j * 256 + FF, 256)])])

                def down(j, u, slot):
                    rows = w_dn[bass.ds(j * 256, 256), :].rearrange("(k p) f -> p k f", p=P)
                    load(u, slot, [(raw[slot][:, D * k:D * k + D], rows[:, k, :]) for k in range(2)])

                up(0, u0, u0 % RING, 0)
                up(0, u0 + 1, (u0 + 1) % RING, 4)

                def step(i):
                    up(i + 1, u0 + 2 + 3 * i, (u0 + 2) % RING, 0)
                    up(i + 1, u0 + 3 + 3 * i, (u0 + 3) % RING, 4)
                    down(i, u0 + 4 + 3 * i, (u0 + 4) % RING)

                with sp.Fori(0, FJ - 2) as i:
                    step(i)
                step(FJ - 2)
                down(FJ - 1, u0 + 32, (u0 + 32) % RING)

            def k_groups(u0, w, cols):
                for g, col in enumerate(cols):
                    k_unit(u0 + 2 * g, w, 0, col)
                    k_unit(u0 + 2 * g + 1, w, 4, col)

            k_groups(U_MEMKV, a["w_mem_kv"][0], (0, 512))
            k_groups(U_IN, a["w_in"][0], (0, 512, 1536, 1024))
            k_groups(U_OUT, a["w_out"][0], (0, 512))
            k_groups(U_MQ, a["w_mem_q"][0], (0,))
            k_unit(U_MO, a["w_mem_out"][0], 0, 0)
            k_unit(U_MO + 1, a["w_mem_out"][0], 0, 512)
            ffn(U_FFN[0], a["w_gate_up"][0], a["w_down"][0])
            ffn(U_FFN[1], a["ffn_w_gu_2"][0, 0], a["ffn_w_down_2"][0, 0])
            k_groups(U_CIN, a["conv_w_in_2"][0], (0, 1024, 2048, 1536, 2560, 512))
            k_groups(U_COUT, a["conv_w_out_2"][0], (0, 512))
            ffn(U_FFN[2], a["ffn_w_gu_2"][0, 1], a["ffn_w_down_2"][0, 1])
            k_groups(U_KV, a["w_kv_2"], (0, 512, 1024, 1536))
            ffn(U_FFN[3], a["ffn_w_gu_2"][1, 0], a["ffn_w_down_2"][1, 0])
            k_groups(U_Q, a["attn_w_q_2"][0], (0, 512))
            k_groups(U_O, a["attn_w_o_2"][0], (0, 512))
            ffn(U_FFN[4], a["ffn_w_gu_2"][1, 1], a["ffn_w_down_2"][1, 1])
            for t in range(TOKS):
                for half in range(2):
                    sp.wait_ge(h_up, h_ready("out", t, half))
                    sp.dma_start(out[0, t * P:t * P + P, half * HALF:half * HALF + HALF],
                                 h[:, t, half * HALF:half * HALF + HALF]).then_inc(out_done, 16)
            sp.wait_ge(out_done, 64)

        @block.gpsimd
        def _(pool):
            steps = [0]

            def link(ins):
                steps[0] += 1
                ins.then_inc(pool_step, 1)
                pool.wait_ge(pool_step, steps[0])

            for o, n in ((G_MIX, "g_mix"), (G_MEMQ, "g_mem_q"), (G_FFN, "g_ffn")):
                pool.dma_start(grow2[o - G_ROWS1:o - G_ROWS1 + 8, :],
                               a[n][0].rearrange("(k c) -> k c", c=P)).then_inc(in_gain, 16)
            pool.dma_start(grow2[32:40, :], a["kv_norm_g_2"].rearrange("(k c) -> k c", c=P)).then_inc(in_gain, 16)
            pool.dma_start(grow2[40:44, :], a["pool_scale"][0].rearrange("(k c) -> k c", c=P)).then_inc(in_gain, 16)
            pool.dma_start(grow2[44:45, :], a["attn_subln_g_2"]).then_inc(in_gain, 16)
            for r, n in ((45, "g_q_fox"), (46, "g_k_fox")):
                for c in range(2):
                    pool.dma_start(grow2[r:r + 1, 64 * c:64 * c + 64], a[n]).then_inc(in_gain, 16)
            pool.dma_start(grow2[47:48, :], a["g_q_mem"]).then_inc(in_gain, 16)
            pool.dma_start(grow2[48:49, :], a["g_k_mem"]).then_inc(in_gain, 16)
            pool.dma_start(grow1[0:96, :], a["norm_g_2"].rearrange("l i (k c) -> (l i k) c", c=P)).then_inc(in_gain, 16)
            pool.dma_start(grow1[96:120, :], a["conv_k_2"].rearrange("l w (k c) -> (l w k) c", c=P))\
                .then_inc(in_gain, 16)
            pool.memset(logf[:, :, :], 0.0).then_inc(logf_0, 1)
            pool.memset(mhalf[:, :], -0.5).then_inc(pool_step, 1)
            steps[0] += 1
            pool.wait_ge(pool_step, steps[0])
            with nc.allow_non_contiguous_dma(reason="8 columns of w_in"):
                pool.dma_start(wf[:, :, :], a["w_in"][0].rearrange("(k p) f -> p k f", p=P)[:, :, 2048:2056])\
                    .then_inc(in_small, 16)
            pool.dma_start(bf[:, :], a["b_forget"][0].partition_broadcast(P)).then_inc(in_small, 16)
            pool.dma_start(wpool[:, :, :], a["w_pool"][0].rearrange("g c d -> c g d")).then_inc(in_small, 16)
            pool.dma_start(lamp[:, :, :], a["attn_lambda_2"][0].partition_broadcast(P)).then_inc(in_small, 16)
            for dst, name in ((tri, "c_tri"), (foxmask, "c_mask"), (dist, "c_dist"), (sel, "c_sel"), (cnt16, "c_cnt")):
                full = (slice(None),) * len(dst.shape)
                pool.dma_start(dst[full], a[name][full]).then_inc(in_const, 16)

            def post_gain(b, layer, i):
                if b >= 2:
                    pool.wait_ge(h_up, 4 * (3 + b - 2) + 4)
                pool.dma_start(gpost[:, b % 2, :], a["norm_g_2"][layer, i].partition_broadcast(P))\
                    .then_inc(post_in[b % 2], 16)

            def windows():
                pool.wait_ge(pt_out, 2)
                pool.wait_ge(in_const, 80)
                for g, w in enumerate(WINDOWS):
                    if g == 0:
                        pool.wait_ge(pads_ok, 3)
                    src = poolT[:, g, :]
                    for level in range(g + 1):
                        d = 1 << level
                        dst = win[level % 2]
                        link(pool.tensor_tensor(dst[:, PAD:PAD + S], src[:, PAD:PAD + S], src[:, PAD - d:PAD + S - d],
                                                ALU.add))
                        src = dst
                    link(pool.tensor_scalar(wmean, src[:, PAD:PAD + S], 1.0 / w, 0.0, ALU.mult, ALU.add))
                    link(pool.tensor_tensor(wmean[:, 0:16], src[:, PAD:PAD + 16], cnt16[:, g, :], ALU.mult))
                    pool.tensor_tensor(mixT[:, g, :], wmean, poolT[:, g, PAD:PAD + S], ALU.subtract)\
                        .then_inc(mixed_ok, 1)
                    pool.wait_ge(mixed_ok, g + 1)

            def rsqrt(dst, var, src, scale, eps, done):
                link(pool.tensor_scalar(var, src, scale, eps, ALU.mult, ALU.add))
                pool.tensor_tensor(dst, var, mhalf[:, 0:dst.shape[1]], ALU.pow).then_inc(done, 1)

            def row_stat(name):
                s = ST[name]
                for t in range(TOKS):
                    pool.wait_ge(ssq, 4 * s + 2 * t + 2)
                    v = SV[:, s, t:t + 1]
                    link(pool.tensor_scalar(v, SS[:, s, t, 0:1], SS[:, s, t, 1:2], MEAN[name] * EPS, ALU.add, ALU.add))
                    pool.tensor_tensor(RS[:, s, t:t + 1], v, mhalf[:, 0:1], ALU.pow).then_inc(rstd, 1)

            def head_stat(n, count, dh, m=1.0):
                pool.wait_ge(hn_sum, n + 1)
                rsqrt(HR[:, n, 0:count], HV[:, n, 0:count], HS[:, n, 0:count], m / dh, m * EPS, hn_r)

            post_gain(0, 0, 1)
            post_gain(1, 0, 3)
            row_stat("mem")
            head_stat(0, TOKS * MEM_H, MEM_DH)
            row_stat("h0")
            head_stat(1, TOKS * FOX_H, FOX_DH)
            head_stat(2, TOKS * FOX_H, FOX_DH)
            pool.wait_ge(in_const, 80)
            for g in range(2):
                pool.tensor_copy(selr[g], sel[:, 4 * g:4 * g + 4, :]).then_inc(sel_ok, 1)
            windows()
            row_stat("h1")
            for t in range(TOKS):
                c = slice(t * MEM_H, t * MEM_H + MEM_H)
                pool.wait_ge(hn_sum, 3 + t + 1)
                link(pool.tensor_scalar(HV[:, 3, c], HS[:, 3, c], 1.0 / MEM_DH, EPS, ALU.mult, ALU.add))
                link(pool.tensor_tensor(HV[:, 3, c], HV[:, 3, c], mhalf[:, 0:MEM_H], ALU.pow))
                pool.tensor_tensor(HR[:, 3, c], HV[:, 3, c], RS[:, ST["h1"], t:t + 1].to_broadcast([P, MEM_H]),
                                   ALU.mult).then_inc(hn_r, 1)
            row_stat("h2")
            row_stat("h3")
            row_stat("y0")
            row_stat("h4")
            for n, g in enumerate((2, 4)):
                pool.wait_ge(ev_a, EV_CIN + g + 1)
                pool.wait_ge(ev_d, EV_CIN + g + 1)
                pool.tensor_tensor(conv_places[g - 1], conv_places[g - 1], conv_places[g], ALU.mult).then_inc(conv_p, 1)
            row_stat("y1")
            post_gain(2, 0, 5)
            row_stat("h5")
            row_stat("y2")
            post_gain(3, 1, 1)
            pool.tensor_copy(distr[:, :], dist[:, :]).then_inc(alibi_ok, 1)
            row_stat("h6")
            pool.wait_ge(w_used, U_FFN[3] + 32)
            for i in range(DIFF_H):
                pool.tensor_scalar(slopeI[i // 4][:, i % 4, :], ident[:, :], slopes[i], 0.0, ALU.mult, ALU.add)\
                    .then_inc(alibi_ok, 1)
            row_stat("y3")
            post_gain(4, 1, 3)
            row_stat("h7")
            for g in range(2):
                c = slice(8 * g, 8 * g + 8)
                l0 = lsum[:, 16 * g:16 * g + 16].rearrange("p (h c t) -> p c t h", c=2, t=2)[:, 0]
                pool.wait_ge(at_e, D_E + 16 * (g + 1))
                e = epsl[:, c].rearrange("p (t h) -> p t h", t=2)
                link(pool.tensor_tensor(e, l0, l0, ALU.mult))
                pool.tensor_scalar(epsl[:, c], epsl[:, c], SUB_M * EPS, 0.0, ALU.mult, ALU.add).then_inc(eps_l, 1)
                for t in range(TOKS):
                    n = 2 * g + t
                    pool.wait_ge(hn_sum, HN_D + n + 1)
                    pool.tensor_tensor(HR[:, 4, 4 * n:4 * n + 4], HV[:, 4, 4 * n:4 * n + 4], mhalf[:, 0:4], ALU.pow)\
                        .then_inc(hn_r, 1)
            row_stat("y4")
            post_gain(5, 1, 5)
            row_stat("h8")
            row_stat("y5")

        @block.scalar
        def _(act):
            act.dma_start(ident[:, :], a["c_ident"]).then_inc(in_id, 16)
            act.dma_start(grow2[0:8, :], a["g_mem_kv"][0].rearrange("(k c) -> k c", c=P)).then_inc(in_mgain, 16)
            for t in range(TOKS):
                act.dma_start(nat[:, t, :], a["mem"][0, t * P:t * P + P, :]).then_inc(in_mem[t], 16)

            def split(u, slot, n):
                act.wait_ge(w_loaded[slot], 32 * (n + 1))
                if not (isinstance(u, int) and u < RING):
                    act.wait_ge(w_used, u - RING + 1)
                act.activation(whi[slot][:, :], raw[slot][:, :], ACT.Copy).then_inc(w_hi, 1)

            def split_at(*units):
                for u in units:
                    if u < UNITS:
                        split(u, u % RING, u // RING)

            def turned_hi(name, gain_cols, t, k0=0, k1=KD):
                for k in range(k0, min(k1, CHUNKS[name])):
                    if k % 2 == 0:
                        act.wait_ge(t_done, TD[name] + (t * CHUNKS[name] + k) // 2 + 1)
                    g = gain_cols(k)
                    act.activation(xhi[:, k, t * P:t * P + P], TURN[k // 2][:, (k % 2) * P:(k % 2) * P + P], ACT.Copy,
                                   scale=gains[:, g:g + 1]).then_inc(xt_hi, 1)

            def tok_squares(stat, src, t, waits):
                for half in range(2):
                    if waits:
                        act.wait_ge(*waits[half])
                    if ST[stat] or half or t:
                        act.wait_ge(ssq, 4 * ST[stat] + 2 * t + half)
                    act.activation(junk[:, :], src(t, half), ACT.Square, scale=math.sqrt(MEAN[stat] / D),
                                   accum_out=SS[:, ST[stat], t, half:half + 1]).then_inc(ssq, 1)

            def h_squares(stat, reader, t):
                waits = [(in_x, 16)] * 2 if reader == "x" else [(h_up, h_ready(reader, t, half)) for half in range(2)]
                tok_squares(stat, lambda t, half: h[:, t, half * HALF:half * HALF + HALF], t, waits)

            def sum_squares(stat, reader, u_last, late_split=None, gain=0):
                tok_squares(stat, lambda t, half: PAIR[half][t][:, :], 0,
                            [(tok0_done, 2 * H_UP[reader] + half + 1) for half in range(2)])
                if late_split is not None:
                    split_at(late_split)
                    turned_hi(reader, lambda k: gain + k, 0, 0, 4)
                tok_squares(stat, lambda t, half: PAIR[half][t][:, :], 1, [(w_used, u_last + 1)] * 2)

            def turned(name, gain_cols, u0, squares=lambda t: None, k0=0):
                turned_hi(name, gain_cols, 0, k0)
                squares(0)
                turned_hi(name, gain_cols, 1)
                split_at(u0 + 2)
                squares(1)

            def evac(e, u_last, dst, pair, stat):
                act.wait_ge(w_used, u_last + 1)
                act.wait_ge(rstd, 2 * ST[stat] + 1)
                act.activation(dst, pair[0][:, :], ACT.Copy, scale=RS[:, ST[stat], 0:1]).then_inc(ev_a, 1)

            def head_square(n, src, e):
                act.wait_ge(ev_a, e + 1)
                act.wait_ge(ev_d, e + 1)
                if n:
                    act.wait_ge(hn_sum, n)
                act.activation(SQ[:, :].rearrange("p (t c) -> p t c", t=2), src, ACT.Square).then_inc(hn_sq, 1)

            def heads_out(n, dst, gain_col=None, scale=1.0, bank=T[0]):
                act.wait_ge(ht, 2 * n + 1)
                g = scale if gain_col is None else gains[:, gain_col:gain_col + 1]
                act.activation(dst, bank[:, :].rearrange("p (c t) -> p c t", c=2), ACT.Copy, scale=g)\
                    .then_inc(ht_a, 1)

            split_at(0)
            act.dma_start(h[:, :, :], a["x"][0].rearrange("(t p) d -> p t d", p=P)).then_inc(in_x, 16)
            act.wait_ge(gain_ok, 2)
            turned_hi("mem", lambda k: G_MEMKV + k, 0)
            split_at(1)
            tok_squares("mem", lambda t, half: nat[:, t, half * HALF:half * HALF + HALF], 0, [(in_mem[0], 16)] * 2)
            turned_hi("mem", lambda k: G_MEMKV + k, 1)
            split_at(2)
            tok_squares("mem", lambda t, half: nat[:, t, half * HALF:half * HALF + HALF], 1, [(in_mem[1], 16)] * 2)
            split_at(3, 4)
            evac(EV_MEMKV, 1, nat[:, 0, 0:HALF], PAIR[0], "mem")
            head_square(0, nat[:, :, 0:HALF], EV_MEMKV)
            split_at(5)
            act.wait_ge(gain_ok, 6)
            act.wait_ge(in_small, 64)
            act.activation(wfhi[:, :, :], wf[:, :, :], ACT.Copy).then_inc(wf_hi_s, 1)
            turned_hi("x", lambda k: G_MIX + k, 0)
            h_squares("h0", "x", 0)
            evac(EV_MEMKV + 1, 3, memV[:, 0, :], PAIR[1], "mem")
            turned_hi("x", lambda k: G_MIX + k, 1)
            split_at(6)
            h_squares("h0", "x", 1)
            act.wait_ge(f_done, 1)
            act.activation(fT[:, :], T[0][0:FOX_H, 0:S], ACT.Copy).then_inc(f_raw, 1)
            split_at(7)
            evac(EV_IN, 5, Z[:, 0, 0:512], PAIR[0], "h0")
            head_square(1, Z[:, :, 0:512], EV_IN)
            split_at(8, 9)
            evac(EV_IN + 1, 7, Z[:, 0, 512:1024], PAIR[1], "h0")
            head_square(2, Z[:, :, 512:1024], EV_IN + 1)
            split_at(10)
            act.wait_ge(f_out, 3)
            act.activation(fl[:, 2, :], fl[:, 1, :], ACT.Exp, scale=-1.0).then_inc(f_act, 1)
            act.wait_ge(lam_ok, 2)
            act.activation(lam4[:, 2:4], lam4[:, 0:2], ACT.Exp).then_inc(lam_ok, 1)
            heads_out(HT_KM, memKT[:, 0:2, :], G_KM)
            split_at(11)
            act.wait_ge(f_act, 1)
            act.activation(fl[:, 3, :], fl[:, 2, :], ACT.Ln, bias=1.0).then_inc(f_act, 1)
            evac(EV_IN + 2, 9, Z[:, 0, 1024:1536], PAIR[2], "h0")
            heads_out(HT_QF, QT[:, 0:2, :], G_QF)
            split_at(12)
            heads_out(HT_KF, KT[:, 0:2, :], G_KF)
            act.wait_ge(c_done, 1)
            act.activation(cT[:, :], B[3][0:CK, 0:S], ACT.Copy).then_inc(c_hi, 1)
            split_at(13)
            evac(EV_IN + 3, 11, Z[:, 0, 1536:2048], PAIR[0], "h0")
            act.wait_ge(pt_done, 1)
            act.wait_ge(pads_ok, 3)
            act.activation(poolT[:, 0:2, PAD:PAD + S], T[0][:, :].rearrange("p (c t) -> p c t", c=2), ACT.Copy)\
                .then_inc(pt_out, 1)

            def probs_out(r0, i, cols):
                act.wait_ge(at_r, r0 + i + 1)
                if i >= 2:
                    act.wait_ge(at_v, r0 + i - 1)
                act.activation(pT[i % 2][:, 0:cols], T[i % 2][:, 0:cols], ACT.Copy).then_inc(at_c, 1)

            def causal_exp(x0, i, src):
                act.wait_ge(at_x, x0 + 2 * i + 2)
                for t, c0, c1 in ((0, 0, 128), (1, 128, 384)):
                    col = 2 * i + t
                    act.activation(probs[i % 4][:, c0:c1], src[:, c0:c1], ACT.Exp,
                                   bias=nmax[:, col:col + 1], accum_out=lsum[:, col:col + 1]).then_inc(at_e, 1)

            for i in range(FOX_H + 1):
                if i < FOX_H:
                    if i >= 4:
                        act.wait_ge(at_r, i - 3)
                    causal_exp(0, i, scores[i % 4])
                if i:
                    probs_out(0, i - 1, 384)
            act.wait_ge(py_done, 1)
            for t in range(TOKS):
                act.activation(nat[:, t, HALF:D], B[t][:, :], ACT.Copy).then_inc(py_out, 1)
            turned("mix", lambda k: G_ONE if k < 4 else G_POOL + k - 4, U_OUT)
            split_at(15, 16, 17)
            for t in range(TOKS):
                turned_hi("mq", lambda k: G_MEMQ + k, t)
                h_squares("h1", "mq", t)
            def mem_queries_out():
                act.wait_ge(ht, 2 * HT_QM + 1)
                act.activation(QT[:, 0:4, 0:P], T[0][:, :].rearrange("p (c t) -> p c t", c=4), ACT.Copy,
                               scale=gains[:, G_QM:G_QM + 1]).then_inc(ht_a, 1)

            for t in range(TOKS):
                act.wait_ge(*((w_used, U_MQ + 2) if t else (mq_tok0, 1)))
                act.wait_ge(rstd, 2 * ST["h1"] + t + 1)
                act.wait_ge(hn_sum, 3)
                act.activation(SQ[:, t * HALF:t * HALF + HALF], PAIR[0][t][:, :], ACT.Square,
                               scale=RS[:, ST["h1"], t:t + 1]).then_inc(hn_sq, 1)
                if t == 0:
                    split_at(18)
            mem_queries_out()
            for i in range(MEM_H + 1):
                if i < MEM_H:
                    act.wait_ge(at_x, M_X + i + 1)
                    for t in range(TOKS):
                        col = 2 * i + t
                        act.activation(mprobs[i][:, t * S:t * S + S], B[i][:, t * S:t * S + S], ACT.Exp,
                                       bias=nmax[:, col:col + 1], accum_out=lsum[:, col:col + 1]).then_inc(at_e, 1)
                if i:
                    probs_out(M_R, i - 1, 512)
                if i == 2:
                    split_at(19)
            turned("mo", lambda k: G_ONE, U_MO)
            split_at(21)

            def ffn(f, stat, reader, gain, squares=True, k0=0):
                u0 = U_FFN[f]
                v = u0 + 2
                turned(reader, lambda k: gain + k, u0,
                       (lambda t: h_squares(stat, reader, t)) if squares else lambda t: None, k0)

                def gate_of(j, u, pair):
                    act.wait_ge(w_used, u + 1)
                    if not (isinstance(j, int) and j == 0 and f == 0):
                        act.wait_ge(act_ok, 2 * (FJ * f + j))
                    for t in range(TOKS):
                        act.activation(gate[:, t, :], pair[t][:, 0:256], ACT.Silu,
                                       scale=RS[:, ST[stat], t:t + 1]).then_inc(gate_ok, 1)

                def act_out(j, hi=ahi[:, :]):
                    act.wait_ge(act_t, FJ * f + j + 1)
                    act.activation(hi, T[0][:, :], ACT.Copy).then_inc(act_hi, 1)

                split_at(u0 + 3)
                act.wait_ge(rstd, 2 * ST[stat] + 2)
                gate_of(0, u0 + 1, PAIR[0])

                def step(i, last):
                    split(v + 3 * i + 2, (v + 2) % RING, i + (v + 2) // RING)
                    act_out(i)
                    split(v + 3 * i + 3, (v + 3) % RING, i + (v + 3) // RING)
                    gate_of(i + 1, v + 3 * i + 1, GU)
                    if not (last and v + 3 * i + 4 >= UNITS):
                        split(v + 3 * i + 4, (v + 4) % RING, i + (v + 4) // RING)

                with act.Fori(0, FJ - 2) as i:
                    step(i, False)
                step(FJ - 2, True)
                act_out(FJ - 1, last_hi)
                split_at(u0 + 34)

            ffn(0, "h2", "ffn0", G_FFN)
            ffn(1, "h3", "ffn1", n2(0, 0))
            sum_squares("y0", "cin", U_FFN[1] + 32)
            turned("cin", lambda k: n2(0, 2) + k, U_CIN, lambda t: h_squares("h4", "cin", t))
            def conv_evac(g):
                evac(EV_CIN + g, U_CIN + 2 * g + 1, conv_places[g][:, 0, :], PAIR[g % 3], "h4")

            def conv_u_out(p):
                act.wait_ge(conv_t, FEED_U[p])
                if p >= 2:
                    act.wait_ge(conv_c, p - 1)
                else:
                    act.wait_ge(pads_ok, 4)
                u = T[p % 2][:, :].rearrange("p (k t) -> p k t", k=2)
                act.activation(uT[:, 2 * p % 4:2 * p % 4 + 2, 2:2 + S], u, ACT.Copy)
                for k in (2 * p, 2 * p + 1):
                    ins = act.activation(convx[:, k, :], u[:, k % 2, :], ACT.Copy,
                                         scale=gains[:, G_CONV + 16 + k:G_CONV + 17 + k])
                ins.then_inc(conv_u, 1)

            def conv_hi(p):
                act.wait_ge(conv_x, p + 1)
                act.wait_ge(w_used, U_CIN + 11 if p < 2 else U_CIN + 12)
                act.activation(xhi[:, 2 * p:2 * p + 2, :], convx[:, 2 * p:2 * p + 2, :], ACT.Copy).then_inc(xt_hi, 2)

            split_at(U_CIN + 3)
            conv_evac(0)
            for g in (1, 2, 3):
                split_at(U_CIN + 2 * g + 2, U_CIN + 2 * g + 3)
                if g == 3:
                    conv_u_out(0)
                conv_evac(g)
            split_at(U_CIN + 10)
            conv_u_out(1)
            split_at(U_CIN + 11)
            conv_evac(4)
            split_at(U_COUT, U_COUT + 1)
            conv_u_out(2)
            conv_hi(0)
            conv_hi(1)
            conv_u_out(3)
            conv_evac(5)
            conv_hi(2)
            conv_hi(3)
            split_at(*range(U_COUT + 2, U_COUT + 5))
            sum_squares("y1", "ffn2", U_COUT + 3, U_COUT + 5, n2(0, 4))
            ffn(2, "h5", "ffn2", n2(0, 4), k0=4)
            sum_squares("y2", "kv", U_FFN[2] + 32)
            turned("kv", lambda k: G_KV + k, U_KV, lambda t: h_squares("h6", "kv", t))
            for g in range(4):
                if g:
                    split_at(U_KV + 2 * g + 2)
                if g >= 2:
                    heads_out(HT_KD + g - 2, KT[:, 4 * g - 8:4 * g - 6, :])
                split_at(U_KV + 2 * g + 3)
                evac(EV_KV + g, U_KV + 2 * g + 1, kv_places[g][:, 0, :], PAIR[KV_PAIR[g]], "h6")
            ffn(3, "h6", "ffn3", n2(1, 0), squares=False)
            sum_squares("y3", "q", U_FFN[3] + 32)
            turned("q", lambda k: n2(1, 2) + k, U_Q, lambda t: h_squares("h7", "q", t))
            split_at(U_Q + 3)
            evac(EV_Q, U_Q + 1, Z[:, 0, 0:HALF], PAIR[0], "h7")
            split_at(U_Q + 4)
            heads_out(HT_QD, QT[:, 0:2, :], scale=DIFF_DH ** -0.5)
            split_at(U_Q + 5)

            def o_squares(g, t):
                act.wait_ge(at_v, D_R + 4 * g + 4)
                act.activation(osq[:, t, g * HALF:g * HALF + HALF], PAIR[g][t][:, :], ACT.Square).then_inc(hn_sq, 1)

            for i in range(DIFF_H + 1):
                for m in (2 * i, 2 * i + 1):
                    if i < DIFF_H:
                        if m >= 4:
                            act.wait_ge(at_r, D_R + i - 1)
                        causal_exp(D_X, m, B[4 + m % 2])
                    if i and m == 2 * i:
                        probs_out(D_R, i - 1, 384)
                if i == 2:
                    evac(EV_Q + 1, U_Q + 3, Z[:, 0, HALF:D], PAIR[1], "h7")
                if i == 3:
                    heads_out(HT_QD + 1, QT[:, 4:6, :], scale=DIFF_DH ** -0.5, bank=B[2])
                if i == 5:
                    o_squares(0, 0)
                    o_squares(0, 1)
            o_squares(1, 0)
            turned_hi("ao", lambda k: G_SUB, 0, 0, 4)
            o_squares(1, 1)
            turned_hi("ao", lambda k: G_SUB, 0, 4)
            turned_hi("ao", lambda k: G_SUB, 1)
            split_at(U_O + 2)
            split_at(*range(U_O + 3, U_O + 5))
            sum_squares("y4", "ffn4", U_O + 3, U_O + 5, n2(1, 4))
            ffn(4, "h8", "ffn4", n2(1, 4), k0=4)
            sum_squares("y5", "out", U_FFN[4] + 32)

        @block.vector
        def _(dve):
            steps = [0]

            def link(ins):
                steps[0] += 1
                ins.then_inc(dve_step, 1)
                dve.wait_ge(dve_step, steps[0])

            def split(u, slot):
                dve.wait_ge(w_hi, u + 1)
                dve.tensor_tensor(wlo[slot][:, :], raw[slot][:, :], whi[slot][:, :].bitcast(F32), ALU.subtract)\
                    .then_inc(w_lo, 1)

            def split_at(*units):
                for u in units:
                    if u < UNITS:
                        split(u, u % RING)

            def turned_lo(name, gain_cols, t, k0=0, k1=KD):
                for k in range(k0, min(k1, CHUNKS[name])):
                    if k % 2 == 0:
                        dve.wait_ge(xt_hi, XT[name] + t * CHUNKS[name] + k + 2)
                    g = gain_cols(k)
                    x = slice(t * P, t * P + P)
                    dve.scalar_tensor_tensor(out=xlo[:, k, x], in0=TURN[k // 2][:, (k % 2) * P:(k % 2) * P + P],
                                             scalar=gains[:, g:g + 1], in1=xhi[:, k, x].bitcast(F32),
                                             op0=ALU.mult, op1=ALU.subtract).then_inc(xt_lo, 1)

            def turned(name, gain_cols, u0, update=lambda t: None, late_split=None):
                update(0)
                if late_split == "before":
                    split_at(u0 + 1)
                turned_lo(name, gain_cols, 0, 0, 4)
                if late_split == "between":
                    split_at(u0 + 1)
                turned_lo(name, gain_cols, 0, 4)
                update(1)
                turned_lo(name, gain_cols, 1)
                split_at(u0 + 2)

            def evac(e, u_last, dst, pair, stat):
                dve.wait_ge(w_used, u_last + 1)
                dve.wait_ge(rstd, 2 * ST[stat] + 2)
                dve.tensor_scalar(dst, pair[1][:, :], RS[:, ST[stat], 1:2], None, ALU.mult).then_inc(ev_d, 1)

            def head_sum(n, heads, dh):
                dve.wait_ge(hn_sq, n + 1)
                dve.tensor_reduce(HS[:, n, 0:TOKS * heads], SQ[:, :].rearrange("p (h d) -> p h d", d=dh), AX.X, ALU.add)\
                    .then_inc(hn_sum, 1)

            def head_scale(n, x, heads, dh):
                dve.wait_ge(hn_r, n + 1)
                v = x.rearrange("p t (h d) -> p t h d", d=dh)
                for t in range(TOKS):
                    r = HR[:, n, t * heads:(t + 1) * heads].unsqueeze(2).to_broadcast([P, heads, dh])
                    dve.tensor_tensor(v[:, t], v[:, t], r, ALU.mult).then_inc(hn_x, 1)

            def heads_out(n, dst, gain_col=None, scale=1.0, bank=T[1]):
                dve.wait_ge(ht, 2 * n + 2)
                g = scale if gain_col is None else gains[:, gain_col:gain_col + 1]
                dve.tensor_scalar(dst, bank[:, :].rearrange("p (c t) -> p c t", c=2), g, None, ALU.mult)\
                    .then_inc(ht_d, 1)

            def h_update(reader, u_last, t):
                for half in range(2):
                    dve.wait_ge(*((w_used, u_last + 1) if t else (tok0_done, 2 * H_UP[reader] + half + 1)))
                    part = h[:, t, half * HALF:half * HALF + HALF]
                    dve.tensor_tensor(part, part, PAIR[half][t][:, :], ALU.add).then_inc(h_up, 1)

            def post_update(b, stat, reader, t):
                if t == 0:
                    dve.wait_ge(post_in[b % 2], 16 * (b // 2 + 1))
                else:
                    dve.wait_ge(h_up, h_ready(reader, 0, 1))
                for half in range(2):
                    c = slice(half * HALF, half * HALF + HALF)
                    dve.wait_ge(ssq, 4 * ST[stat] + 2 * t + half + 1)
                    ins = dve.tensor_tensor(tmp[:, half, :], PAIR[half][t][:, :], gpost[:, b % 2, c], ALU.mult)
                link(ins)
                dve.wait_ge(rstd, 2 * ST[stat] + t + 1)
                for half in range(2):
                    c = slice(half * HALF, half * HALF + HALF)
                    dve.scalar_tensor_tensor(out=h[:, t, c], in0=tmp[:, half, :], scalar=RS[:, ST[stat], t:t + 1],
                                             in1=h[:, t, c], op0=ALU.mult, op1=ALU.add).then_inc(h_up, 1)

            dve.memset(VD[:, :, :], 0.0).then_inc(pads_ok, 1)
            dve.memset(win[0], 0.0).then_inc(pads_ok, 1)
            dve.memset(win[1], 0.0).then_inc(pads_ok, 1)
            dve.memset(gains[:, G_ONE:G_ONE + 1], 1.0).then_inc(gain_ok, 1)
            dve.wait_ge(gain_T, 1)
            dve.tensor_copy(gains[:, G_MEMKV:G_MEMKV + 8], T[0][:, 0:8]).then_inc(gain_ok, 1)
            dve.wait_ge(gain_ok, 2)
            split_at(0)
            turned("mem", lambda k: G_MEMKV + k, U_MEMKV, late_split="between")
            split_at(3, 4)
            evac(EV_MEMKV, 1, nat[:, 1, 0:HALF], PAIR[0], "mem")
            dve.wait_ge(gain_T, 2)
            dve.tensor_copy(gains[:, 0:G_ROWS1], T[0][:, 0:G_ROWS1]).then_inc(gain_ok, 1)
            dve.tensor_copy(gains[:, G_ROWS1 + 8:G_ROWS1 + G_ROWS2], T[0][:, 136:128 + G_ROWS2]).then_inc(gain_ok, 1)
            dve.wait_ge(gain_ok, 4)
            for g, dh in ((G_QF, FOX_DH), (G_QM, MEM_DH)):
                dve.tensor_scalar(gains[:, g:g + 1], gains[:, g:g + 1], dh ** -0.5, None, ALU.mult).then_inc(gain_ok, 1)
            dve.wait_ge(gain_ok, 6)
            head_sum(0, MEM_H, MEM_DH)
            split_at(5)
            turned_lo("x", lambda k: G_MIX + k, 0)
            dve.wait_ge(wf_hi_s, 1)
            dve.tensor_tensor(wflo[:, :, :], wf[:, :, :], wfhi[:, :, :].bitcast(F32), ALU.subtract).then_inc(wf_lo_s, 1)
            head_scale(0, nat[:, :, 0:HALF], MEM_H, MEM_DH)
            evac(EV_MEMKV + 1, 3, memV[:, 1, :], PAIR[1], "mem")
            turned_lo("x", lambda k: G_MIX + k, 1)
            split_at(6)
            for i in range(2):
                link(dve.tensor_tensor(work[:, 64 * i:64 * i + DIFF_DH], lamp[:, 2 * i, :], lamp[:, 2 * i + 1, :], ALU.mult))
                dve.reduce_sum(lam4[:, i:i + 1], work[:, 64 * i:64 * i + DIFF_DH], AX.X).then_inc(lam_ok, 1)
            split_at(7)
            evac(EV_IN, 5, Z[:, 1, 0:512], PAIR[0], "h0")
            head_sum(1, FOX_H, FOX_DH)
            split_at(8, 9)
            dve.wait_ge(f_done, 2)
            f2 = fl[:, 0, :].rearrange("p (t c) -> p t c", t=2)
            for t in range(TOKS):
                dve.scalar_tensor_tensor(out=f2[:, t, :], in0=T[1][:, 8 * t:8 * t + 8], scalar=RS[:, ST["h0"], t:t + 1],
                                         in1=bf[:, :], op0=ALU.mult, op1=ALU.add).then_inc(f_out, 1)
            head_scale(1, Z[:, :, 0:512], FOX_H, FOX_DH)
            evac(EV_IN + 1, 7, Z[:, 1, 512:1024], PAIR[1], "h0")
            head_sum(2, FOX_H, FOX_DH)
            split_at(10)
            dve.wait_ge(f_out, 2)
            dve.scalar_tensor_tensor(out=fl[:, 1, :], in0=fl[:, 0, :], scalar=-1.0, in1=fl[:, 0, :], op0=ALU.mult,
                                     op1=ALU.max).then_inc(f_out, 1)
            heads_out(HT_KM, memKT[:, 2:4, :], G_KM)
            split_at(11)
            head_scale(2, Z[:, :, 512:1024], FOX_H, FOX_DH)
            dve.wait_ge(lam_ok, 3)
            dve.scalar_tensor_tensor(out=lam4[:, 0:1], in0=lam4[:, 3:4], scalar=-lambda_init, in1=lam4[:, 2:3],
                                     op0=ALU.add, op1=ALU.subtract).then_inc(lam_ok, 1)
            dve.wait_ge(f_act, 2)
            dve.wait_ge(logf_0, 1)
            for c in (0, 64):
                dve.scalar_tensor_tensor(out=logf[:, :, c:c + FOX_H], in0=f2, scalar=0.0,
                                         in1=fl[:, 3, :].rearrange("p (t c) -> p t c", t=2), op0=ALU.min,
                                         op1=ALU.subtract).then_inc(f_log, 1)
            evac(EV_IN + 2, 9, Z[:, 1, 1024:1536], PAIR[2], "h0")
            heads_out(HT_QF, QT[:, 2:4, :], G_QF)
            split_at(12)
            heads_out(HT_KF, KT[:, 2:4, :], G_KF)
            dve.wait_ge(c_done, 1)
            dve.tensor_copy(cn[:, :, :], B[2][:, 0:16].rearrange("p (t c) -> p t c", t=2)).then_inc(c_out, 1)
            dve.wait_ge(c_hi, 1)
            low = slice(64, CK)
            dve.tensor_tensor(cT[low, :], B[3][low, 0:S], cT[low, :].bitcast(F32), ALU.subtract).then_inc(c_out, 1)
            split_at(13)
            evac(EV_IN + 3, 11, Z[:, 1, 1536:2048], PAIR[0], "h0")
            dve.wait_ge(pt_done, 2)
            dve.tensor_copy(poolT[:, 2:4, PAD:PAD + S], T[1][:, :].rearrange("p (c t) -> p c t", c=2)).then_inc(pt_out, 1)

            def row_max(i, src):
                for t, c0, c1 in ((0, 0, 128), (1, 128, 384)):
                    col = 2 * i + t
                    dve.tensor_reduce(nmax[:, col:col + 1], src[:, c0:c1], AX.X, ALU.max, negate=True)\
                        .then_inc(at_x, 1)

            dve.wait_ge(in_const, 80)
            dve.wait_ge(c_out, 2)
            for i in range(FOX_H):
                dve.wait_ge(at_s, i + 1)
                if i >= 4:
                    dve.wait_ge(at_e, 2 * (i - 3))
                for t, c0, c1 in ((0, 0, 128), (1, 128, 384)):
                    dve.scalar_tensor_tensor(out=scores[i % 4][:, c0:c1], in0=B[i % 4][:, c0:c1],
                                             scalar=cn[:, t, i:i + 1], in1=foxmask[:, c0:c1], op0=ALU.add,
                                             op1=ALU.add).then_inc(at_m, 1)
                dve.wait_ge(at_m, 2 * i + 2)
                row_max(i, scores[i % 4])

            def values_out(e0, count, v0, heads, dh):
                dve.wait_ge(at_e, e0 + count)
                link(dve.reciprocal(linv[:, 0:count], lsum[:, 0:count]))
                dve.wait_ge(at_v, v0 + heads)
                r = linv[:, 0:count].rearrange("p (h t) -> p t h", t=2)
                for t in range(TOKS):
                    dve.tensor_tensor(nat[:, t, 0:HALF].rearrange("p (h d) -> p h d", d=dh),
                                      B[4 + t][:, :].rearrange("p (h d) -> p h d", d=dh),
                                      r[:, t].unsqueeze(2).to_broadcast([P, heads, dh]), ALU.mult).then_inc(at_o, 1)

            values_out(0, 16, 0, FOX_H, FOX_DH)
            turned("mix", lambda k: G_ONE if k < 4 else G_POOL + k - 4, U_OUT)
            split_at(15, 16)
            for t in range(TOKS):
                h_update("mq", U_OUT + 3, t)
                turned_lo("mq", lambda k: G_MEMQ + k, t, 0, 4)
                if t == 0:
                    split_at(17)
                turned_lo("mq", lambda k: G_MEMQ + k, t, 4)
            for t in range(TOKS):
                c = slice(t * MEM_H, t * MEM_H + MEM_H)
                dve.wait_ge(hn_sq, 3 + t + 1)
                dve.tensor_reduce(HS[:, 3, c], SQ[:, t * HALF:t * HALF + HALF].rearrange("p (h d) -> p h d", d=MEM_DH),
                                  AX.X, ALU.add).then_inc(hn_sum, 1)
                dve.wait_ge(hn_r, 3 + t + 1)
                dve.tensor_tensor(Z[:, t, 0:HALF].rearrange("p (h d) -> p h d", d=MEM_DH),
                                  PAIR[0][t][:, :].rearrange("p (h d) -> p h d", d=MEM_DH),
                                  HR[:, 3, c].unsqueeze(2).to_broadcast([P, MEM_H, MEM_DH]), ALU.mult).then_inc(hn_x, 1)
            dve.wait_ge(ht, 2 * HT_QM + 2)
            dve.tensor_scalar(QT[:, 0:4, P:2 * P], T[1][:, :].rearrange("p (c t) -> p c t", c=4), gains[:, G_QM:G_QM + 1],
                              None, ALU.mult).then_inc(ht_d, 1)
            for i in range(MEM_H):
                if i == 3:
                    split_at(18)
                dve.wait_ge(at_s, M_S + i + 1)
                dve.tensor_reduce(nmax[:, 2 * i:2 * i + 2], B[i][:, :].rearrange("p (t c) -> p t c", t=2), AX.X,
                                  ALU.max, negate=True).then_inc(at_x, 1)
            split_at(19)
            values_out(M_E, 8, M_R, MEM_H, MEM_DH)
            turned("mo", lambda k: G_ONE, U_MO)

            def ffn(f, stat, reader, gain, update=lambda t: None, late_split=None):
                u0 = U_FFN[f]
                v = u0 + 2
                turned(reader, lambda k: gain + k, u0, update, late_split)

                def act_of(j, pair):
                    for t in range(TOKS):
                        dve.wait_ge(gate_ok, 2 * (FJ * f + j) + t + 1)
                        dve.scalar_tensor_tensor(out=actn[:, t, :], in0=pair[t][:, 256:512],
                                                 scalar=RS[:, ST[stat], t:t + 1], in1=gate[:, t, :],
                                                 op0=ALU.mult, op1=ALU.mult).then_inc(act_ok, 1)

                def act_out(j, hi=ahi[:, :], lo=alo[:, :]):
                    dve.wait_ge(act_hi, FJ * f + j + 1)
                    dve.tensor_tensor(lo, T[0][:, :], hi.bitcast(F32), ALU.subtract).then_inc(act_lo, 1)

                split_at(u0 + 3)
                dve.wait_ge(rstd, 2 * ST[stat] + 2)
                act_of(0, PAIR[0])

                def step(i, last):
                    split(v + 3 * i + 2, (v + 2) % RING)
                    act_out(i)
                    split(v + 3 * i + 3, (v + 3) % RING)
                    act_of(i + 1, GU)
                    if not (last and v + 3 * i + 4 >= UNITS):
                        split(v + 3 * i + 4, (v + 4) % RING)

                with dve.Fori(0, FJ - 2) as i:
                    step(i, False)
                step(FJ - 2, True)
                act_out(FJ - 1, last_hi, last_lo)
                split_at(u0 + 34)

            ffn(0, "h2", "ffn0", G_FFN, lambda t: h_update("ffn0", U_MO + 1, t),
                late_split="between")
            ffn(1, "h3", "ffn1", n2(0, 0), lambda t: h_update("ffn1", U_FFN[0] + 32, t))
            turned("cin", lambda k: n2(0, 2) + k, U_CIN, lambda t: post_update(0, "y0", "cin", t))
            def conv_evac(g):
                evac(EV_CIN + g, U_CIN + 2 * g + 1, conv_places[g][:, 1, :], PAIR[g % 3], "h4")

            def conv_taps(p):
                dve.wait_ge(conv_u, p + 1)
                for w in (1, 0):
                    for k in (2 * p, 2 * p + 1):
                        if w == 0 and k == 2 * p:
                            dve.wait_ge(dve_step, steps[0])
                        g = gains[:, G_CONV + 8 * w + k:G_CONV + 8 * w + k + 1]
                        ins = dve.scalar_tensor_tensor(out=convx[:, k, :], in0=uT[:, k % 4, w:w + S], scalar=g,
                                                       in1=convx[:, k, :], op0=ALU.mult, op1=ALU.add)
                    if w:
                        steps[0] += 1
                        ins.then_inc(dve_step, 1)
                ins.then_inc(conv_c, 1)

            def conv_gate(p):
                dve.wait_ge(conv_t, FEED_B[p])
                dve.wait_ge(conv_c, p + 1)
                x = convx[:, 2 * p:2 * p + 2, :]
                dve.tensor_tensor(x, T[p % 2][:, :].rearrange("p (k t) -> p k t", k=2), x, ALU.mult).then_inc(conv_x, 1)

            def conv_lo(p):
                k = slice(2 * p, 2 * p + 2)
                dve.wait_ge(xt_hi, XT["cout"] + 2 * p + 2)
                dve.tensor_tensor(xlo[:, k, :], convx[:, k, :], xhi[:, k, :].bitcast(F32), ALU.subtract)\
                    .then_inc(xt_lo, 2)

            split_at(U_CIN + 3)
            conv_evac(0)
            for g in (1, 2, 3):
                split_at(U_CIN + 2 * g + 2, U_CIN + 2 * g + 3)
                if g == 1:
                    dve.memset(uT[:, :, 0:2], 0.0).then_inc(pads_ok, 1)
                if g == 3:
                    conv_taps(0)
                conv_evac(g)
            split_at(U_CIN + 10)
            conv_taps(1)
            conv_gate(0)
            split_at(U_CIN + 11)
            conv_gate(1)
            conv_evac(4)
            split_at(U_COUT, U_COUT + 1)
            conv_taps(2)
            conv_lo(0)
            conv_lo(1)
            conv_evac(5)
            conv_taps(3)
            conv_gate(2)
            conv_gate(3)
            conv_lo(2)
            conv_lo(3)
            split_at(*range(U_COUT + 2, U_COUT + 5))
            ffn(2, "h5", "ffn2", n2(0, 4), lambda t: post_update(1, "y1", "ffn2", t), late_split="before")
            turned("kv", lambda k: G_KV + k, U_KV, lambda t: post_update(2, "y2", "kv", t))
            for g in range(4):
                if g:
                    split_at(U_KV + 2 * g + 2)
                if g >= 2:
                    heads_out(HT_KD + g - 2, KT[:, 4 * g - 6:4 * g - 4, :])
                split_at(U_KV + 2 * g + 3)
                evac(EV_KV + g, U_KV + 2 * g + 1, kv_places[g][:, 1, :], PAIR[KV_PAIR[g]], "h6")
            ffn(3, "h6", "ffn3", n2(1, 0))
            turned("q", lambda k: n2(1, 2) + k, U_Q, lambda t: post_update(3, "y3", "q", t))
            split_at(U_Q + 3)
            evac(EV_Q, U_Q + 1, Z[:, 1, 0:HALF], PAIR[0], "h7")
            split_at(U_Q + 4)
            heads_out(HT_QD, QT[:, 2:4, :], scale=DIFF_DH ** -0.5)

            def combine(i):
                p0, p1 = probs[2 * i % 4], probs[(2 * i + 1) % 4]
                l0, l1 = slice(4 * i, 4 * i + 2), slice(4 * i + 2, 4 * i + 4)
                dve.wait_ge(at_e, D_E + 4 * i + 4)
                link(dve.reciprocal(linv[:, l1], lsum[:, l1]))
                link(dve.scalar_tensor_tensor(out=linv[:, l0], in0=lsum[:, l0], scalar=lam4[:, 0:1], in1=linv[:, l1],
                                              op0=ALU.mult, op1=ALU.mult))
                for t, c0, c1 in ((0, 0, 128), (1, 128, 384)):
                    dve.scalar_tensor_tensor(out=p0[:, c0:c1], in0=p1[:, c0:c1],
                                             scalar=linv[:, 4 * i + t:4 * i + t + 1], in1=p0[:, c0:c1],
                                             op0=ALU.mult, op1=ALU.add).then_inc(at_a, 1)

            def o_sum(g, t):
                c = slice(8 * g + 4 * t, 8 * g + 4 * t + 4)
                dve.wait_ge(hn_sq, HN_D + 2 * g + t + 1)
                link(dve.tensor_reduce(HS[:, 4, c], osq[:, t, g * HALF:g * HALF + HALF].rearrange(
                    "p (h d) -> p h d", d=2 * DIFF_DH), AX.X, ALU.add))
                dve.wait_ge(eps_l, g + 1)
                dve.scalar_tensor_tensor(out=HV[:, 4, c], in0=HS[:, 4, c], scalar=SUB_M / (2 * DIFF_DH),
                                         in1=epsl[:, c], op0=ALU.mult, op1=ALU.add).then_inc(hn_sum, 1)

            def o_norm(g, t):
                c = slice(8 * g + 4 * t, 8 * g + 4 * t + 4)
                dve.wait_ge(hn_r, HN_D + 2 * g + t + 1)
                r = HR[:, 4, c].unsqueeze(2).to_broadcast([P, 4, 128])
                dve.tensor_tensor(nat[:, t, g * HALF:g * HALF + HALF].rearrange("p (h d) -> p h d", d=128),
                                  PAIR[g][t][:, :].rearrange("p (h d) -> p h d", d=128), r, ALU.mult).then_inc(at_o, 1)

            def diff_max(m):
                if m < 2 * DIFF_H:
                    dve.wait_ge(at_s, D_S + m + 1)
                    row_max(m, B[4 + m % 2])

            diff_max(0)
            diff_max(1)
            split_at(U_Q + 5)
            for i in range(DIFF_H):
                diff_max(2 * i + 2)
                combine(i)
                diff_max(2 * i + 3)
                if i == 1:
                    evac(EV_Q + 1, U_Q + 3, Z[:, 1, HALF:D], PAIR[1], "h7")
                if i == 2:
                    heads_out(HT_QD + 1, QT[:, 6:8, :], scale=DIFF_DH ** -0.5, bank=B[3])
                if i == 5:
                    o_sum(0, 0)
                    o_sum(0, 1)
                if i == 6:
                    o_norm(0, 0)
                    o_norm(0, 1)
            o_sum(1, 0)
            turned_lo("ao", lambda k: G_SUB, 0, 0, 4)
            o_norm(1, 0)
            o_sum(1, 1)
            turned_lo("ao", lambda k: G_SUB, 0, 4)
            o_norm(1, 1)
            turned_lo("ao", lambda k: G_SUB, 1)
            split_at(U_O + 2)
            split_at(*range(U_O + 3, U_O + 5))
            ffn(4, "h8", "ffn4", n2(1, 4), lambda t: post_update(4, "y4", "ffn4", t), late_split="before")
            for t in range(TOKS):
                post_update(5, "y5", "out", t)

        @block.tensor
        def _(pe):
            def turn(name, t, j, src, waits):
                for w in waits(t, j // 2):
                    pe.wait_ge(*w)
                if t:
                    pe.wait_ge(xt_lo, XT[name] + 2 * j + 2)
                for k in (2 * j, 2 * j + 1):
                    ins = pe.transpose(TURN[j][:, (k % 2) * P:(k % 2) * P + P], src[:, t, k * P:k * P + P], ident[:, :])
                ins.then_inc(t_done, 1)

            def product(bank, s, c, k, t, first, last):
                x = slice(t * P, t * P + P)
                pe.matmul(bank[:, :], xlo[:, k, x], whi[s][:, c], start=first, stop=False)
                pe.matmul(bank[:, :], xhi[:, k, x], wlo[s][:, c], start=False, stop=False)
                return pe.matmul(bank[:, :], xhi[:, k, x], whi[s][:, c], start=False, stop=last)

            def columns(k):
                return slice(k % 4 * HALF, k % 4 * HALF + HALF)

            def k_unit(u, banks, k0):
                pe.wait_ge(w_lo, u + 1)
                for k in range(k0, k0 + 4):
                    for t in range(TOKS):
                        ins = product(banks[t], u % RING, columns(k), k, t, k == 0, k == KD - 1)
                ins.then_inc(w_used, 1)

            def group(u, banks):
                k_unit(u, banks, 0)
                k_unit(u + 1, banks, 4)

            def first_group(u, name, banks, src, waits, halves=False, tok0=None):
                for j in range(2 if halves else 4):
                    turn(name, 0, j, src, waits)
                for t in range(TOKS):
                    for k in range(KD):
                        if t == 0 and k % 4 == 0:
                            pe.wait_ge(w_lo, u + k // 4 + 1)
                        pe.wait_ge(xt_lo, XT[name] + t * KD + k + 1)
                        ins = product(banks[t], (u + k // 4) % RING, columns(k), k, t, k == 0, k == KD - 1)
                        if t and k % 4 == 3:
                            ins.then_inc(w_used, 1)
                        if tok0 and t == 0 and k == KD - 1:
                            ins.then_inc(tok0, 1)
                        if halves and t == 0 and k == 3:
                            turn(name, 0, 2, src, waits)
                            turn(name, 0, 3, src, waits)
                        if t == 0 and k in (5, 7):
                            turn(name, 1, k - 5, src, waits)
                            turn(name, 1, k - 4, src, waits)

            def last_group(u, banks):
                for t in range(TOKS):
                    for k in range(KD):
                        if t == 0 and k % 4 == 0:
                            pe.wait_ge(w_lo, u + k // 4 + 1)
                        ins = product(banks[t], (u + k // 4) % RING, columns(k), k, t, k == 0, k == KD - 1)
                        if t and k % 4 == 3:
                            ins.then_inc(w_used, 1)
                        if t == 0 and k in (0, KD - 1):
                            ins.then_inc(tok0_done, 1)

            def h_waits(reader):
                return lambda t, half: [(h_up, h_ready(reader, t, half))]

            def evacuated(e):
                pe.wait_ge(ev_a, e + 1)
                pe.wait_ge(ev_d, e + 1)

            def heads_turn(n, src, banks=T):
                for b in range(2):
                    for c in range(2):
                        for t in range(TOKS):
                            col = (2 * b + c) * P
                            ins = pe.transpose(banks[b][:, (2 * c + t) * P:(2 * c + t) * P + P],
                                               src[:, t, col:col + P], ident[:, :])
                    ins.then_inc(ht, 1)

            def t_free_heads(n):
                pe.wait_ge(ht_a, n + 1)
                pe.wait_ge(ht_d, n + 1)

            pe.wait_ge(in_id, 16)
            pe.wait_ge(in_mgain, 16)
            pe.transpose(T[0][:, 0:8], grow2[0:8, :], ident[0:8, 0:8]).then_inc(gain_T, 1)
            pe.wait_ge(gain_ok, 2)
            first_group(U_MEMKV, "mem", PAIR[0], nat, lambda t, half: [(in_mem[t], 16)])
            k_unit(U_MEMKV + 2, PAIR[1], 0)
            pe.wait_ge(in_gain, 14 * 16)
            pe.transpose(T[0][:, 0:G_ROWS1], grow1[0:G_ROWS1, :], ident[0:G_ROWS1, 0:G_ROWS1])
            pe.transpose(T[0][:, 128:128 + G_ROWS2], grow2[0:G_ROWS2, :], ident[0:G_ROWS2, 0:G_ROWS2])\
                .then_inc(gain_T, 1)
            k_unit(U_MEMKV + 3, PAIR[1], 4)
            pe.wait_ge(gain_ok, 4)
            evacuated(EV_MEMKV)
            first_group(U_IN, "x", PAIR[0], h, lambda t, half: [(in_x, 16)])
            pe.wait_ge(wf_lo_s, 1)
            f = T[0][0:FOX_H, 0:S]
            for k in range(KD):
                pe.matmul(f, wfhi[:, k, :], xlo[:, k, :], start=k == 0, stop=False)
                pe.matmul(f, wflo[:, k, :], xhi[:, k, :], start=False, stop=False)
                ins = pe.matmul(f, wfhi[:, k, :], xhi[:, k, :], start=False, stop=k == KD - 1)
            ins.then_inc(f_done, 1)
            evacuated(EV_MEMKV + 1)
            k_unit(U_IN + 2, PAIR[1], 0)
            pe.wait_ge(f_raw, 1)
            for t in range(TOKS):
                ins = pe.transpose(T[1][:, 8 * t:8 * t + 8], fT[:, t * P:t * P + P], ident[0:FOX_H, 0:FOX_H])
            ins.then_inc(f_done, 1)
            k_unit(U_IN + 3, PAIR[1], 4)
            k_unit(U_IN + 4, PAIR[2], 0)
            pe.wait_ge(f_out, 2)
            pe.wait_ge(hn_x, 2)
            heads_turn(HT_KM, nat)
            k_unit(U_IN + 5, PAIR[2], 4)
            t_free_heads(HT_KM)
            pe.wait_ge(hn_x, 4)
            heads_turn(HT_QF, Z[:, :, 0:512])
            evacuated(EV_IN)
            k_unit(U_IN + 6, PAIR[0], 0)
            t_free_heads(HT_QF)
            pe.wait_ge(hn_x, 6)
            heads_turn(HT_KF, Z[:, :, 512:1024])
            pe.wait_ge(f_log, 2)
            pe.wait_ge(in_const, 80)
            evacuated(EV_IN + 1)
            for t in range(TOKS):
                for j in range(t + 1):
                    pe.matmul(B[2][:, 8 * t:8 * t + 8], tri[:, j, t * P:t * P + P], logf[:, j, 0:FOX_H],
                              start=j == 0, stop=j == t)
            for j in range(TOKS):
                ins = pe.matmul(B[3][0:CK, 0:S], logf[:, j, :], tri[:, j, :], start=j == 0, stop=j == 1)
            ins.then_inc(c_done, 1)
            k_unit(U_IN + 7, PAIR[0], 4)
            t_free_heads(HT_KF)
            evacuated(EV_IN + 2)
            for b in range(2):
                for c in range(2):
                    for t in range(TOKS):
                        col = 1024 + (2 * b + c) * P
                        ins = pe.transpose(T[b][:, (2 * c + t) * P:(2 * c + t) * P + P], Z[:, t, col:col + P],
                                           ident[:, :])
                ins.then_inc(pt_done, 1)

            def causal_turn(i, src, done):
                for b in range(3):
                    ins = pe.transpose(T[i % 2][:, b * P:b * P + P], src[:, b * P:b * P + P], ident[:, :])
                ins.then_inc(done, 1)

            def causal_values(i, out0, out1, v):
                pe.matmul(out0, pT[i % 2][:, 0:P], v[:, 0, :], start=True, stop=True)
                pe.matmul(out1, pT[i % 2][:, P:2 * P], v[:, 0, :], start=True, stop=False)
                pe.matmul(out1, pT[i % 2][:, 2 * P:3 * P], v[:, 1, :], start=False, stop=True).then_inc(at_v, 1)

            def fox_scores(i):
                c, r = i // 2, slice(64 * (i % 2), 64 * (i % 2) + 64)
                if i >= 4:
                    pe.wait_ge(at_m, 2 * (i - 3))
                b = B[i % 4]
                for q, lo, width in ((0, 0, P), (1, P, S)):
                    pe.matmul(b[:, lo:lo + width], QT[r, c, q * P:q * P + P], KT[r, c, 0:width], start=True, stop=False)
                    ins = pe.matmul(b[:, lo:lo + width], selr[i // 4][:, i % 4, :], cT[:, 0:width], start=False, stop=True)
                ins.then_inc(at_s, 1)

            def fox_values(i):
                pe.wait_ge(at_c, i + 1)
                d = slice(64 * i, 64 * i + 64)
                causal_values(i, B[4][:, d], B[5][:, d], Z[:, :, 1536 + 64 * i:1600 + 64 * i])

            pe.wait_ge(c_out, 2)
            pe.wait_ge(sel_ok, 2)
            evacuated(EV_IN + 3)
            fox_scores(0)
            fox_scores(1)
            fox_scores(2)
            for i in range(FOX_H):
                pe.wait_ge(at_e, 2 * i + 2)
                if i < 2:
                    pe.wait_ge(pt_out, 2)
                else:
                    pe.wait_ge(at_c, i - 1)
                causal_turn(i, probs[i % 4], at_r)
                if i + 3 < FOX_H:
                    fox_scores(i + 3)
                if i:
                    fox_values(i - 1)
            fox_values(FOX_H - 1)
            pe.wait_ge(mixed_ok, 4)
            pe.wait_ge(in_small, 64)
            pe.wait_ge(at_m, 16)
            for g in range(4):
                for t in range(TOKS):
                    ins = pe.matmul(B[t][:, g * P:g * P + P], mixT[:, g, t * P:t * P + P], wpool[:, g, :],
                                    start=True, stop=True)
            ins.then_inc(py_done, 1)
            pe.wait_ge(at_o, 2)
            first_group(U_OUT, "mix", PAIR[0], nat, lambda t, half: [(py_out, 2)] if half else [(at_o, 2)])
            last_group(U_OUT + 2, PAIR[1])
            first_group(U_MQ, "mq", PAIR[0], h, h_waits("mq"), tok0=mq_tok0)

            def turn_queries(t):
                for c in range(MEM_H):
                    ins = pe.transpose(T[t][:, c * P:c * P + P], Z[:, t, c * P:c * P + P], ident[:, :])
                ins.then_inc(ht, 1)

            def mem_scores(i, t):
                return pe.matmul(B[i][:, t * S:t * S + S], QT[:, i, t * P:t * P + P], memKT[:, i, :],
                                 start=True, stop=True)

            pe.wait_ge(hn_x, 7)
            turn_queries(0)
            pe.wait_ge(ht_a, HT_QM + 1)
            for i in (0, 2, 3):
                mem_scores(i, 0)
            pe.wait_ge(hn_x, 8)
            turn_queries(1)
            pe.wait_ge(ht_d, HT_QM + 1)

            for i in range(MEM_H):
                if i == 1:
                    mem_scores(1, 0)
                mem_scores(i, 1).then_inc(at_s, 1)
            def mem_values(i):
                pe.wait_ge(at_c, M_R + i + 1)
                for t in range(TOKS):
                    for b in range(2):
                        c = (2 * t + b) * P
                        ins = pe.matmul(B[4 + t][:, i * P:i * P + P], pT[i % 2][:, c:c + P],
                                        memV[:, b, i * P:i * P + P], start=b == 0, stop=b == 1)
                ins.then_inc(at_v, 1)

            for i in range(MEM_H):
                pe.wait_ge(at_e, M_E + 2 * i + 2)
                if i >= 2:
                    pe.wait_ge(at_c, M_R + i - 1)
                for t in range(TOKS):
                    for b in range(2):
                        c = (2 * t + b) * P
                        ins = pe.transpose(T[i % 2][:, c:c + P], mprobs[i][:, c:c + P], ident[:, :])
                ins.then_inc(at_r, 1)
                if i:
                    mem_values(i - 1)
            mem_values(MEM_H - 1)
            for j in range(2):
                turn("mo", 0, j, nat, lambda t, half: [(at_o, 3)])
            for j in range(2):
                turn("mo", 1, j, nat, lambda t, half: [(at_o, 4)])
            for t in range(TOKS):
                for half in range(2):
                    for k in range(4):
                        if t == 0:
                            pe.wait_ge(w_lo, U_MO + half + 1)
                        pe.wait_ge(xt_lo, XT["mo"] + 4 * t + k + 1)
                        ins = product(PAIR[half][t], (U_MO + half) % RING, columns(k), k, t, k == 0, k == 3)
                    ins.then_inc(w_used if t else tok0_done, 1)

            def ffn(f, reader, waits):
                u0 = U_FFN[f]
                first_group(u0, reader, PAIR[0], h, waits)

                def up_unit(u, slot, k0):
                    pe.wait_ge(w_lo, u + 1)
                    for k in range(k0, k0 + 4):
                        for t in range(TOKS):
                            ins = product(GU[t], slot, columns(k), k, t, k == 0, k == KD - 1)
                    ins.then_inc(w_used, 1)

                def down(slot, t, half, first=False, last=False):
                    hi, lo = (last_hi, last_lo) if last else (ahi, alo)
                    for k in range(2):
                        c = slice(k * D + half * HALF, k * D + half * HALF + HALF)
                        x = slice((2 * k + t) * P, (2 * k + t) * P + P)
                        o = PAIR[half][t][:, :]
                        pe.matmul(o, lo[:, x], whi[slot][:, c], start=first and k == 0, stop=False)
                        pe.matmul(o, hi[:, x], wlo[slot][:, c], start=False, stop=False)
                        ins = pe.matmul(o, hi[:, x], whi[slot][:, c], start=False, stop=last and k == 1)
                    return ins

                def down_ready(u, j):
                    pe.wait_ge(w_lo, u + 1)
                    pe.wait_ge(act_lo, FJ * f + j + 1)

                def turn_act(j):
                    pe.wait_ge(act_ok, 2 * (FJ * f + j) + 2)
                    for k in range(2):
                        for t in range(TOKS):
                            ins = pe.transpose(T[0][:, (2 * k + t) * P:(2 * k + t) * P + P],
                                               actn[:, t, k * P:k * P + P], ident[:, :])
                    ins.then_inc(act_t, 1)

                v = u0 + 2

                def up(i, first):
                    if not first:
                        pe.wait_ge(act_ok, 2 * (FJ * f + i) + 2)
                    up_unit(v + 3 * i, v % RING, 0)
                    turn_act(i)
                    up_unit(v + 3 * i + 1, (v + 1) % RING, 4)

                def step(i, first):
                    up(i, first)
                    down_ready(v + 3 * i + 2, i)
                    for t in range(TOKS):
                        for half in range(2):
                            ins = down((v + 2) % RING, t, half, first)
                    ins.then_inc(w_used, 1)

                step(0, True)
                with pe.Fori(1, FJ - 2) as i:
                    step(i, False)
                up(FJ - 2, False)
                u, last = u0 + 31, u0 + 32
                down_ready(u, FJ - 2)
                down(u % RING, 0, 0)
                down(u % RING, 0, 1)
                turn_act(FJ - 1)
                down(u % RING, 1, 0)
                down(u % RING, 1, 1).then_inc(w_used, 1)
                down_ready(last, FJ - 1)
                down(last % RING, 0, 0, last=True).then_inc(tok0_done, 1)
                down(last % RING, 0, 1, last=True).then_inc(tok0_done, 1)
                down(last % RING, 1, 0, last=True)
                down(last % RING, 1, 1, last=True).then_inc(w_used, 1)

            ffn(0, "ffn0", h_waits("ffn0"))
            ffn(1, "ffn1", h_waits("ffn1"))
            first_group(U_CIN, "cin", PAIR[0], h, h_waits("cin"))
            def conv_feed(p, is_b):
                if not is_b:
                    pe.wait_ge(conv_p, p // 2 + 1)
                    src = Z[:, :, 512:1024] if p < 2 else Z[:, :, 1536:2048]
                    if p >= 2:
                        pe.wait_ge(conv_x, p - 1)
                else:
                    evacuated(EV_CIN + (0 if p < 2 else 5))
                    src = Z[:, :, 0:512] if p < 2 else nat[:, :, 512:1024]
                    pe.wait_ge(conv_u, p + 1)
                for k in range(2):
                    c = (2 * p + k) % 4 * P
                    for t in range(TOKS):
                        ins = pe.transpose(T[p % 2][:, (2 * k + t) * P:(2 * k + t) * P + P], src[:, t, c:c + P],
                                           ident[:, :])
                ins.then_inc(conv_t, 1)

            group(U_CIN + 2, PAIR[1])
            group(U_CIN + 4, PAIR[2])
            evacuated(EV_CIN)
            k_unit(U_CIN + 6, PAIR[0], 0)
            conv_feed(0, False)
            k_unit(U_CIN + 7, PAIR[0], 4)
            conv_feed(1, False)
            conv_feed(0, True)
            evacuated(EV_CIN + 1)
            k_unit(U_CIN + 8, PAIR[1], 0)
            conv_feed(1, True)
            k_unit(U_CIN + 9, PAIR[1], 4)
            evacuated(EV_CIN + 2)
            k_unit(U_CIN + 10, PAIR[2], 0)
            conv_feed(2, False)
            conv_feed(3, False)
            k_unit(U_CIN + 11, PAIR[2], 4)
            evacuated(EV_CIN + 3)
            for k in range(KD):
                if k % 4 == 0:
                    pe.wait_ge(w_lo, U_COUT + k // 4 + 1)
                if k % 2 == 0:
                    pe.wait_ge(xt_lo, XT["cout"] + k + 2)
                for t in range(TOKS):
                    ins = product(PAIR[0][t], (U_COUT + k // 4) % RING, columns(k), k, t, k == 0, k == KD - 1)
                if k % 4 == 3:
                    ins.then_inc(w_used, 1)
                if k < 2:
                    conv_feed(k + 2, True)
            last_group(U_COUT + 2, PAIR[1])
            ffn(2, "ffn2", h_waits("ffn2"))
            first_group(U_KV, "kv", PAIR[KV_PAIR[0]], h, h_waits("kv"))
            group(U_KV + 2, PAIR[KV_PAIR[1]])
            k_unit(U_KV + 4, PAIR[KV_PAIR[2]], 0)
            evacuated(EV_KV)
            heads_turn(HT_KD, Z[:, :, 0:512])
            k_unit(U_KV + 5, PAIR[KV_PAIR[2]], 4)
            evacuated(EV_KV + 1)
            k_unit(U_KV + 6, PAIR[KV_PAIR[3]], 0)
            t_free_heads(HT_KD)
            heads_turn(HT_KD + 1, Z[:, :, 512:1024])
            k_unit(U_KV + 7, PAIR[KV_PAIR[3]], 4)
            t_free_heads(HT_KD + 1)
            evacuated(EV_KV + 2)
            ffn(3, "ffn3", lambda t, half: [])
            first_group(U_Q, "q", PAIR[0], h, h_waits("q"))
            def q_chunks(*ks):
                for k in ks:
                    if k % 4 == 0:
                        pe.wait_ge(w_lo, U_Q + 2 + k // 4 + 1)
                    for t in range(TOKS):
                        ins = product(PAIR[1][t], (U_Q + 2 + k // 4) % RING, columns(k), k, t, k == 0, k == KD - 1)
                    if k % 4 == 3:
                        ins.then_inc(w_used, 1)

            def diff_scores(m):
                if m >= 2 * DIFF_H:
                    return
                c, r = m // 2, slice(64 * (m % 2), 64 * (m % 2) + 64)
                if m >= 2:
                    pe.wait_ge(at_e, D_E + 2 * m - 2)
                b = B[4 + m % 2]
                for q, lo, width in ((0, 0, P), (1, P, S)):
                    pe.matmul(b[:, lo:lo + width], slopeI[c // 4][:, c % 4, :], distr[:, lo:lo + width], start=True,
                              stop=False)
                    ins = pe.matmul(b[:, lo:lo + width], QT[r, c, q * P:q * P + P], KT[r, c, 0:width], start=False,
                                    stop=True)
                ins.then_inc(at_s, 1)

            def diff_values(i):
                pe.wait_ge(at_c, D_R + i + 1)
                d = slice((i % 4) * P, (i % 4) * P + P)
                causal_values(i, PAIR[i // 4][0][:, d], PAIR[i // 4][1][:, d], VD[:, :, i * P:i * P + P])

            q_chunks(0, 1)
            evacuated(EV_Q)
            heads_turn(HT_QD, Z[:, :, 0:512])
            q_chunks(2, 3)
            t_free_heads(HT_QD)
            pe.wait_ge(alibi_ok, DIFF_H + 1)
            diff_scores(0)
            diff_scores(1)
            q_chunks(4)
            for i in range(DIFF_H):
                if i == 3:
                    t_free_heads(HT_QD + 1)
                diff_scores(2 * i + 2)
                if i:
                    diff_values(i - 1)
                diff_scores(2 * i + 3)
                if i == 0:
                    q_chunks(5, 6)
                if i == 1:
                    q_chunks(7)
                pe.wait_ge(at_a, 2 * i + 2)
                if i >= 2:
                    pe.wait_ge(at_c, D_R + i - 1)
                causal_turn(i, probs[2 * i % 4], at_r)
                if i == 2:
                    evacuated(EV_Q + 1)
                    heads_turn(HT_QD + 1, Z[:, :, 512:1024], PAIR[1])
            diff_values(DIFF_H - 1)
            first_group(U_O, "ao", PAIR[0], nat, lambda t, half: [(at_o, 4 + 2 * (half + 1) if half == 0 else 7 + t)],
                        halves=True)
            last_group(U_O + 2, PAIR[1])
            ffn(4, "ffn4", h_waits("ffn4"))


_INS = ["x", "mem", "g_mix", "w_in", "b_forget", "g_q_fox", "g_k_fox", "w_pool", "pool_scale", "w_out", "g_mem_q",
        "g_mem_kv", "w_mem_q", "w_mem_kv", "g_q_mem", "g_k_mem", "w_mem_out", "g_ffn", "w_gate_up", "w_down",
        "ffn_w_gu_2", "ffn_w_down_2", "norm_g_2", "conv_w_in_2", "conv_k_2", "conv_w_out_2", "kv_norm_g_2",
        "w_kv_2", "attn_w_q_2", "attn_lambda_2", "attn_subln_g_2", "attn_w_o_2"]


def constants():
    p, t = np.arange(P), np.arange(S)
    ones = np.float32(1.0)
    tri = np.stack([(j * P + p[:, None] <= t[None, :]) for j in range(TOKS)], axis=1).astype(np.float32)
    q = np.concatenate([np.zeros(P), np.full(S, P)])
    k = np.concatenate([np.arange(P), np.arange(S)])
    gap = (q[None, :] + p[:, None] - k[None, :]).astype(np.float32)
    sel = np.zeros((64 + FOX_H, FOX_H, P), np.float32)
    for i in range(FOX_H):
        sel[i, i, :] = sel[64 + i, i, :] = -ones
    cnt = np.stack([1.0 / np.minimum(np.arange(16) + 1, w) for w in WINDOWS]).astype(np.float32)
    return {
        "c_ident": np.eye(P, dtype=np.float32),
        "c_tri": tri,
        "c_mask": np.where(gap >= 0, 0.0, NEG).astype(np.float32),
        "c_dist": np.where(gap >= 0, -gap, NEG).astype(np.float32),
        "c_sel": sel,
        "c_cnt": np.ascontiguousarray(np.broadcast_to(cnt, (P, 4, 16))),
    }


def kernel(**inputs):
    import concourse.bacc as bacc
    from concourse.bass_utils import run_bass_kernel_spmd

    nc = bacc.Bacc("TRN2", target_bir_lowering=False, num_devices=1)
    arrays, args = {}, {}
    for name, value in [(n, inputs[n]) for n in _INS] + list(constants().items()):
        v = np.ascontiguousarray(value)
        arrays[f"in_{name}"] = v
        args[name] = nc.dram_tensor(f"in_{name}", v.shape, mybir.dt.from_np(v.dtype), kind="ExternalInput").ap()
    out = nc.dram_tensor("out_0", (1, S, D), F32, kind="ExternalOutput").ap()
    build(nc, args, out)
    r = run_bass_kernel_spmd(nc, [arrays], core_ids=[0])
    return r.results[0]["out_0"]
```
